# Optimizing a Trainium2 kernel written in Bass

```python
import math
import jax, jax.numpy as jnp
from jax import lax
import numpy as np

D_MODEL = 1024
BATCH = 1
SEQ = 256
DEPTH = 2

CHUNK = 64
Q_BLOCK = 128
N_A_LAYERS = DEPTH // 2
N_B_LAYERS = DEPTH - N_A_LAYERS
RWKV_HEAD = 64
RWKV_HEADS = D_MODEL // RWKV_HEAD
DECAY_LORA = 64
ICLR_LORA = 64
GATE_LORA = 160
LNX_EPS = 64e-5
MLA_HEADS = 16
QK_NOPE = 64
QK_ROPE = 32
V_HEAD = 64
Q_LORA = 384
KV_LORA = 256
ROPE_THETA = 10000.0
NEG_INF = -1e30
D_FF = 2816
CONV_W = 3
NORM_EPS = 1e-6


def rmsnorm(x, g):
    xf = x.astype(jnp.float32)
    y = xf * lax.rsqrt(jnp.mean(xf * xf, axis=-1, keepdims=True) + NORM_EPS)
    return (y * g.astype(jnp.float32)).astype(x.dtype)

def conv_ffn(x, w_in, conv_w, conv_b, w_out):
    T = x.shape[1]
    gate, up = jnp.split(x @ w_in, 2, axis=-1)
    gp = jnp.pad(gate, ((0, 0), (CONV_W - 1, 0), (0, 0)))
    gc = conv_b
    for j in range(CONV_W):
        gc = gc + gp[:, j:j + T, :] * conv_w[j]
    h = jax.nn.gelu(gc) * up
    return h @ w_out

def _rwkv7_step(S, inp):
    r, w, k, v, a, b = inp
    sa = jnp.einsum('bhvk,bhk->bhv', S, a)
    S = S * w[:, :, None, :] + sa[..., None] * b[:, :, None, :] + v[..., None] * k[:, :, None, :]
    y = jnp.einsum('bhvk,bhk->bhv', S, r)
    return S, y

def rwkv7_time_mix(x, mu, w_rkv, w0, w1, w2, a0, a1, a2, g1, g2, k_k, k_a, r_k, lnx_w, lnx_b, w_o):
    B, T, D = x.shape
    H, N = RWKV_HEADS, RWKV_HEAD
    f32 = jnp.float32
    x_prev = jnp.pad(x, ((0, 0), (1, 0), (0, 0)))[:, :T]
    xx = x_prev - x
    xs = x[None] + xx[None] * mu[:, None, None, :]
    rkv = jnp.einsum('nbtd,nde->nbte', xs[:3], w_rkv)
    r, k, v = rkv[0], rkv[1], rkv[2]
    xw, xa, xg = xs[3], xs[4], xs[5]
    w_log = -jax.nn.softplus(-(w0 + jnp.tanh(xw @ w1) @ w2)) - 0.5
    decay = jnp.exp(-jnp.exp(w_log.astype(f32)))
    a = jax.nn.sigmoid(a0 + (xa @ a1) @ a2)
    g = jax.nn.sigmoid(xg @ g1) @ g2
    kk = (k * k_k).reshape(B, T, H, N).astype(f32)
    kk = kk / jnp.maximum(jnp.sqrt(jnp.sum(kk * kk, axis=-1, keepdims=True)), 1e-12)
    k = k * (1.0 + (a - 1.0) * k_a)
    heads = lambda t: t.reshape(B, T, H, N).astype(f32)
    rh, kh, vh, wh, ah = heads(r), heads(k), heads(v), heads(decay), heads(a)
    seq = tuple(jnp.moveaxis(t, 1, 0) for t in (rh, wh, kh, vh, -kk, kk * ah))
    S0 = jnp.zeros((B, H, N, N), f32)
    _, y = lax.scan(_rwkv7_step, S0, seq)
    y = jnp.moveaxis(y, 0, 1)
    mean = jnp.mean(y, axis=-1, keepdims=True)
    var = jnp.mean(jnp.square(y - mean), axis=-1, keepdims=True)
    yn = ((y - mean) * lax.rsqrt(var + LNX_EPS)).reshape(B, T, D) * lnx_w + lnx_b
    bonus = (jnp.sum(rh * kh * r_k, axis=-1, keepdims=True) * vh).reshape(B, T, D)
    out = ((yn + bonus) * g).astype(x.dtype)
    return out @ w_o

def rope_tables(T):
    inv = 1.0 / (ROPE_THETA ** (jnp.arange(0, QK_ROPE, 2, dtype=jnp.float32) / QK_ROPE))
    ang = jnp.arange(T, dtype=jnp.float32)[:, None] * inv[None, :]
    return jnp.cos(ang), jnp.sin(ang)

def apply_rope(x, cos, sin):
    half = x.shape[-1] // 2
    xf = x.astype(jnp.float32)
    x1, x2 = xf[..., :half], xf[..., half:]
    return jnp.concatenate([x1 * cos - x2 * sin, x1 * sin + x2 * cos], axis=-1).astype(x.dtype)

def mla_attend(q_nope, q_rope, k_nope, k_rope, v):
    B, T, H, _ = q_nope.shape
    nb = T // Q_BLOCK
    scale = 1.0 / math.sqrt(QK_NOPE + QK_ROPE)
    k_chunk = jnp.arange(T) // CHUNK

    def blocks(t):
        return jnp.moveaxis(t.reshape((B, nb, Q_BLOCK) + t.shape[2:]), 1, 0)

    def one_block(args):
        qn, qr, bi = args
        s = jnp.einsum('bqhd,bkhd->bhqk', qn, k_nope) + jnp.einsum('bqhr,bkr->bhqk', qr, k_rope)
        s = s.astype(jnp.float32) * scale
        q_chunk = (bi * Q_BLOCK + jnp.arange(Q_BLOCK)) // CHUNK
        mask = k_chunk[None, :] <= q_chunk[:, None]
        s = jnp.where(mask[None, None], s, NEG_INF)
        p = jax.nn.softmax(s, axis=-1)
        return jnp.einsum('bhqk,bkhd->bqhd', p.astype(v.dtype), v)

    out = lax.map(one_block, (blocks(q_nope), blocks(q_rope), jnp.arange(nb)))
    return jnp.moveaxis(out, 0, 1).reshape(B, T, H, V_HEAD)

def first_inputs(seed: int = 0) -> dict:
    key = jax.random.key(seed)
    ks = jax.random.split(key, 32)
    D, F, H, N = D_MODEL, D_FF, RWKV_HEADS, RWKV_HEAD
    nA, nB = N_A_LAYERS, N_B_LAYERS
    nrm = lambda k, shape, s: jax.random.normal(k, shape, jnp.float32) * s
    return {
        'x': nrm(ks[0], (BATCH, SEQ, D), 1.0),
        'norm_g': 1.0 + nrm(ks[1], (DEPTH, 4, D), 0.05),
        'ffn_w_in': nrm(ks[2], (DEPTH, D, 2 * F), D ** -0.5),
        'ffn_conv_w': nrm(ks[3], (DEPTH, CONV_W, F), CONV_W ** -0.5),
        'ffn_conv_b': nrm(ks[4], (DEPTH, F), 0.01),
        'ffn_w_out': nrm(ks[5], (DEPTH, F, D), F ** -0.5),
        'a_mu': jax.random.uniform(ks[6], (nA, 6, D), jnp.float32),
        'a_w_rkv': nrm(ks[7], (nA, 3, D, D), D ** -0.5),
        'a_w0': jax.random.uniform(ks[8], (nA, D), jnp.float32, minval=-6.5, maxval=-1.5),
        'a_w1': nrm(ks[9], (nA, D, DECAY_LORA), 0.1 * D ** -0.5),
        'a_w2': nrm(ks[10], (nA, DECAY_LORA, D), DECAY_LORA ** -0.5),
        'a_a0': nrm(ks[11], (nA, D), 0.1),
        'a_a1': nrm(ks[12], (nA, D, ICLR_LORA), 0.1 * D ** -0.5),
        'a_a2': nrm(ks[13], (nA, ICLR_LORA, D), ICLR_LORA ** -0.5),
        'a_g1': nrm(ks[14], (nA, D, GATE_LORA), D ** -0.5),
        'a_g2': nrm(ks[15], (nA, GATE_LORA, D), GATE_LORA ** -0.5),
        'a_k_k': 0.85 + nrm(ks[16], (nA, D), 0.05),
        'a_k_a': 1.0 + nrm(ks[17], (nA, D), 0.05),
        'a_r_k': nrm(ks[18], (nA, H, N), 0.1),
        'a_lnx_w': 1.0 + nrm(ks[19], (nA, D), 0.05),
        'a_lnx_b': nrm(ks[20], (nA, D), 0.01),
        'a_w_o': nrm(ks[21], (nA, D, D), D ** -0.5),
        'kv_norm_g': 1.0 + nrm(ks[22], (D,), 0.05),
        'kv_w_down': nrm(ks[23], (D, KV_LORA + QK_ROPE), D ** -0.5),
        'kv_a_norm_g': 1.0 + nrm(ks[24], (KV_LORA,), 0.05),
        'kv_w_up': nrm(ks[25], (KV_LORA, MLA_HEADS * (QK_NOPE + V_HEAD)), KV_LORA ** -0.5),
        'q_w_down': nrm(ks[26], (nB, D, Q_LORA), D ** -0.5),
        'q_norm_g': 1.0 + nrm(ks[27], (nB, Q_LORA), 0.05),
        'q_w_up': nrm(ks[28], (nB, Q_LORA, MLA_HEADS * (QK_NOPE + QK_ROPE)), Q_LORA ** -0.5),
        'o_w': nrm(ks[29], (nB, MLA_HEADS * V_HEAD, D), (MLA_HEADS * V_HEAD) ** -0.5),
    }

def first_block(x, norm_g, ffn_w_in, ffn_conv_w, ffn_conv_b, ffn_w_out,
              a_mu, a_w_rkv, a_w0, a_w1, a_w2, a_a0, a_a1, a_a2, a_g1, a_g2,
              a_k_k, a_k_a, a_r_k, a_lnx_w, a_lnx_b, a_w_o,
              kv_norm_g, kv_w_down, kv_a_norm_g, kv_w_up,
              q_w_down, q_norm_g, q_w_up, o_w):
    B, T, _ = x.shape
    cos, sin = rope_tables(T)
    k_nope = k_rope = v_sh = None
    for layer in range(DEPTH):
        h = rmsnorm(x, norm_g[layer, 0])
        if layer < N_A_LAYERS:
            i = layer
            m = rwkv7_time_mix(h, a_mu[i], a_w_rkv[i], a_w0[i], a_w1[i], a_w2[i],
                               a_a0[i], a_a1[i], a_a2[i], a_g1[i], a_g2[i],
                               a_k_k[i], a_k_a[i], a_r_k[i], a_lnx_w[i], a_lnx_b[i], a_w_o[i])
        else:
            if layer == N_A_LAYERS:
                down = rmsnorm(x, kv_norm_g) @ kv_w_down
                c_kv = rmsnorm(down[..., :KV_LORA], kv_a_norm_g)
                k_rope = apply_rope(down[..., KV_LORA:], cos, sin)
                up = (c_kv @ kv_w_up).reshape(B, T, MLA_HEADS, QK_NOPE + V_HEAD)
                k_nope, v_sh = up[..., :QK_NOPE], up[..., QK_NOPE:]
            j = layer - N_A_LAYERS
            c_q = rmsnorm(h @ q_w_down[j], q_norm_g[j])
            q = (c_q @ q_w_up[j]).reshape(B, T, MLA_HEADS, QK_NOPE + QK_ROPE)
            q_nope = q[..., :QK_NOPE]
            q_rope = apply_rope(q[..., QK_NOPE:], cos[:, None, :], sin[:, None, :])
            o = mla_attend(q_nope, q_rope, k_nope, k_rope, v_sh)
            m = o.reshape(B, T, MLA_HEADS * V_HEAD) @ o_w[j]
        x = x + rmsnorm(m, norm_g[layer, 1])
        f = conv_ffn(rmsnorm(x, norm_g[layer, 2]), ffn_w_in[layer], ffn_conv_w[layer],
                     ffn_conv_b[layer], ffn_w_out[layer])
        x = x + rmsnorm(f, norm_g[layer, 3])
    return x


ROPE_THETA_2 = 500000.0
ROPE_FRACTION = 4
N_MIXERS = 2
DIFF_HEAD_DIM = 64
DIFF_HEADS = D_MODEL // (2 * DIFF_HEAD_DIM)
DIFF_V_DIM = 2 * DIFF_HEAD_DIM
DSA_HEAD_DIM = 64
DSA_HEADS = D_MODEL // DSA_HEAD_DIM
DSA_Q_RANK = D_MODEL // 4
IDX_HEADS = 8
IDX_DIM = 64
TOPK_MAX = 256
D_FF_2 = 4 * D_MODEL

N_DIFF_LAYERS = (DEPTH + 1) // 2
N_DSA_LAYERS = DEPTH // 2


def rms_norm(x, g=None):
    xf = x.astype(jnp.float32)
    y = xf * lax.rsqrt(jnp.mean(xf * xf, axis=-1, keepdims=True) + NORM_EPS)
    if g is not None:
        y = y * g.astype(jnp.float32)
    return y.astype(x.dtype)

def rope_tables_2(positions, head_dim):
    rot = head_dim // ROPE_FRACTION
    inv = ROPE_THETA_2 ** (-jnp.arange(0, rot, 2, dtype=jnp.float32) / rot)
    ang = positions.astype(jnp.float32)[..., None] * inv
    return jnp.cos(ang)[:, :, None, :], jnp.sin(ang)[:, :, None, :]

def apply_partial_rope(x, cos, sin):
    half = cos.shape[-1]
    rot = 2 * half
    x1 = x[..., :half].astype(jnp.float32)
    x2 = x[..., half:rot].astype(jnp.float32)
    r = jnp.concatenate([x1 * cos - x2 * sin, x2 * cos + x1 * sin], axis=-1).astype(x.dtype)
    return jnp.concatenate([r, x[..., rot:]], axis=-1)

def diff_attention(h, w_in, q_g, k_g, lam_q1, lam_k1, lam_q2, lam_k2, subln_g, w_out,
                   cos, sin, lam_init):
    B, S, _ = h.shape
    H, d = DIFF_HEADS, DIFF_HEAD_DIM
    proj = h @ w_in
    q, k, v = jnp.split(proj, [2 * H * d, 4 * H * d], axis=-1)
    q = apply_partial_rope(rms_norm(q.reshape(B, S, 2 * H, d), q_g), cos, sin) * (d ** -0.5)
    k = apply_partial_rope(rms_norm(k.reshape(B, S, 2 * H, d), k_g), cos, sin)
    q = q.reshape(B, S, H, 2, d)
    k = k.reshape(B, S, H, 2, d)
    v = v.reshape(B, S, H, DIFF_V_DIM)
    lam = (jnp.exp(jnp.sum(lam_q1.astype(jnp.float32) * lam_k1.astype(jnp.float32)))
           - jnp.exp(jnp.sum(lam_q2.astype(jnp.float32) * lam_k2.astype(jnp.float32)))
           + lam_init)
    n_blocks = S // Q_BLOCK
    key_chunk = jnp.arange(S) // CHUNK
    q_blocks = q.reshape(B, n_blocks, Q_BLOCK, H, 2, d).swapaxes(0, 1)

    def block(args):
        qb, start = args
        q_chunk = (start + jnp.arange(Q_BLOCK)) // CHUNK
        mask = key_chunk[None, :] <= q_chunk[:, None]
        s = jnp.einsum('bqhcd,bkhcd->bhcqk', qb, k).astype(jnp.float32)
        p = jax.nn.softmax(jnp.where(mask, s, -jnp.inf), axis=-1)
        a = p[:, :, 0] - lam * p[:, :, 1]
        return jnp.einsum('bhqk,bkhe->bqhe', a.astype(v.dtype), v)

    o = lax.map(block, (q_blocks, jnp.arange(n_blocks) * Q_BLOCK))
    o = o.swapaxes(0, 1).reshape(B, S, H, DIFF_V_DIM)
    o = rms_norm(o, subln_g) * (1.0 - lam_init)
    return o.reshape(B, S, H * DIFF_V_DIM) @ w_out

def dsa_attention(h, w_in, cq_g, w_uq, w_uq_idx, q_g, k_g, w_out, cos, sin):
    B, S, _ = h.shape
    H, d, R, HI, DI = DSA_HEADS, DSA_HEAD_DIM, DSA_Q_RANK, IDX_HEADS, IDX_DIM
    proj = h @ w_in
    c_q, k, v, k_idx, w_idx = jnp.split(
        proj, [R, R + H * d, R + 2 * H * d, R + 2 * H * d + DI], axis=-1)
    c_q = rms_norm(c_q, cq_g)
    q = (c_q @ w_uq).reshape(B, S, H, d)
    q_idx = apply_partial_rope((c_q @ w_uq_idx).reshape(B, S, HI, DI), cos, sin)
    k_idx = apply_partial_rope(rms_norm(k_idx)[:, :, None, :], cos, sin)[:, :, 0]
    w_idx = w_idx * ((HI ** -0.5) * (DI ** -0.5))
    q = apply_partial_rope(rms_norm(q, q_g), cos, sin) * (d ** -0.5)
    k = apply_partial_rope(rms_norm(k.reshape(B, S, H, d), k_g), cos, sin)
    v = v.reshape(B, S, H, d)
    topk = min(TOPK_MAX, S // 4)
    n_blocks = S // Q_BLOCK
    key_chunk = jnp.arange(S) // CHUNK
    qb_all = q.reshape(B, n_blocks, Q_BLOCK, H, d).swapaxes(0, 1)
    qib_all = q_idx.reshape(B, n_blocks, Q_BLOCK, HI, DI).swapaxes(0, 1)
    wb_all = w_idx.reshape(B, n_blocks, Q_BLOCK, HI).swapaxes(0, 1)
    gather = jax.vmap(lambda arr, ids: arr[ids])

    def block(args):
        qb, qib, wb, start = args
        q_chunk = (start + jnp.arange(Q_BLOCK)) // CHUNK
        mask = key_chunk[None, :] <= q_chunk[:, None]
        dots = jnp.einsum('bqhe,bke->bqhk', qib, k_idx).astype(jnp.float32)
        score = jnp.einsum('bqh,bqhk->bqk', wb.astype(jnp.float32), jax.nn.relu(dots))
        score = jnp.where(mask, score, -jnp.inf)
        vals, idx = lax.top_k(score, topk)
        valid = jnp.isfinite(vals)
        kg = gather(k, idx)
        vg = gather(v, idx)
        s = jnp.einsum('bqhd,bqkhd->bhqk', qb, kg).astype(jnp.float32)
        p = jax.nn.softmax(jnp.where(valid[:, None], s, -jnp.inf), axis=-1)
        return jnp.einsum('bhqk,bqkhd->bqhd', p.astype(vg.dtype), vg)

    o = lax.map(block, (qb_all, qib_all, wb_all, jnp.arange(n_blocks) * Q_BLOCK))
    o = o.swapaxes(0, 1).reshape(B, S, H * d)
    return o @ w_out

def sq_relu_mlp(h, w1, w2):
    u = jax.nn.relu(h @ w1)
    return (u * u) @ w2

def second_inputs(seed: int = 0) -> dict:
    key = jax.random.key(seed)
    ks = iter(jax.random.split(key, 32))
    D = D_MODEL

    def nrm(shape, scale):
        return jax.random.normal(next(ks), shape, jnp.float32) * scale

    def gain(shape):
        return 1.0 + nrm(shape, 0.02)

    nA, nB = N_DIFF_LAYERS, N_DSA_LAYERS
    dsa_in = DSA_Q_RANK + 2 * DSA_HEADS * DSA_HEAD_DIM + IDX_DIM + IDX_HEADS
    x = nrm((BATCH, SEQ, D), 1.0)
    offset = jax.random.randint(next(ks), (BATCH, 1), 0, 4096, dtype=jnp.int32)
    positions = (offset + jnp.arange(SEQ, dtype=jnp.int32)[None, :]).astype(jnp.int32)
    return {
        "x": x,
        "positions": positions,
        "norm_mix": gain((DEPTH, D)),
        "norm_mlp": gain((DEPTH, D)),
        "mlp_w1": nrm((DEPTH, D, D_FF_2), D ** -0.5),
        "mlp_w2": nrm((DEPTH, D_FF_2, D), D_FF_2 ** -0.5),
        "diff_w_in": nrm((nA, D, 6 * DIFF_HEADS * DIFF_HEAD_DIM), D ** -0.5),
        "diff_q_norm": gain((nA, DIFF_HEAD_DIM)),
        "diff_k_norm": gain((nA, DIFF_HEAD_DIM)),
        "diff_lam_q1": nrm((nA, DIFF_HEAD_DIM), 0.1),
        "diff_lam_k1": nrm((nA, DIFF_HEAD_DIM), 0.1),
        "diff_lam_q2": nrm((nA, DIFF_HEAD_DIM), 0.1),
        "diff_lam_k2": nrm((nA, DIFF_HEAD_DIM), 0.1),
        "diff_subln": gain((nA, DIFF_V_DIM)),
        "diff_w_out": nrm((nA, DIFF_HEADS * DIFF_V_DIM, D), (DIFF_HEADS * DIFF_V_DIM) ** -0.5),
        "dsa_w_in": nrm((nB, D, dsa_in), D ** -0.5),
        "dsa_cq_norm": gain((nB, DSA_Q_RANK)),
        "dsa_w_uq": nrm((nB, DSA_Q_RANK, DSA_HEADS * DSA_HEAD_DIM), DSA_Q_RANK ** -0.5),
        "dsa_w_uq_idx": nrm((nB, DSA_Q_RANK, IDX_HEADS * IDX_DIM), DSA_Q_RANK ** -0.5),
        "dsa_q_norm": gain((nB, DSA_HEAD_DIM)),
        "dsa_k_norm": gain((nB, DSA_HEAD_DIM)),
        "dsa_w_out": nrm((nB, DSA_HEADS * DSA_HEAD_DIM, D), (DSA_HEADS * DSA_HEAD_DIM) ** -0.5),
    }

def second_block(x, positions, norm_mix, norm_mlp, mlp_w1, mlp_w2,
              diff_w_in, diff_q_norm, diff_k_norm, diff_lam_q1, diff_lam_k1,
              diff_lam_q2, diff_lam_k2, diff_subln, diff_w_out,
              dsa_w_in, dsa_cq_norm, dsa_w_uq, dsa_w_uq_idx, dsa_q_norm, dsa_k_norm,
              dsa_w_out):
    cos, sin = rope_tables_2(positions, DIFF_HEAD_DIM)
    for i in range(DEPTH):
        h = rms_norm(x, norm_mix[i])
        j = i // N_MIXERS
        if i % N_MIXERS == 0:
            lam_init = 0.8 - 0.6 * math.exp(-0.3 * i)
            mix = diff_attention(h, diff_w_in[j], diff_q_norm[j], diff_k_norm[j],
                                 diff_lam_q1[j], diff_lam_k1[j], diff_lam_q2[j],
                                 diff_lam_k2[j], diff_subln[j], diff_w_out[j],
                                 cos, sin, lam_init)
        else:
            mix = dsa_attention(h, dsa_w_in[j], dsa_cq_norm[j], dsa_w_uq[j],
                                dsa_w_uq_idx[j], dsa_q_norm[j], dsa_k_norm[j],
                                dsa_w_out[j], cos, sin)
        x = x + mix
        x = x + sq_relu_mlp(rms_norm(x, norm_mlp[i]), mlp_w1[i], mlp_w2[i])
    return x


def setup_inputs(seed=0):
    out = dict(first_inputs(seed))
    for name, value in second_inputs(seed + 1).items():
        if name != "x":
            out[name + "_2"] = value
    return out


def reference(
    x, norm_g, ffn_w_in, ffn_conv_w, ffn_conv_b, ffn_w_out, a_mu, a_w_rkv, a_w0, a_w1, a_w2,
    a_a0, a_a1, a_a2, a_g1, a_g2, a_k_k, a_k_a, a_r_k, a_lnx_w, a_lnx_b, a_w_o, kv_norm_g,
    kv_w_down, kv_a_norm_g, kv_w_up, q_w_down, q_norm_g, q_w_up, o_w, positions_2, norm_mix_2,
    norm_mlp_2, mlp_w1_2, mlp_w2_2, diff_w_in_2, diff_q_norm_2, diff_k_norm_2, diff_lam_q1_2,
    diff_lam_k1_2, diff_lam_q2_2, diff_lam_k2_2, diff_subln_2, diff_w_out_2, dsa_w_in_2,
    dsa_cq_norm_2, dsa_w_uq_2, dsa_w_uq_idx_2, dsa_q_norm_2, dsa_k_norm_2, dsa_w_out_2,
):
    x = first_block(
        x, norm_g, ffn_w_in, ffn_conv_w, ffn_conv_b, ffn_w_out, a_mu, a_w_rkv, a_w0, a_w1, a_w2,
        a_a0, a_a1, a_a2, a_g1, a_g2, a_k_k, a_k_a, a_r_k, a_lnx_w, a_lnx_b, a_w_o, kv_norm_g,
        kv_w_down, kv_a_norm_g, kv_w_up, q_w_down, q_norm_g, q_w_up, o_w,
    )
    return second_block(
        x, positions_2, norm_mix_2, norm_mlp_2, mlp_w1_2, mlp_w2_2, diff_w_in_2, diff_q_norm_2,
        diff_k_norm_2, diff_lam_q1_2, diff_lam_k1_2, diff_lam_q2_2, diff_lam_k2_2, diff_subln_2,
        diff_w_out_2, dsa_w_in_2, dsa_cq_norm_2, dsa_w_uq_2, dsa_w_uq_idx_2, dsa_q_norm_2,
        dsa_k_norm_2, dsa_w_out_2,
    )


_drawn_inputs = setup_inputs


def setup_inputs(seed=0):
    import zlib

    import numpy as np

    out = dict(_drawn_inputs(seed))
    spreads = {}
    factors = {'ffn_conv_b': 4.873,
     'a_w1': 6.473,
     'a_w2': 6.807,
     'norm_mix_2': 4.338,
     'norm_mlp_2': 3.507,
     'diff_q_norm_2': 8.0,
     'diff_k_norm_2': 8.0,
     'diff_lam_q1_2': 4.913,
     'diff_lam_k1_2': 8.0,
     'diff_subln_2': 5.899,
     'dsa_cq_norm_2': 7.153,
     'dsa_q_norm_2': 8.0,
     'dsa_k_norm_2': 8.0}
    for name, (base, spread) in spreads.items():
        noise = np.random.default_rng([zlib.crc32(name.encode()), seed]).standard_normal(out[name].shape)
        drawn = base * np.exp(spread * noise) if base else spread * noise
        out[name] = __import__('jax').numpy.asarray(drawn.astype(out[name].dtype))
    for name, factor in factors.items():
        out[name] = (out[name] * factor).astype(out[name].dtype)
    return out
```

```python
from contextlib import ExitStack
import math

import numpy as np
import concourse.bass as bass
from concourse import mybir

F32 = mybir.dt.float32
I32 = mybir.dt.int32
ALU = mybir.AluOpType
ACT = mybir.ActivationFunctionType
AX_X = mybir.AxisListType.X

P = 128
T = 256
NT = T // P
D = 1024
KT = D // P
DFF = 2816
DFF2 = 4096
H = 16
HD = 64
LORA = 64
GLORA = 160
KV_LORA = 256
QK_ROPE = 32
QK_NOPE = 64
QD = QK_NOPE + QK_ROPE
Q_LORA = 384
TOPK = min(256, T // 4)
IDX_H = 8
EPS_NORM = 1e-6
EPS_LNX = 64e-5
NEG = -1e30
PAD = -3.0e38
TAKEN = -3.3e38
DSA_Q = 256
MAGIC = 1.5 * 2 ** 23
TWO_PI = (6.28125, 253 / 2 ** 17, 2 * math.pi - 6.28125 - 253 / 2 ** 17)
E05 = math.exp(-0.5)
LAM_INIT = 0.8 - 0.6 * math.exp(-0.3 * 0)

COLS = [("g0_mix", 8), ("g0_ffn", 8), ("g1_mix", 8), ("g_kv", 8), ("g1_ffn", 8), ("n0_mix", 8),
        ("n0_mlp", 8), ("n1_mix", 8), ("n1_mlp", 8), ("mu", 48), ("w0", 8), ("a0", 8), ("k_k", 8),
        ("k_a", 8), ("r_k", 8), ("kv_a", 2), ("q_n", 3), ("cq_n", 2), ("conv_w0", 66),
        ("conv_b0", 22), ("conv_w1", 66), ("conv_b1", 22)]
ROWS = [("g0_res", D), ("g0_fres", D), ("g1_res", D), ("g1_fres", D), ("lnx_w", D), ("lnx_b", D),
        ("dq", 64), ("dk", 64), ("sub", 128), ("sq", 64), ("sk", 64), ("lam", 256)]
CONSTS = [("ident", 128), ("blk1", 128), ("sel2", 2), ("amask", 384), ("cos1", 32), ("sin1", 32),
          ("inv2", 8), ("eps", 2), ("ones", 128)]
MASKS = ["incl", "strict", "dstrict", "dlow", "olow"]


def offsets(table):
    at, out = 0, {}
    for name, n in table:
        out[name] = (at, n)
        at += n
    return out, at


def program(nc, d, out_d):
    COL, NCOL = offsets(COLS)
    ROW, NROW = offsets(ROWS)
    CON, NCON = offsets(CONSTS)
    ctx = ExitStack()
    with ctx:
        def sb(name, shape, dt=F32):
            return ctx.enter_context(nc.sbuf_tensor(name, shape, dt))

        def sem(name):
            return ctx.enter_context(nc.semaphore(name))

        ps = ctx.enter_context(nc.psum_tensor("ps", [P, 8, 512], F32))
        ringA = sb("ringA", [P, 2, 4096])
        ringB = sb("ringB", [P, 2, 4096])
        x = sb("x", [P, NT, D])
        hT = sb("hT", [P, KT, T])
        xn = sb("xn", [P, NT, D])
        cols = sb("cols", [P, NCOL])
        rows = sb("rows", [P, NROW])
        con = sb("con", [P, NCON])
        masks = sb("masks", [P, len(MASKS), P])
        posi = sb("posi", [P, NT], I32)
        cs2 = sb("cs2", [P, 2, NT, 8])
        st = sb("st", [P, 256])
        NAR = 21640
        arena = sb("arena", [P, NAR])

        def col(name, k):
            return cols[:, COL[name][0] + k:COL[name][0] + k + 1]

        def colx(name, k):
            return cols[:, bass.ds(COL[name][0] + k, 1)]

        def row(name):
            a, n = ROW[name]
            return rows[:, a:a + n]

        def cst(name):
            a, n = CON[name]
            return con[:, a:a + n]

        ident = cst("ident")

        def mask(name):
            return masks[:, MASKS.index(name), :].bitcast(I32)

        class Carve:
            def __init__(self):
                self.at = 0

            def __call__(self, n):
                a = self.at
                self.at += n
                assert self.at <= NAR, self.at
                return arena[:, a:a + n]

        const_in = sem("const_in")
        x_in = sem("x_in")
        a_loaded = [sem("a_loaded0"), sem("a_loaded1")]
        b_loaded = [sem("b_loaded0"), sem("b_loaded1")]
        a_used = sem("a_used")
        b_used = sem("b_used")
        out_done = sem("out_done")
        dve_c = sem("dve_c")
        act_c = sem("act_c")
        ss_rdy = sem("ss_rdy")
        sd_rdy = sem("sd_rdy")
        xn_rdy = sem("xn_rdy")
        tp_rdy = sem("tp_rdy")
        hv_rdy = sem("hv_rdy")
        ha_rdy = sem("ha_rdy")
        job_rdy = sem("job_rdy")
        job_out = sem("job_out")
        m_rdy = sem("m_rdy")
        msd_rdy = sem("msd_rdy")
        x_done = sem("x_done")
        f1_rdy = sem("f1_rdy")
        gc_rdy = sem("gc_rdy")
        ge_rdy = sem("ge_rdy")
        h_rdy = sem("h_rdy")
        xs_rdy = sem("xs_rdy")
        xs_used = sem("xs_used")
        wk = {n: sem("wk_" + n) for n in
              ["ang", "cs",
               "sq", "rkp",
               "lc", "kkn",
               "exp",
               "ops", "clr",
               "mm", "cpv", "cpa",
               "g", "cv"]}
        pre = {n: sem("at_" + n) for n in
               ["tsm", "src",
                "src2", "osd",
                "osq",
                "sc", "s", "e",
                "p",
                "pt", "pte",
                "o", "ov",
                "ix", "ixr", "ixs"]}

        def kview(name, w):
            return d[name].rearrange("(k p) n -> p k n", p=P)

        def std(name, n0, n):
            v = kview(name, n)
            return [(0, 4, n, v[:, 0:4, n0:n0 + n]), (4 * n, 4, n, v[:, 4:8, n0:n0 + n])]

        A = []
        a_at = {}

        def add(name, loads):
            a_at.setdefault(name, len(A))
            A.append(loads)

        for w in ("w_r", "w_k", "w_v"):
            for c in range(2):
                add("rkv", std(w, c * 512, 512))
        add("lora", std("w_lora", 0, 2 * LORA + GLORA))
        for c in range(2):
            add("wo0", std("a_w_o", c * 512, 512))
        a_at["ffn0"] = len(A)
        A += [None] * 11
        add("kvd", std("kv_w_down", 0, KV_LORA + QK_ROPE))
        v = kview("kv_w_up", 2048)
        add("kvu", [(0, 1, 2048, v[:, 0:1, :]), (2048, 1, 2048, v[:, 1:2, :])])
        add("qd", std("q_w_down", 0, Q_LORA))
        v = kview("q_w_up", 1536)
        for c in range(2):
            add("qu", [(0, 2, 768, v[:, 0:2, c * 768:(c + 1) * 768]),
                       (2 * 768, 1, 768, v[:, 2:3, c * 768:(c + 1) * 768])])
        for c in range(2):
            add("wo1", std("o_w", c * 512, 512))
        a_at["ffn1"] = len(A)
        A += [None] * 11
        for c in range(6):
            add("din", std("diff_w_in", c * 512, 512))
        for c in range(2):
            add("wo2", std("diff_w_out", c * 512, 512))
        a_at["mlp0"] = len(A)
        A += [None] * 8
        DSA_IN = 256 + 2048 + 64 + 8
        for c in range(5):
            add("sin", std("dsa_w_in", c * 512, min(512, DSA_IN - c * 512)))
        v = kview("w_uqi", 1536)
        add("uq", [(0, 1, 1536, v[:, 0:1, :]), (1536, 1, 1536, v[:, 1:2, :])])
        for c in range(2):
            add("wo3", std("dsa_w_out", c * 512, 512))
        a_at["mlp1"] = len(A)
        A += [None] * 8

        G0 = {"ffn0": 0, "ffn1": 11, "mlp0": 22, "mlp1": 30}
        NCH = {"ffn0": 11, "ffn1": 11, "mlp0": 8, "mlp1": 8}

        def chunk_walk(eng, name, step):
            n = NCH[name]
            step(0, 0)
            step(1, 1)
            pairs = (n - 2) // 2
            with eng.Fori(0, pairs) as i:
                step(i * 2 + 2, 0)
                step(i * 2 + 3, 1)
            for c in range(2 + 2 * pairs, n):
                step(c, c % 2)

        JOBS = [("rkv", 12), ("lora", 2), ("wz", 4), ("az", 4), ("kk", 4), ("bonus", 1), ("gg", 0),
                ("bk", 4), ("kvd", 2), ("ckv", 1), ("kvu", 8), ("qd", 2), ("cq", 2), ("qu", 8),
                ("qk1", 16), ("din", 12), ("qk2", 8), ("sin", 10), ("scq", 1), ("uq", 6), ("qk3", 8),
                ("ixt", 3), ("ixs", 0)]
        J, NJ = offsets(JOBS)

        def bank(j):
            return 4 + j % 4

        TI = {n: i for i, n in enumerate(["n0", "o0", "nf0", "n1", "o1", "nf1", "n2", "o2", "nm0",
                                          "n3", "o3", "nm1"])}
        XN = {n: i for i, n in enumerate([n for n in TI if n not in ("o1", "o3")])}
        MI = {n: i for i, n in enumerate(["o0", "ffn0", "o1", "ffn1", "o2", "mlp0", "o3", "mlp1"])}
        SD = {n: i for i, n in enumerate(
            ["n0", "lnx", "nf0", "n1", "ckv", "cq", "nf1", "n2", "dqk", "dsub", "nm0", "n3",
             "scq", "kidx", "sqk", "nm1"])}

        INST = ["ffn0", "ffn1", "mlp0", "mlp1"]
        a_last = {}

        def jobs_use(name, per_slot):
            def put(a0, n, j0):
                for s in range(n):
                    a_last[a0 + s] = (job_rdy, j0 + per_slot * (s + 1))
            return put

        jobs_use("rkv", 2)(a_at["rkv"], 6, J["rkv"][0])
        jobs_use("lora", 2)(a_at["lora"], 1, J["lora"][0])
        jobs_use("kvd", 2)(a_at["kvd"], 1, J["kvd"][0])
        jobs_use("kvu", 8)(a_at["kvu"], 1, J["kvu"][0])
        jobs_use("qd", 2)(a_at["qd"], 1, J["qd"][0])
        jobs_use("qu", 4)(a_at["qu"], 2, J["qu"][0])
        jobs_use("din", 2)(a_at["din"], 6, J["din"][0])
        jobs_use("sin", 2)(a_at["sin"], 5, J["sin"][0])
        jobs_use("uq", 6)(a_at["uq"], 1, J["uq"][0])
        for n, w in enumerate(["wo0", "wo1", "wo2", "wo3"]):
            a_last[a_at[w]] = (a_used, n + 1)
            a_last[a_at[w] + 1] = (m_rdy, 2 * (MI["o%d" % n] + 1))
        for w in INST:
            for c in range(NCH[w]):
                a_last[a_at[w] + c] = (f1_rdy, 2 * (G0[w] + c) + 2)

        def b_last(g):
            for n, w in enumerate(INST):
                if G0[w] <= g < G0[w] + NCH[w]:
                    if g == G0[w] + NCH[w] - 1:
                        return m_rdy, 2 * (MI[w] + 1)
                    return b_used, g - n + 1

        c = Carve()
        lo2 = c(4096)
        w2_sb, a2_sb = lo2[0:LORA, 0:1024], lo2[0:LORA, 1024:2048]
        g2a_sb, g2b_sb = lo2[:, 2048:3072], lo2[0:GLORA - P, 3072:4096]
        xx = c(2048)
        rT, kT_, vtok, zs, aT = c(2048), c(2048), c(2048), c(2048), c(2048)
        AR = c(4096).rearrange("p (k c j t) -> p k c j t", k=KT, c=2, j=2)
        sigg = c(512)
        lT = ringB[:, 1, 2048:2560]
        lm = c(16)
        cl = c(8)
        bon = c(32)
        Sst = c(512).rearrange("p (k v) -> p k v", k=KT)
        gs_ = c(64)
        xs = [ringB[:, 0, 0:2048], ringB[:, 0, 2048:4096]]
        kkb, Lc = xs[0], xs[1]
        btk = ringB[:, 1, 0:2048].rearrange("p (j c) -> p j c", j=2)
        eN = ringB[:, 1, 2048:4096]
        hflat = hT[:, :, :].rearrange("p k t -> p (k t)")
        xnflat = xn[:, :, :].rearrange("p t n -> p (t n)")
        eQ, eP = xnflat, hflat
        k2 = xx
        bT = aT
        ytok = hflat
        lanes = []
        for pool in ([rT, kT_, zs], [kkb, Lc, eN]):
            bufs = [r[:, 512 * i:512 * i + 512] for r in pool for i in range(4)]
            n = len(lanes)
            names = ["NdT", "rb", "ak", "rk", "Nd", "No", "N2", "N2T", "N4", "N4T", "N8", "E"]
            lane = dict(zip(names, bufs))
            lane.update(M=lane["N2T"], MT=lane["N4T"], M2=lane["N2"], M2T=lane["N4"], M4T=lane["N8"])
            for i, r in enumerate(["R", "u0", "u1"]):
                lane[r] = lo2[:, n * 768 + i * 256:n * 768 + i * 256 + 256]
            lanes.append(lane)

        c = Carve()
        hid = c(2048).rearrange("p (g n) -> p g n", g=2)
        gc = c(1024).rearrange("p (g n) -> p g n", g=2)
        ge = c(1024).rearrange("p (g n) -> p g n", g=2)
        rl = c(2048).rearrange("p (g q n) -> p g q n", g=2, q=2)

        c = Carve()
        m_down = c(576).rearrange("p (t n) -> p t n", t=2)
        m_ckvn = c(512).rearrange("p (t n) -> p t n", t=2)
        m_ckvT = c(512).rearrange("p (k n) -> p k n", k=2)
        m_qd = c(768).rearrange("p (t n) -> p t n", t=2)
        m_cqn = c(768).rearrange("p (t n) -> p t n", t=2)
        m_cqT = c(768).rearrange("p (k n) -> p k n", k=3)
        m_k = c(3072).rearrange("p (t h n) -> p t h n", t=2, h=H)
        m_q = c(3072).rearrange("p (t h n) -> p t h n", t=2, h=H)
        m_rt = c(1024)
        m_KT = c(4096).rearrange("p (h t) -> p h t", h=H)
        m_QT = c(4096).rearrange("p (h t) -> p h t", h=H)
        hT2 = m_QT.rearrange("p h t -> p (h t)")[:, 0:2048].rearrange("p (k t) -> p k t", k=KT)
        m_v = rows[:, ROW["lnx_w"][0]:ROW["lnx_w"][0] + 2048].rearrange("p (t n) -> p t n", t=2)
        c2 = Carve()
        m_soft = c2(3456)

        c = Carve()
        d_p = c(6144).rearrange("p (j t n) -> p j t n", j=3, t=2)
        d_QT = c(2048).rearrange("p (k t) -> p k t", k=8)
        d_KT = c(2048).rearrange("p (k t) -> p k t", k=8)
        d_sq = c(4096)
        d_rt = c(1024)
        d_soft = c(3456)
        d_lam = c(8)

        c = Carve()
        s_p = c(2 * DSA_IN).rearrange("p (t n) -> p t n", t=2)
        s_q = c(2048).rearrange("p (t n) -> p t n", t=2)
        s_qi = c(1024).rearrange("p (t n) -> p t n", t=2)
        s_cqn = c(512).rearrange("p (t n) -> p t n", t=2)
        s_cqT = c(512).rearrange("p (k n) -> p k n", k=2)
        s_ki = c(256).rearrange("p (t j n) -> p t j n", t=2, j=2)
        s_QIT = c(1024).rearrange("p (k t) -> p k t", k=4)
        s_KIT = c(256)
        qk_at = c(4096)
        s_QT = qk_at[:, 0:2048].rearrange("p (k t) -> p k t", k=8)
        s_KT = qk_at[:, 2048:4096].rearrange("p (k t) -> p k t", k=8)
        s_sq = qk_at
        s_rt = c(512)
        s_ixr = c(768).rearrange("p (j n) -> p j n", j=2)
        s_acc = c(384)
        s_w = c(384)
        s_sel = c(384)
        s_soft = c(3456)

        def soft(r):
            return (r[:, 0:1152].rearrange("p (j n) -> p j n", j=3),
                    r[:, 1152:2688].rearrange("p (j n) -> p j n", j=4),
                    r[:, 2688:3456].rearrange("p (j n) -> p j n", j=2))

        def fm(ap):
            return ap.rearrange("p (k t) -> p k t", k=KT)

        def bc(ap, axis, n):
            shape = list(ap.shape)
            shape.insert(axis, n)
            return ap.unsqueeze(axis).to_broadcast(shape)

        STEPS = [("sb", "v"), ("sk", "v"), ("sn", "v"), ("N2", "a"), ("N2T", "a"), ("E2", "v"),
                 ("N4", "a"), ("N4T", "a"), ("E3", "v"), ("N8", "a"), ("E4", "v"), ("M", "a"),
                 ("MT", "v"), ("M2", "a"), ("M2T", "a"), ("M4T", "v"), ("rhs", "a"), ("y0", "a"),
                 ("y1", "v"), ("y2", "v"), ("U", "v"), ("Y", "a"), ("S", "v")]
        BANKS = {"sb": (0, 1), "sk": (2, 3), "sn": (0, 1), "N2": (2,), "N2T": (3,), "E2": (0,),
                 "N4": (1,), "N4T": (2,), "E3": (3,), "N8": (0,), "E4": (1,), "M": (2,), "MT": (3,),
                 "M2": (0,), "M2T": (1,), "M4T": (2,), "rhs": (3, 0), "y0": (1,), "y1": (2,),
                 "y2": (3,), "U": (0,), "Y": (1, 2), "S": (3,)}
        ORDER = [(u, name, e) for pair in range(4) for name, e in STEPS
                 for u in (2 * pair, 2 * pair + 1) if name != "S" or u < 4]
        PE_N = {(u, name): n + 1 for n, (u, name, _) in enumerate(ORDER)}
        EV_N = {}
        for e in "va":
            for n, (u, name, _) in enumerate([o for o in ORDER if o[2] == e]):
                EV_N[u, name] = (wk["cpv"] if e == "v" else wk["cpa"], n + 1)

        def heads_of(u):
            g = u % 4
            return u // 4, [(0, 2 * g, 0), (1, 2 * g + 1, 0), (2, 2 * g, 64), (3, 2 * g + 1, 64)]

        def lane_bank(u, name, i=0):
            return 4 * (u % 2) + BANKS[name][i]

        block = ctx.enter_context(nc.Block())

        @block.sync
        def _(sp):
            cons = [(cols[:, :], d["cols"]), (con[:, :], d["con"]),
                    (masks[:, :, :], d["masks"].rearrange("p (m t) -> p m t", m=len(MASKS))),
                    (rows[:, :], d["rows"].to_broadcast([P, NROW])),
                    (posi[:, :], d["positions"]),
                    (w2_sb, d["a_w2"]), (a2_sb, d["a_a2"]), (g2a_sb, d["a_g2"][0:P, :]),
                    (g2b_sb, d["a_g2"][P:GLORA, :])]
            sp.dma_start(x[:, :, :], d["x"].rearrange("(t p) n -> p t n", p=P)).then_inc(x_in, 16)
            for dst, src in cons:
                sp.dma_start(dst, src).then_inc(const_in, 16)

            def load_a(i):
                if i >= 2:
                    s, v = a_last[i - 2]
                    sp.wait_ge(s, v)
                for off, k, n, src in A[i]:
                    dst = ringA[:, i % 2, off:off + k * n].rearrange("p (k n) -> p k n", k=k)
                    sp.dma_start(dst, src).then_inc(a_loaded[i % 2], 16)

            def ffn_loads(w, gate_up):
                n = INST.index(w)

                def step(ch, par):
                    a0, g0 = a_at[w], G0[w]
                    ap, bp = (a0 + par) % 2, (g0 + par) % 2
                    if isinstance(ch, int):
                        s, v = a_last[a0 + ch - 2]
                        sp.wait_ge(s, v)
                    else:
                        sp.wait_ge(f1_rdy, ch * 2 + (2 * g0 - 2))
                    dst = ringA[:, ap, :].rearrange("p (k j n) -> p k j n", k=KT, j=2)
                    if gate_up:
                        wi = d["ffn_w_in%d" % n].rearrange("(k p) m -> p k m", p=P)
                        for j in range(2):
                            sp.dma_start(dst[:, :, j, :], wi[:, :, bass.ds(ch * 256 + j * DFF, 256)]
                                         ).then_inc(a_loaded[ap], 16)
                    else:
                        wi = d["mlp_w1_%d" % (n - 2)].rearrange("(k p) m -> p k m", p=P)
                        dst = ringA[:, ap, :].rearrange("p (k n) -> p k n", k=KT)
                        for j in range(2):
                            sp.dma_start(dst[:, 4 * j:4 * j + 4, :],
                                         wi[:, 4 * j:4 * j + 4, bass.ds(ch * 512, 512)]
                                         ).then_inc(a_loaded[ap], 16)
                    if w == "ffn0" and isinstance(ch, int) and ch == 0:
                        sp.wait_ge(m_rdy, 2)
                    elif isinstance(ch, int) and ch < 2 and w == "ffn0":
                        pass
                    elif isinstance(ch, int):
                        s, v = b_last(g0 + ch - 2)
                        sp.wait_ge(s, v)
                    else:
                        sp.wait_ge(b_used, ch + (g0 - n - 1))
                    if gate_up:
                        wo, kk_ = d["ffn_w_out%d" % n], 1
                    else:
                        wo, kk_ = d["mlp_w2_%d" % (n - 2)], 2
                    dst = ringB[:, bp, 0:2048 * kk_].rearrange("p (j k n) -> p j k n", j=2, k=kk_)
                    for j in range(2):
                        src = wo[bass.ds((ch * 2 + j) * kk_ * P, kk_ * P), :].rearrange(
                            "(k p) m -> p k m", p=P)
                        sp.dma_start(dst[:, j], src).then_inc(b_loaded[bp], 16)

                chunk_walk(sp, w, step)

            for i in range(0, a_at["ffn0"]):
                load_a(i)
            ffn_loads("ffn0", True)
            for i in range(a_at["kvd"], a_at["ffn1"]):
                load_a(i)
            ffn_loads("ffn1", True)
            for i in range(a_at["din"], a_at["mlp0"]):
                load_a(i)
            ffn_loads("mlp0", False)
            for i in range(a_at["sin"], a_at["mlp1"]):
                load_a(i)
            ffn_loads("mlp1", False)
            for t in range(NT):
                sp.wait_ge(x_done, 14 + t + 1)
                sp.dma_start(out_d.rearrange("(t p) n -> p t n", p=P)[:, t, :], x[:, t, :]
                             ).then_inc(out_done, 16)
            sp.wait_ge(out_done, 32)

        @block.tensor
        def _(pe):
            mm = nc.tensor.matmul

            def wait_a(i):
                pe.wait_ge(a_loaded[i % 2], 32 * (i // 2 + 1))

            def turn16(name):
                if name in XN:
                    pe.wait_ge(xn_rdy, 2 * (XN[name] + 1))
                else:
                    pe.wait_ge(pre["ov"], {"o1": 16, "o3": 40}[name])
                for b in range(4):
                    for k in (2 * b, 2 * b + 1):
                        for t in range(NT):
                            last = nc.tensor.transpose(
                                ps[:, 4 + b, (k % 2) * T + t * P:(k % 2) * T + t * P + P],
                                xn[:, t, k * P:(k + 1) * P], ident)
                    last.then_inc(tp_rdy, 1)

            def wait_hT(name):
                pe.wait_ge(hv_rdy, 4 * (TI[name] + 1))
                pe.wait_ge(ha_rdy, 4 * (TI[name] + 1))

            def job_bank(j):
                if j >= 4:
                    pe.wait_ge(job_out, j - 3)
                return bank(j)

            def token_jobs(a, j0, src, kts, chunks):
                wait_a(a)
                w = sum(chunks)
                j, off = j0, 0
                for n in chunks:
                    for t in range(NT):
                        b = job_bank(j)
                        for k in range(kts):
                            last = mm(ps[:, b, 0:n], src[:, k, t * P:(t + 1) * P],
                                      ringA[:, a % 2, k * w + off:k * w + off + n],
                                      start=(k == 0), stop=(k == kts - 1))
                        last.then_inc(job_rdy, 1)
                        j += 1
                    off += n

            def out_proj(n):
                a = a_at["wo%d" % n]
                mi = MI["o%d" % n]
                wait_hT("o%d" % n)
                if mi:
                    pe.wait_ge(x_done, 2 * mi)
                for half in range(2):
                    wait_a(a + half)
                    for t in range(NT):
                        for k in range(KT):
                            last = mm(ps[:, 2 * t + half, :], hT[:, k, t * P:(t + 1) * P],
                                      ringA[:, (a + half) % 2, k * 512:(k + 1) * 512],
                                      start=(k == 0), stop=(k == KT - 1))
                        if half == 1:
                            last.then_inc(m_rdy, 1)
                        elif t == 1:
                            last.then_inc(a_used, 1)

            def ffn(w, hbuf, nf):
                n = INST.index(w)
                a0, g0 = a_at[w], G0[w]

                def first(ch, par):
                    ap, gp = (a0 + par) % 2, (g0 + par) % 2
                    if isinstance(ch, int):
                        wait_a(a0 + ch)
                        if g0 + ch >= 2:
                            pe.wait_ge(h_rdy, 2 * (g0 + ch) - 2)
                    else:
                        pe.wait_ge(a_loaded[ap], ch * 16 + (32 * ((a0 + par) // 2 + 1) - 16 * par))
                        pe.wait_ge(h_rdy, ch * 2 + (2 * g0 - 2))
                    for q in range(2):
                        for j in range(2):
                            for k in range(KT):
                                if nf == 2:
                                    o = k * 512 + j * 256 + q * P
                                else:
                                    o = k * 512 + (2 * q + j) * P
                                last = mm(ps[:, 4 + 2 * gp + q, j * T:(j + 1) * T],
                                          ringA[:, ap, o:o + P], hT[:, k, :],
                                          start=(k == 0), stop=(k == KT - 1))
                        last.then_inc(f1_rdy, 1)

                def second(ch, par, first_one=False, last_one=False):
                    bp = (g0 + par) % 2
                    if isinstance(ch, int):
                        g = g0 + ch
                        pe.wait_ge(b_loaded[bp], 32 * (g // 2 + 1))
                        pe.wait_ge(h_rdy, 2 * g + 2)
                    else:
                        pe.wait_ge(b_loaded[bp], ch * 16 + (32 * ((g0 + par) // 2 + 1) - 16 * par))
                        pe.wait_ge(h_rdy, ch * 2 + (2 * g0 + 2))
                    if first_one and MI[w]:
                        pe.wait_ge(x_done, 2 * MI[w])
                    for t in range(NT):
                        for f in range(nf):
                            for half in range(2):
                                o = f * D + half * 512
                                last = mm(ps[:, 2 * t + half, :],
                                          hbuf[:, bp, f * T + t * P:f * T + t * P + P],
                                          ringB[:, bp, o:o + 512],
                                          start=(first_one and f == 0), stop=(last_one and f == nf - 1))
                        if last_one:
                            last.then_inc(m_rdy, 1)
                    if not last_one:
                        last.then_inc(b_used, 1)

                nch = NCH[w]
                pairs = (nch - 2) // 2
                first(0, 0)
                first(1, 1)
                second(0, 0, first_one=True)
                with pe.Fori(0, pairs) as i:
                    first(i * 2 + 2, 0)
                    second(i * 2 + 1, 1)
                    first(i * 2 + 3, 1)
                    second(i * 2 + 2, 0)
                for ch in range(2 + 2 * pairs, nch):
                    first(ch, ch % 2)
                    second(ch - 1, (ch - 1) % 2)
                second(nch - 1, (nch - 1) % 2, last_one=True)

            pe.wait_ge(const_in, 16 * 9)
            turn16("n0")
            j = J["rkv"][0]
            for i in range(3):
                pe.wait_ge(xs_rdy, i + 1)
                xi = fm(xs[i % 2])
                for s in range(2):
                    a = 2 * i + s
                    if i == 2:
                        token_jobs(a, j, xi, KT, [512])
                        j += 2
                        continue
                    wait_a(a)
                    for jj in range(2):
                        b = job_bank(j)
                        for q in range(2):
                            for k in range(KT):
                                o = k * 512 + (2 * jj + q) * P
                                last = mm(ps[:, b, q * T:(q + 1) * T], ringA[:, a % 2, o:o + P],
                                          xi[:, k, :], start=(k == 0), stop=(k == KT - 1))
                        last.then_inc(job_rdy, 1)
                        j += 1
            a = a_at["lora"]
            wait_a(a)
            wl = 2 * LORA + GLORA
            b = job_bank(j)
            for i in range(2):
                pe.wait_ge(xs_rdy, 4 + i)
                xi = fm(xs[(3 + i) % 2])
                for k in range(KT):
                    o = k * wl + i * LORA
                    last = mm(ps[0:LORA, b, i * T:(i + 1) * T], ringA[:, a % 2, o:o + LORA],
                              xi[:, k, :], start=(k == 0), stop=(k == KT - 1))
            last.then_inc(job_rdy, 1)
            j += 1
            b = job_bank(j)
            pe.wait_ge(xs_rdy, 6)
            xi = fm(xs[1])
            for q, (o0, n) in enumerate([(2 * LORA, P), (2 * LORA + P, GLORA - P)]):
                for k in range(KT):
                    o = k * wl + o0
                    last = mm(ps[0:n, b, q * T:(q + 1) * T], ringA[:, a % 2, o:o + n],
                              xi[:, k, :], start=(k == 0), stop=(k == KT - 1))
            last.then_inc(job_rdy, 1)
            j += 1
            pe.wait_ge(job_out, J["lora"][0] + 1)
            for i, wsb in enumerate((w2_sb, a2_sb)):
                for jj in range(4):
                    b = job_bank(j)
                    for q in range(2):
                        k = 2 * jj + q
                        last = mm(ps[:, b, q * T:(q + 1) * T], wsb[:, k * P:(k + 1) * P],
                                  lT[0:LORA, i * T:(i + 1) * T], start=True, stop=True)
                    last.then_inc(job_rdy, 1)
                    j += 1
            pe.wait_ge(wk["sq"], 1)
            for jj in range(4):
                b = job_bank(j)
                last = mm(ps[:, b, :], cst("blk1"), xnflat[:, jj * 512:(jj + 1) * 512],
                          start=True, stop=True)
                last.then_inc(job_rdy, 1)
                j += 1
            pe.wait_ge(wk["rkp"], 1)
            b = job_bank(j)
            for t in range(NT):
                for k in range(KT):
                    last = mm(ps[:, b, t * H + 2 * k:t * H + 2 * k + 2],
                              fm(hflat)[:, k, t * P:(t + 1) * P], cst("sel2"), start=True, stop=True)
            last.then_inc(job_rdy, 1)
            j += 1
            pe.wait_ge(wk["ops"], 1)
            for m, src in enumerate((bT, k2)):
                for jj in range(2):
                    b = job_bank(j)
                    for q in range(4):
                        k = 4 * jj + q
                        last = nc.tensor.transpose(ps[:, b, q * P:(q + 1) * P],
                                                   fm(src)[:, k, 0:P], ident)
                    last.then_inc(job_rdy, 1)
                    j += 1
            pe.wait_ge(job_out, j)
            pe.wait_ge(wk["clr"], 1)

            def need(u, *names):
                for n in names:
                    pe.wait_ge(*EV_N[u, n])

            BEFORE = {"sn": "sb", "N2": "sk", "N2T": "sk", "E2": "sn", "N4": "sn", "N4T": "N2",
                      "E3": "N2T", "N8": "E2", "E4": "N4", "M": "N4T", "MT": "E3", "M2": "N8",
                      "M2T": "E4", "M4T": "M", "rhs": "MT", "y0": "M2T", "y1": "M4T", "y2": "rhs",
                      "U": "rhs", "Y": "y0", "S": "y2"}
            PROD = {"N2": ("NdT", "Nd"), "N2T": ("Nd", "NdT"), "E2": ("N2", "E"),
                    "N4": ("N2T", "N2"), "N4T": ("N2", "N2T"), "E3": ("N4", "E"),
                    "N8": ("N4T", "N4"), "E4": ("N8", "E"), "M": ("E", "No"), "MT": ("No", "E"),
                    "M2": ("MT", "M"), "M2T": ("M", "MT"), "M4T": ("M2", "M2T"),
                    "y0": ("E", "R"), "y1": ("M4T", "u0"), "y2": ("M2T", "u1"), "U": ("MT", "u0")}
            FROM = {"N2": ("sb", "sn"), "N2T": (), "E2": ("N2",), "N4": ("N2T",), "N4T": (),
                    "E3": ("N4", "E2"), "N8": ("N4T",), "E4": ("N8", "E3"), "M": ("E4",), "MT": (),
                    "M2": ("MT", "M"), "M2T": (), "M4T": ("M2", "M2T"), "y0": ("rhs",),
                    "y1": ("y0", "M4T"), "y2": ("y1",), "U": ("y2",)}
            for u, name, _e in ORDER:
                ch, hs = heads_of(u)
                L = lanes[u % 2]
                if name in BEFORE:
                    need(u, BEFORE[name])
                elif name == "sb" and u >= 2:
                    need(u - 2, "U", "Y")
                elif name == "sk" and u >= 2:
                    need(u - 2, "Y", "S" if u - 2 < 4 else "y2")
                if name == "Y":
                    need(u, "y1", "U")
                if name in PROD:
                    need(u, *FROM[name])
                    lhs, rhs = PROD[name]
                    w = 64 if rhs in ("R", "u0", "u1") else P
                    b = lane_bank(u, name)
                    for q in range(4):
                        last = mm(ps[:, b, q * w:(q + 1) * w], L[lhs][:, q * P:(q + 1) * P],
                                  L[rhs][:, q * w:(q + 1) * w], start=True, stop=True)
                elif name in ("sb", "sk", "sn"):
                    for s, k, p0 in hs:
                        b = lane_bank(u, name, s // 2)
                        rowsl = slice(p0, p0 + 64)
                        toks = slice(ch * P, (ch + 1) * P)
                        if name == "sn":
                            last = mm(ps[:, b, (s % 2) * P:(s % 2) * P + P],
                                      AR[rowsl, k, ch, 0, :], fm(bT)[rowsl, k, toks],
                                      start=True, stop=True)
                        else:
                            src = bT if name == "sb" else k2
                            last = mm(ps[:, b, (s % 2) * T:(s % 2) * T + T], fm(src)[rowsl, k, toks],
                                      AR[rowsl, k, ch, :, :].rearrange("p j t -> p (j t)"),
                                      start=True, stop=True)
                elif name == "rhs":
                    need(u, "sk", "M2")
                    if ch:
                        need(u - 4, "S")
                    for s, k, p0 in hs:
                        b = lane_bank(u, name, s // 2)
                        o = ps[:, b, (s % 2) * 64:(s % 2) * 64 + 64]
                        hv = k * P + p0
                        last = mm(o, L["ak"][:, s * P:(s + 1) * P],
                                  vtok[:, ch * D + hv:ch * D + hv + 64], start=True, stop=(ch == 0))
                        if ch:
                            last = mm(o, AR[p0:p0 + 64, k, ch, 0, :], Sst[p0:p0 + 64, k, :],
                                      start=False, stop=True)
                elif name == "Y":
                    for s, k, p0 in hs:
                        b = lane_bank(u, name, s // 2)
                        o = ps[:, b, (s % 2) * 64:(s % 2) * 64 + 64]
                        hv = k * P + p0
                        mm(o, L["rk"][:, s * P:(s + 1) * P], vtok[:, ch * D + hv:ch * D + hv + 64],
                           start=True, stop=False)
                        last = mm(o, L["rb"][:, s * P:(s + 1) * P], L["u1"][:, s * 64:(s + 1) * 64],
                                  start=False, stop=(ch == 0))
                        if ch:
                            last = mm(o, AR[p0:p0 + 64, k, ch, 1, :], Sst[p0:p0 + 64, k, :],
                                      start=False, stop=True)
                else:
                    b = lane_bank(u, name)
                    uv = L["u1"].rearrange("p (j q v) -> p q j v", j=2, q=2)
                    for q in range(2):
                        k = hs[q][1]
                        o = ps[:, b, q * P:(q + 1) * P]
                        mm(o, btk[:, 1, k * P:(k + 1) * P], vtok[:, k * P:(k + 1) * P],
                           start=True, stop=False)
                        last = mm(o, btk[:, 0, k * P:(k + 1) * P], uv[:, q, :, :],
                                  start=False, stop=True)
                last.then_inc(wk["mm"], 1)
            need(6, "U", "Y", "y2")
            for t in range(NT):
                for half in range(2):
                    o = ps[:, 2 * t + half, :]
                    mm(o, sigg[:, t * P:(t + 1) * P], g2a_sb[:, half * 512:(half + 1) * 512],
                       start=True, stop=False)
                    last = mm(o, sigg[0:GLORA - P, T + t * P:T + (t + 1) * P],
                              g2b_sb[:, half * 512:(half + 1) * 512], start=False, stop=True)
            last.then_inc(wk["g"], 1)
            need(7, "U", "Y", "y2")
            turn16("o0")
            out_proj(0)

            turn16("nf0")
            wait_hT("nf0")
            ffn("ffn0", hid, 2)

            def small_turn(j0, src, kts, n):
                pe.wait_ge(pre["tsm"], n)
                for jj in range((kts + 1) // 2):
                    b = job_bank(j0 + jj)
                    for k in range(2 * jj, min(2 * jj + 2, kts)):
                        for t in range(NT):
                            last = nc.tensor.transpose(
                                ps[:, b, (k % 2) * T + t * P:(k % 2) * T + t * P + P],
                                src[:, t, k * P:(k + 1) * P], ident)
                    last.then_inc(job_rdy, 1)

            def turn_blocks(j0, blocks):
                for jj in range((len(blocks) + 1) // 2):
                    b = job_bank(j0 + jj)
                    for i in range(2 * jj, min(2 * jj + 2, len(blocks))):
                        src, w = blocks[i]
                        for t in range(NT):
                            o = (i % 2) * T + t * P
                            last = nc.tensor.transpose(ps[0:w, b, o:o + P], src(t), ident)
                    last.then_inc(job_rdy, 1)

            def attend(layer, qt, kt, v, dv, softs):
                _, pr, pT = soft(softs)
                diff = layer == 1
                per = 2 if diff else 1
                u0, h0 = 16 * layer, [0, 16, 24][layer]

                def scores(u):
                    if u0 + u >= 3:
                        pe.wait_ge(pre["s"], u0 + u - 2)
                    b = 3 + (u0 + u) % 3
                    q, k = qt(u), kt(u)
                    mm(ps[:, b, 0:P], q[:, 0:P], k[:, 0:P], start=True, stop=True)
                    mm(ps[:, b, P:3 * P], q[:, P:T], k[:, :], start=True, stop=True
                       ).then_inc(pre["sc"], 1)

                def turn(h):
                    if diff:
                        pe.wait_ge(pre["p"], h + 1)
                    else:
                        pe.wait_ge(pre["e"], u0 + h + 1)
                    if h0 + h >= 2:
                        pe.wait_ge(pre["pte"], h0 + h - 1)
                    b = 6 + (h0 + h) % 2
                    for i in range(3):
                        last = nc.tensor.transpose(ps[:, b, i * P:(i + 1) * P],
                                                   pr[:, (per * h) % 4, i * P:(i + 1) * P], ident)
                    last.then_inc(pre["pt"], 1)

                def out(h):
                    pe.wait_ge(pre["pte"], h0 + h + 1)
                    if h0 + h >= 2:
                        pe.wait_ge(pre["ov"], h0 + h - 1)
                    b = (h0 + h) % 2
                    w = pT[:, (h0 + h) % 2, :]
                    mm(ps[:, b, 0:dv], w[:, 0:P], v(0, h), start=True, stop=True)
                    mm(ps[:, b, dv:2 * dv], w[:, P:2 * P], v(0, h), start=True, stop=False)
                    mm(ps[:, b, dv:2 * dv], w[:, 2 * P:3 * P], v(1, h), start=False, stop=True
                       ).then_inc(pre["o"], 1)

                heads = 16 // per
                for u in range(min(2 * per, 16)):
                    scores(u)
                for h in range(heads):
                    turn(h)
                    for u in range(per * (h + 2), min(per * (h + 3), 16)):
                        scores(u)
                    if h:
                        out(h - 1)
                out(heads - 1)

            turn16("n1")
            wait_hT("n1")
            token_jobs(a_at["kvd"], J["kvd"][0], hT2, KT, [KV_LORA + QK_ROPE])
            small_turn(J["ckv"][0], m_ckvn, 2, 1)
            pe.wait_ge(job_out, J["ckv"][0] + 1)
            token_jobs(a_at["kvu"], J["kvu"][0], m_ckvT, 2, [512] * 4)
            token_jobs(a_at["qd"], J["qd"][0], hT, KT, [Q_LORA])
            small_turn(J["cq"][0], m_cqn, 3, 2)
            pe.wait_ge(job_out, J["cq"][0] + 2)
            for s in range(2):
                token_jobs(a_at["qu"] + s, J["qu"][0] + 4 * s, m_cqT, 3, [384, 384])
            pe.wait_ge(job_out, J["qk1"][0])
            pe.wait_ge(pre["src"], 1)
            turn_blocks(J["qk1"][0], [((lambda t, s=s, h=h: s[:, t, h, :]), QD)
                                      for s in (m_q, m_k) for h in range(H)])
            pe.wait_ge(job_out, J["qk1"][0] + 16)
            attend(0, lambda u: m_QT[0:QD, u, :], lambda u: m_KT[0:QD, u, :],
                   lambda t, h: m_v[:, t, h * 64:(h + 1) * 64], 64, m_soft)
            turn16("o1")
            out_proj(1)
            turn16("nf1")
            wait_hT("nf1")
            ffn("ffn1", hid, 2)

            turn16("n2")
            wait_hT("n2")
            for s in range(6):
                token_jobs(a_at["din"] + s, J["din"][0] + 2 * s, hT, KT, [512])
            pe.wait_ge(pre["src"], 2)
            turn_blocks(J["qk2"][0], [((lambda t, i=i, k=k: d_p[:, i, t, k * P:(k + 1) * P]), P)
                                      for i in range(2) for k in range(8)])
            pe.wait_ge(job_out, J["qk2"][0] + 8)

            def half(ap, u):
                return ap[64 * (u % 2):64 * (u % 2) + 64, u // 2, :]

            attend(1, lambda u: half(d_QT, u), lambda u: half(d_KT, u),
                   lambda t, h: d_p[:, 2, t, h * P:(h + 1) * P], P, d_soft)
            turn16("o2")
            out_proj(2)
            turn16("nm0")
            wait_hT("nm0")
            ffn("mlp0", hid, 4)

            turn16("n3")
            wait_hT("n3")
            for s in range(5):
                token_jobs(a_at["sin"] + s, J["sin"][0] + 2 * s, hT, KT,
                           [min(512, DSA_IN - 512 * s)])
            small_turn(J["scq"][0], s_cqn, 2, 3)
            pe.wait_ge(job_out, J["scq"][0] + 1)
            token_jobs(a_at["uq"], J["uq"][0], s_cqT, 2, [512] * 3)
            pe.wait_ge(pre["src"], 3)
            turn_blocks(J["qk3"][0], [((lambda t, s=s, k=k: s[:, t, k * P:(k + 1) * P]), P)
                                      for s in (s_q, s_p[:, :, 256:1280]) for k in range(8)])
            turn_blocks(J["ixt"][0], [((lambda t, k=k: s_qi[:, t, k * P:(k + 1) * P]), P)
                                      for k in range(4)] +
                        [((lambda t: s_ki[:, t, :, :].rearrange("p j n -> p (j n)")), P)])
            pe.wait_ge(job_out, J["ixt"][0] + 3)
            for i in range(IDX_H):
                if i >= 3:
                    pe.wait_ge(pre["ixr"], i - 2)
                b = 3 + i % 3
                q = half(s_QIT, i)
                kx = s_KIT[64 * (i % 2):64 * (i % 2) + 64, :]
                mm(ps[:, b, 0:P], q[:, 0:P], kx[:, 0:P], start=True, stop=True)
                mm(ps[:, b, P:3 * P], q[:, P:T], kx, start=True, stop=True).then_inc(pre["ix"], 1)
            pe.wait_ge(pre["ixr"], 8)
            attend(2, lambda u: half(s_QT, u), lambda u: half(s_KT, u),
                   lambda t, h: s_p[:, t, 1280 + h * 64:1280 + (h + 1) * 64], 64, s_soft)
            turn16("o3")
            out_proj(3)
            turn16("nm1")
            wait_hT("nm1")
            ffn("mlp1", hid, 4)

        @block.scalar
        def _(act):
            chain = [0]
            A_ = nc.scalar.activation

            def link(ins):
                chain[0] += 1
                ins.then_inc(act_c, 1)
                act.wait_ge(act_c, chain[0])

            eps = con[:, CON["eps"][0]:CON["eps"][0] + 1]
            eps_l = con[:, CON["eps"][0] + 1:CON["eps"][0] + 2]

            def root(name, out, in_, n, e):
                act.wait_ge(ss_rdy, SD[name] + 1)
                if e is None:
                    ins = A_(out, in_, ACT.Sqrt, scale=1.0 / n)
                else:
                    ins = A_(out, in_, ACT.Sqrt, bias=e, scale=1.0 / n)
                ins.then_inc(sd_rdy, 1)

            def norm(name):
                root(name, st[:, 2:4], st[:, 0:2], D, eps)

            def turned(name, gain, gain2=None):
                n = TI[name]
                for k in range(4, 8):
                    act.wait_ge(tp_rdy, 4 * n + k // 2 + 1)
                    src = ps[:, 4 + k // 2, (k % 2) * T:(k % 2) * T + T]
                    if gain2:
                        A_(hT2[:, k, :], src, ACT.Copy, scale=col(gain2, k))
                    if gain:
                        A_(hT[:, k, :], src, ACT.Copy, scale=col(gain, k)).then_inc(ha_rdy, 1)
                    else:
                        nc.scalar.copy(hT[:, k, :], src).then_inc(ha_rdy, 1)

            def res_root(mi):
                for t in range(NT):
                    act.wait_ge(m_rdy, 2 * mi + t + 1)
                    link(A_(xn[:, t, :], ps[:, 2 * t:2 * t + 2, :].rearrange("p b n -> p (b n)"),
                            ACT.Square, accum_out=st[:, 8 + t:9 + t]))
                    A_(st[:, 10 + t:11 + t], st[:, 8 + t:9 + t], ACT.Sqrt, bias=eps, scale=1.0 / D
                       ).then_inc(msd_rdy, 1)

            def job(j, *copies):
                act.wait_ge(job_rdy, j + 1)
                for f in copies:
                    last = f(ps[:, bank(j), :])
                last.then_inc(job_out, 1)

            def ffn(w, gelu):
                g0 = G0[w]

                def step(ch, par):
                    gp = (g0 + par) % 2
                    for q in range(2):
                        if gelu:
                            act.wait_ge(gc_rdy, ch * 2 + (2 * g0 + q + 1))
                            A_(ge[:, gp, q * T:(q + 1) * T], gc[:, gp, q * T:(q + 1) * T],
                               ACT.Gelu_apprx_tanh).then_inc(ge_rdy, 1)
                        else:
                            act.wait_ge(f1_rdy, ch * 2 + (2 * g0 + q + 1))
                            act.wait_ge(h_rdy, ch * 2 + (2 * g0 + q + 1 - 4))
                            A_(rl[:, gp, q, :], ps[:, 4 + 2 * gp + q, :], ACT.Relu
                               ).then_inc(ge_rdy, 1)

                chunk_walk(act, w, step)

            act.wait_ge(const_in, 16 * 9)
            act.wait_ge(wk["ang"], 1)
            A_(cs2[:, :, :, :], cs2[:, :, :, :], ACT.Sin).then_inc(wk["cs"], 1)
            norm("n0")
            turned("n0", "g0_mix")
            j = J["rkv"][0]
            for dst in (fm(rT), fm(kT_)):
                for s in range(4):
                    o = dst[:, 2 * s:2 * s + 2, :].rearrange("p k t -> p (k t)")
                    job(j, lambda p, o=o: nc.scalar.copy(o, p))
                    j += 1
            for half in range(2):
                for t in range(NT):
                    o = vtok[:, t * D + half * 512:t * D + half * 512 + 512]
                    job(j, lambda p, o=o: nc.scalar.copy(o, p))
                    j += 1
            job(j, lambda p: A_(lT[0:LORA, 0:T], p[0:LORA, 0:T], ACT.Tanh),
                lambda p: nc.scalar.copy(lT[0:LORA, T:2 * T], p[0:LORA, T:2 * T]))
            job(j + 1, lambda p: A_(sigg[:, 0:T], p[:, 0:T], ACT.Sigmoid),
                lambda p: A_(sigg[0:GLORA - P, T:2 * T], p[0:GLORA - P, T:2 * T], ACT.Sigmoid))
            j += 2
            for dst, bias in ((zs, "w0"), (aT, "a0")):
                for s in range(4):
                    job(j, *[lambda p, q=q: A_(fm(dst)[:, 2 * s + q, :], p[:, q * T:(q + 1) * T],
                                               ACT.Sigmoid, bias=col(bias, 2 * s + q))
                             for q in range(2)])
                    j += 1
            for s in range(4):
                job(j, lambda p: A_(xnflat[:, s * 512:(s + 1) * 512], p, ACT.Sqrt))
                j += 1
            job(j, lambda p: nc.scalar.copy(bon, p[:, 0:32]))
            j += 1
            act.wait_ge(wk["lc"], 1)
            act.wait_ge(wk["kkn"], 1)
            A_(eQ, zs, ACT.Exp).then_inc(wk["exp"], 1)
            A_(eN, Lc, ACT.Exp, scale=-1.0).then_inc(wk["exp"], 1)
            A_(eP, Lc, ACT.Exp).then_inc(wk["exp"], 1)
            A_(cl, cl, ACT.Exp).then_inc(wk["exp"], 1)
            for m in range(2):
                for s in range(2):
                    o = btk[:, m, s * 512:(s + 1) * 512]
                    job(j, lambda p, o=o: nc.scalar.copy(o, p))
                    j += 1
            for u, name, e in ORDER:
                if e != "a":
                    continue
                ch, hs = heads_of(u)
                L = lanes[u % 2]
                act.wait_ge(wk["mm"], PE_N[u, name])
                if name == "rhs":
                    for i in range(2):
                        last = nc.scalar.copy(L["R"][:, i * P:(i + 1) * P],
                                              ps[:, lane_bank(u, name, i), 0:P])
                elif name == "y0":
                    last = nc.scalar.copy(L["u0"], ps[:, lane_bank(u, name), 0:T])
                elif name == "Y":
                    for i in range(2):
                        yv = ytok.rearrange("p (c k i v) -> p c k i v", c=2, k=KT, i=2)
                        k = hs[0][1]
                        last = nc.scalar.copy(yv[:, ch, k:k + 2, i, :],
                                              ps[:, lane_bank(u, name, i), 0:P].rearrange(
                                                  "p (k v) -> p k v", k=2))
                else:
                    last = nc.scalar.copy(L[name], ps[:, lane_bank(u, name), :])
                last.then_inc(wk["cpa"], 1)
            root("lnx", gs_[:, 32:64], gs_[:, 0:32], HD, eps_l)
            turned("o0", None)
            res_root(0)
            norm("nf0")
            turned("nf0", "g0_ffn")
            ffn("ffn0", True)
            res_root(1)

            def attend(layer, softs):
                s_, pr, pT = soft(softs)
                diff = layer == 1
                per = 2 if diff else 1
                u0, h0 = 16 * layer, [0, 16, 24][layer]

                def turned_p(h):
                    act.wait_ge(pre["pt"], h0 + h + 1)
                    nc.scalar.copy(pT[:, (h0 + h) % 2, :], ps[:, 6 + (h0 + h) % 2, 0:384]
                                   ).then_inc(pre["pte"], 1)

                for u in range(16):
                    act.wait_ge(pre["s"], u0 + u + 1)
                    nm = st[:, 64 + 2 * u:66 + 2 * u]
                    sm = st[:, 96 + 2 * u:98 + 2 * u]
                    i = u % 4
                    A_(pr[:, i, 0:P], s_[:, (u0 + u) % 3, 0:P], ACT.Exp, bias=nm[:, 0:1],
                       accum_out=sm[:, 0:1])
                    A_(pr[:, i, P:384], s_[:, (u0 + u) % 3, P:384], ACT.Exp, bias=nm[:, 1:2],
                       accum_out=sm[:, 1:2]).then_inc(pre["e"], 1)
                    if diff and u % 2 and u >= 3:
                        turned_p(u // 2 - 1)
                    if not diff and u:
                        turned_p(u - 1)
                turned_p(16 // per - 1)

            norm("n1")
            turned("n1", "g1_mix", "g_kv")
            j = J["kvd"][0]
            for t in range(NT):
                job(j + t, lambda p: nc.scalar.copy(m_down[:, t, :], p[:, 0:288]))
            root("ckv", st[:, 18:20], st[:, 16:18], KV_LORA, eps)
            j = J["ckv"][0]
            job(j, *[lambda p, k=k: A_(m_ckvT[:, k, :], p[:, k * T:(k + 1) * T], ACT.Copy,
                                       scale=col("kv_a", k)) for k in range(2)])
            j = J["kvu"][0]
            for q in range(4):
                for t in range(NT):
                    def kpart(p):
                        return nc.scalar.copy(m_k[:, t, 4 * q:4 * q + 4, 0:64],
                                              p.rearrange("p (h n) -> p h n", h=4)[:, :, 0:64])

                    def vpart(p):
                        return nc.scalar.copy(
                            m_v[:, t, q * 256:(q + 1) * 256].rearrange("p (h n) -> p h n", h=4),
                            p.rearrange("p (h n) -> p h n", h=4)[:, :, 64:128])
                    job(j, kpart, vpart)
                    j += 1
            for t in range(NT):
                job(J["qd"][0] + t, lambda p: nc.scalar.copy(m_qd[:, t, :], p[:, 0:Q_LORA]))
            root("cq", st[:, 22:24], st[:, 20:22], Q_LORA, eps)
            j = J["cq"][0]
            job(j, *[lambda p, k=k: A_(m_cqT[:, k, :], p[:, k * T:(k + 1) * T], ACT.Copy,
                                       scale=col("q_n", k)) for k in range(2)])
            job(j + 1, lambda p: A_(m_cqT[:, 2, :], p[:, 0:T], ACT.Copy, scale=col("q_n", 2)))
            j = J["qu"][0]
            for q in range(4):
                for t in range(NT):
                    job(j, lambda p: nc.scalar.copy(m_q[:, t, 4 * q:4 * q + 4, :],
                                                    p[:, 0:384].rearrange("p (h n) -> p h n", h=4)))
                    j += 1
            j = J["qk1"][0]
            for dst in (m_QT, m_KT):
                for s in range(8):
                    job(j, lambda p: nc.scalar.copy(
                        dst[0:QD, 2 * s:2 * s + 2, :].rearrange("p h t -> p (h t)"), p[0:QD, :]))
                    j += 1
            attend(0, m_soft)
            turned("o1", None)
            res_root(2)
            norm("nf1")
            turned("nf1", "g1_ffn")
            ffn("ffn1", True)
            res_root(3)

            norm("n2")
            turned("n2", "n0_mix")
            j = J["din"][0]
            for i in range(3):
                for half in range(2):
                    for t in range(NT):
                        job(j, lambda p: nc.scalar.copy(d_p[:, i, t, half * 512:half * 512 + 512], p))
                        j += 1
            act.wait_ge(pre["src2"], 1)
            A_(d_lam[:, 2:4], d_lam[:, 0:2], ACT.Exp).then_inc(pre["osd"], 1)
            root("dqk", st[:, 192:256], st[:, 128:192], HD, eps)
            j = J["qk2"][0]
            for dst in (d_QT, d_KT):
                for s in range(4):
                    job(j, lambda p: nc.scalar.copy(
                        dst[:, 2 * s:2 * s + 2, :].rearrange("p h t -> p (h t)"), p))
                    j += 1
            attend(1, d_soft)
            root("dsub", st[:, 40:56], st[:, 24:40], 2 * HD, eps)
            turned("o2", None)
            norm("nm0")
            turned("nm0", "n0_mlp")
            ffn("mlp0", False)

            norm("n3")
            turned("n3", "n1_mix")
            j = J["sin"][0]
            for s in range(5):
                w = min(512, DSA_IN - 512 * s)
                for t in range(NT):
                    job(j, lambda p: nc.scalar.copy(s_p[:, t, s * 512:s * 512 + w], p[:, 0:w]))
                    j += 1
            root("scq", st[:, 18:20], st[:, 16:18], DSA_Q, eps)
            job(J["scq"][0], *[lambda p, k=k: A_(s_cqT[:, k, :], p[:, k * T:(k + 1) * T], ACT.Copy,
                                                 scale=col("cq_n", k)) for k in range(2)])
            root("kidx", st[:, 22:24], st[:, 20:22], 64, eps)
            j = J["uq"][0]
            for q in range(3):
                for t in range(NT):
                    dst = s_q[:, t, q * 512:(q + 1) * 512] if q < 2 else s_qi[:, t, :]
                    job(j, lambda p: nc.scalar.copy(dst, p))
                    j += 1
            root("sqk", st[:, 192:256], st[:, 128:192], HD, eps)
            j = J["qk3"][0]
            for dst in (s_QT, s_KT):
                for s in range(4):
                    job(j, lambda p: nc.scalar.copy(
                        dst[:, 2 * s:2 * s + 2, :].rearrange("p h t -> p (h t)"), p))
                    j += 1
            for s in range(2):
                job(j, lambda p: nc.scalar.copy(
                    s_QIT[:, 2 * s:2 * s + 2, :].rearrange("p h t -> p (h t)"), p))
                j += 1
            job(j, lambda p: nc.scalar.copy(s_KIT, p[:, 0:T]))
            for i in range(IDX_H):
                act.wait_ge(pre["ix"], i + 1)
                if i >= 2:
                    act.wait_ge(pre["ixs"], i - 1)
                A_(s_ixr[:, i % 2, :], ps[:, 3 + i % 3, 0:384], ACT.Relu).then_inc(pre["ixr"], 1)
            attend(2, s_soft)
            turned("o3", None)
            norm("nm1")
            turned("nm1", "n1_mlp")
            ffn("mlp1", False)

        @block.vector
        def _(dve):
            chain = [0]
            V = nc.vector

            def link(ins):
                chain[0] += 1
                ins.then_inc(dve_c, 1)
                dve.wait_ge(dve_c, chain[0])

            def norm(name, inst):
                for t in range(NT):
                    ins = V.tensor_tensor_reduce(xn[:, t, :], x[:, t, :], x[:, t, :], 1.0, 0.0,
                                                 ALU.mult, ALU.add, st[:, t:t + 1])
                ins.then_inc(ss_rdy, 1)
                dve.wait_ge(sd_rdy, SD[name] + 1)
                link(V.reciprocal(st[:, 4:6], st[:, 2:4]))
                for t in range(NT):
                    V.tensor_scalar(xn[:, t, :], x[:, t, :], st[:, 4 + t:5 + t], None, ALU.mult
                                    ).then_inc(xn_rdy, 1)

            def turned(name, gain, gain2=None):
                n = TI[name]
                for k in range(4):
                    dve.wait_ge(tp_rdy, 4 * n + k // 2 + 1)
                    src = ps[:, 4 + k // 2, (k % 2) * T:(k % 2) * T + T]
                    if gain2:
                        V.tensor_scalar(hT2[:, k, :], src, col(gain2, k), None, ALU.mult)
                    if gain:
                        ins = V.tensor_scalar(hT[:, k, :], src, col(gain, k), None, ALU.mult)
                    else:
                        ins = V.tensor_copy(hT[:, k, :], src)
                    ins.then_inc(hv_rdy, 1)

            def mview(t):
                return ps[:, 2 * t:2 * t + 2, :].rearrange("p b n -> p (b n)")

            def res_norm(mi, gain):
                for t in range(NT):
                    dve.wait_ge(msd_rdy, 2 * mi + t + 1)
                    link(V.reciprocal(st[:, 12 + t:13 + t], st[:, 10 + t:11 + t]))
                    link(V.scalar_tensor_tensor(xn[:, t, :], mview(t), st[:, 12 + t:13 + t], row(gain),
                                                ALU.mult, ALU.mult))
                    V.tensor_tensor(x[:, t, :], x[:, t, :], xn[:, t, :], ALU.add).then_inc(x_done, 1)
                dve.wait_ge(x_done, 2 * mi + 2)

            def res_plain(mi):
                for t in range(NT):
                    dve.wait_ge(m_rdy, 2 * mi + t + 1)
                    V.tensor_tensor(x[:, t, :], x[:, t, :], mview(t), ALU.add).then_inc(x_done, 1)
                dve.wait_ge(x_done, 2 * mi + 2)

            def ffn(w, layer=None):
                g0 = G0[w]
                n = INST.index(w)

                def free_h(ch):
                    if isinstance(ch, int):
                        if g0 + ch >= 2:
                            dve.wait_ge(*b_last(g0 + ch - 2))
                    else:
                        dve.wait_ge(b_used, ch + (g0 - n - 1))

                def chunk_conv(ch, par):
                    gp = (g0 + par) % 2
                    cw, cb = "conv_w%d" % layer, "conv_b%d" % layer
                    F = DFF // P
                    for step in range(3):
                        for q in range(2):
                            gate = ps[:, 4 + 2 * gp + q, 0:T]
                            o = gc[:, gp, q * T:(q + 1) * T]
                            f = ch * 2 + q
                            if step == 0:
                                dve.wait_ge(f1_rdy, ch * 2 + (2 * g0 + q + 1))
                                ins = V.tensor_scalar(o, gate, colx(cw, f + 2 * F), colx(cb, f),
                                                      ALU.mult, ALU.add)
                                ins.then_inc(wk["cv"], 1)
                            elif step == 1:
                                dve.wait_ge(wk["cv"], ch * 4 + (4 * g0 + q + 1))
                                V.scalar_tensor_tensor(o[:, 1:T], gate[:, 0:T - 1], colx(cw, f + F),
                                                       o[:, 1:T], ALU.mult, ALU.add
                                                       ).then_inc(wk["cv"], 1)
                            else:
                                dve.wait_ge(wk["cv"], ch * 4 + (4 * g0 + 2 + q + 1))
                                V.scalar_tensor_tensor(o[:, 2:T], gate[:, 0:T - 2], colx(cw, f),
                                                       o[:, 2:T], ALU.mult, ALU.add
                                                       ).then_inc(gc_rdy, 1)
                    free_h(ch)
                    for q in range(2):
                        dve.wait_ge(ge_rdy, ch * 2 + (2 * g0 + q + 1))
                        V.tensor_tensor(hid[:, gp, q * T:(q + 1) * T], ge[:, gp, q * T:(q + 1) * T],
                                        ps[:, 4 + 2 * gp + q, T:2 * T], ALU.mult).then_inc(h_rdy, 1)

                def chunk_sq(ch, par):
                    gp = (g0 + par) % 2
                    free_h(ch)
                    for q in range(2):
                        dve.wait_ge(ge_rdy, ch * 2 + (2 * g0 + q + 1))
                        V.tensor_tensor(hid[:, gp, q * 512:(q + 1) * 512], rl[:, gp, q, :],
                                        rl[:, gp, q, :], ALU.mult).then_inc(h_rdy, 1)

                chunk_walk(dve, w, chunk_sq if layer is None else chunk_conv)

            dve.wait_ge(const_in, 16 * 9)
            inv = con[:, CON["inv2"][0]:CON["inv2"][0] + 8]
            posf, ang = gs_[:, 0:2], st[:, 128:144].rearrange("p (t n) -> p t n", t=2)
            cnt = st[:, 144:176].rearrange("p (j t n) -> p j t n", j=2, t=2)
            link(V.tensor_copy(posf, posi[:, :]))
            for t in range(NT):
                ins = V.tensor_scalar(ang[:, t, :], inv, posf[:, t:t + 1], None, ALU.mult)
            link(ins)
            V.tensor_scalar(cnt[:, 0], ang, 1.0 / (2 * math.pi), 0.25, ALU.mult, ALU.add)
            link(V.tensor_scalar(cnt[:, 1], ang, 1.0 / (2 * math.pi), None, ALU.mult))
            link(V.tensor_scalar(cnt, cnt, MAGIC, None, ALU.add))
            link(V.tensor_scalar(cnt, cnt, -MAGIC, None, ALU.add))
            for j in range(2):
                ins = V.scalar_tensor_tensor(cs2[:, j], cnt[:, j], -TWO_PI[0], ang, ALU.mult, ALU.add)
            link(ins)
            link(V.scalar_tensor_tensor(cs2[:, :, :, :].rearrange("p j t n -> p (j t n)"),
                                        st[:, 144:176], -TWO_PI[1],
                                        cs2[:, :, :, :].rearrange("p j t n -> p (j t n)"),
                                        ALU.mult, ALU.add))
            link(V.scalar_tensor_tensor(cs2[:, :, :, :].rearrange("p j t n -> p (j t n)"),
                                        st[:, 144:176], -TWO_PI[2],
                                        cs2[:, :, :, :].rearrange("p j t n -> p (j t n)"),
                                        ALU.mult, ALU.add))
            link(V.tensor_scalar(cs2[:, 0], cs2[:, 0], math.pi / 2, None, ALU.add))
            V.tensor_scalar(cs2[:, :, :, :], cs2[:, :, :, :], 3.1415925, -3.1415925, ALU.min, ALU.max
                            ).then_inc(wk["ang"], 1)

            dve.wait_ge(x_in, 16)
            norm("n0", 0)
            turned("n0", "g0_mix")
            dve.wait_ge(hv_rdy, 4)
            dve.wait_ge(ha_rdy, 4)
            xf = fm(xx)
            V.tensor_scalar(xf[:, :, 0:1], hT[:, :, 0:1], -1.0, None, ALU.mult)
            link(V.tensor_tensor(xf[:, :, 1:T], hT[:, :, 0:T - 1], hT[:, :, 1:T], ALU.subtract))
            for i in range(6):
                if i >= 2:
                    dve.wait_ge(job_rdy, [4, 8, 12, 13][i - 2])
                for k in range(KT):
                    last = V.scalar_tensor_tensor(fm(xs[i % 2])[:, k, :], xf[:, k, :],
                                                  col("mu", 8 * i + k), hT[:, k, :],
                                                  ALU.mult, ALU.add)
                last.then_inc(xs_rdy, 1)
            dve.wait_ge(job_rdy, J["lora"][0] + 2)
            for k in range(KT):
                ins = V.tensor_scalar(fm(kkb)[:, k, :], fm(kT_)[:, k, :], col("k_k", k), None, ALU.mult)
            link(ins)
            V.tensor_tensor(xnflat, kkb, kkb, ALU.mult).then_inc(wk["sq"], 1)
            dve.wait_ge(job_out, J["az"][0] + 4)
            for k in range(KT):
                ins = V.tensor_scalar(fm(k2)[:, k, :], fm(aT)[:, k, :], 1.0, col("k_a", k),
                                      ALU.subtract, ALU.mult)
            link(ins)
            link(V.scalar_tensor_tensor(k2, k2, 1.0, kT_, ALU.add, ALU.mult))
            for k in range(KT):
                last = V.scalar_tensor_tensor(hT[:, k, :], fm(rT)[:, k, :], col("r_k", k),
                                              fm(k2)[:, k, :], ALU.mult, ALU.mult)
            last.then_inc(wk["rkp"], 1)
            link(V.tensor_scalar(zs, zs, -E05, None, ALU.mult))
            ones = cst("ones")
            for s in range(2 * KT):
                ins = V.tensor_tensor_scan(Lc[:, s * P:(s + 1) * P], ones, zs[:, s * P:(s + 1) * P],
                                           0.0, ALU.mult, ALU.add)
            link(ins)
            L3 = Lc.rearrange("p (s t) -> p s t", t=P)
            link(V.tensor_copy(lm, L3[:, :, P // 2 - 1]))
            link(V.tensor_tensor(L3, L3, bc(lm, 2, P), ALU.subtract))
            V.tensor_tensor(zs, Lc, zs, ALU.subtract)
            lms = lm.rearrange("p (k c) -> p k c", c=2)
            L4 = Lc.rearrange("p (k c t) -> p k c t", c=2, t=P)
            V.tensor_tensor(cl, L4[:, :, 0, P - 1], lms[:, :, 1], ALU.add).then_inc(wk["lc"], 1)
            dve.wait_ge(job_out, J["kk"][0] + 4)
            link(V.tensor_scalar(xnflat, xnflat, 1e-12, None, ALU.max))
            link(V.reciprocal(xnflat, xnflat))
            V.tensor_tensor(kkb, kkb, xnflat, ALU.mult).then_inc(wk["kkn"], 1)
            dve.wait_ge(wk["kkn"], 1)
            dve.wait_ge(wk["exp"], 1)
            a5 = AR[:, :, :, 0, :]
            r5 = AR[:, :, :, 1, :]

            def v4(ap):
                return ap.rearrange("p (k c t) -> p k c t", c=2, t=P)

            for c_ in range(2):
                V.scalar_tensor_tensor(a5[:, :, c_, :], v4(kkb)[:, :, c_, :], -1.0, v4(eQ)[:, :, c_, :],
                                       ALU.mult, ALU.mult)
            link(V.tensor_tensor(aT, aT, kkb, ALU.mult))
            dve.wait_ge(wk["exp"], 2)
            V.tensor_tensor(aT, aT, eN, ALU.mult)
            V.tensor_tensor(k2, k2, eN, ALU.mult)
            dve.wait_ge(wk["exp"], 4)
            for c_ in range(2):
                last = V.tensor_tensor(r5[:, :, c_, :], v4(rT)[:, :, c_, :], v4(eP)[:, :, c_, :],
                                       ALU.mult)
            last.then_inc(wk["ops"], 1)
            dve.wait_ge(wk["ops"], 1)
            for L in lanes:
                for n_ in ("NdT", "rb", "ak", "rk", "Nd", "No"):
                    last = V.memset(L[n_], 0.0)
            last.then_inc(wk["clr"], 1)
            dve.wait_ge(wk["clr"], 1)

            def h4(ap, i):
                return ap.rearrange("p (q t) -> p q t", q=4)[:, 2 * i:2 * i + 2, :]

            for u, name, e in ORDER:
                if e != "v":
                    continue
                ch, hs = heads_of(u)
                L = lanes[u % 2]
                dve.wait_ge(wk["mm"], PE_N[u, name])
                if name in ("sb", "sk"):
                    for i in range(2):
                        p4 = ps[:, lane_bank(u, name, i), :].rearrange("p (q j t) -> p q j t", q=2, j=2)
                        for j, (dst, m) in enumerate((("NdT", "dstrict"), ("rb", "incl"))
                                                     if name == "sb" else
                                                     (("ak", "strict"), ("rk", "incl"))):
                            last = V.copy_predicated(h4(L[dst], i), bc(mask(m), 1, 2), p4[:, :, j, :])
                elif name == "sn":
                    for i in range(2):
                        p4 = ps[:, lane_bank(u, name, i), 0:T].rearrange("p (q t) -> p q t", q=2)
                        V.copy_predicated(h4(L["Nd"], i), bc(mask("dlow"), 1, 2), p4)
                        V.copy_predicated(h4(L["No"], i), bc(mask("olow"), 1, 2), p4)
                    last = V.tensor_tensor(L["E"].rearrange("p (q t) -> p q t", q=4),
                                           L["NdT"].rearrange("p (q t) -> p q t", q=4),
                                           bc(ident, 1, 4), ALU.add)
                elif name in ("E2", "E3", "E4"):
                    last = V.tensor_tensor(L["E"], L["E"], ps[:, lane_bank(u, name), :], ALU.add)
                elif name in ("MT", "M4T"):
                    last = V.tensor_copy(L[name], ps[:, lane_bank(u, name), :])
                elif name in ("y1", "y2", "U"):
                    src, dst = ("u1", "u0") if name == "y2" else ("u0", "u1")
                    last = V.tensor_tensor(L[dst], L[src], ps[:, lane_bank(u, name), 0:T], ALU.add)
                else:
                    b = lane_bank(u, name)
                    for q in range(2):
                        k = hs[q][1]
                        for p0 in (0, 64):
                            o = q * P + p0
                            last = V.tensor_scalar(Sst[p0:p0 + 64, k, :], ps[p0:p0 + 64, b, o:o + 64],
                                                   cl[p0:p0 + 64, k:k + 1], None, ALU.mult)
                last.then_inc(wk["cpv"], 1)

            dve.wait_ge(*EV_N[7, "Y"])
            y3 = ytok.rearrange("p (g v) -> p g v", v=64)
            x3 = xnflat.rearrange("p (g v) -> p g v", v=64)
            v3 = vtok.rearrange("p (g v) -> p g v", v=64)
            link(V.tensor_reduce(gs_[:, 0:32], y3, AX_X, ALU.add))
            link(V.tensor_scalar(gs_[:, 0:32], gs_[:, 0:32], 1.0 / HD, None, ALU.mult))
            link(V.tensor_tensor(y3, y3, bc(gs_[:, 0:32], 2, 64), ALU.subtract))
            link(V.tensor_tensor(xnflat, ytok, ytok, ALU.mult))
            V.tensor_reduce(gs_[:, 0:32], x3, AX_X, ALU.add).then_inc(ss_rdy, 1)
            dve.wait_ge(sd_rdy, SD["lnx"] + 1)
            link(V.reciprocal(gs_[:, 0:32], gs_[:, 32:64]))
            link(V.tensor_tensor(y3, y3, bc(gs_[:, 0:32], 2, 64), ALU.mult))
            yt = ytok.rearrange("p (t n) -> p t n", t=2)
            link(V.tensor_tensor(yt, yt, bc(row("lnx_w"), 1, 2), ALU.mult))
            V.tensor_tensor(x3, v3, bc(bon, 2, 64), ALU.mult)
            link(V.tensor_tensor(yt, yt, bc(row("lnx_b"), 1, 2), ALU.add))
            link(V.tensor_tensor(ytok, ytok, xnflat, ALU.add))
            dve.wait_ge(wk["g"], 1)
            for t in range(NT):
                V.tensor_tensor(xn[:, t, :], yt[:, t, :], mview(t), ALU.mult).then_inc(xn_rdy, 1)
            turned("o0", None)
            res_norm(0, "g0_res")
            norm("nf0", 2)
            turned("nf0", "g0_ffn")
            ffn("ffn0", 0)
            res_norm(1, "g0_fres")

            def attend(layer, dv, softs, scale, add):
                s_, pr, _ = soft(softs)
                diff = layer == 1
                u0, h0 = 16 * layer, [0, 16, 24][layer]

                def out(h):
                    dve.wait_ge(pre["o"], h0 + h + 1)
                    b = (h0 + h) % 2
                    for t in range(NT):
                        dst = xn[:, t, h * dv:(h + 1) * dv]
                        src = ps[:, b, t * dv:(t + 1) * dv]
                        if diff:
                            ins = V.tensor_copy(dst, src)
                        else:
                            ins = V.tensor_scalar(dst, src, st[:, 128 + 2 * h + t:129 + 2 * h + t],
                                                  None, ALU.mult)
                    ins.then_inc(pre["ov"], 1)

                def combine(h):
                    u = 2 * h
                    dve.wait_ge(pre["e"], u0 + u + 2)
                    r = st[:, 128 + 4 * h:132 + 4 * h]
                    link(V.reciprocal(r, st[:, 96 + 2 * u:100 + 2 * u]))
                    V.tensor_scalar(pr[:, u % 4, 0:P], pr[:, u % 4, 0:P], r[:, 0:1], None, ALU.mult)
                    V.tensor_scalar(pr[:, u % 4, P:384], pr[:, u % 4, P:384], r[:, 1:2], None, ALU.mult)
                    link(V.tensor_scalar(r[:, 2:4], r[:, 2:4], d_lam[:, 5:6], None, ALU.mult))
                    V.scalar_tensor_tensor(pr[:, u % 4, 0:P], pr[:, u % 4 + 1, 0:P], r[:, 2:3],
                                           pr[:, u % 4, 0:P], ALU.mult, ALU.add)
                    V.scalar_tensor_tensor(pr[:, u % 4, P:384], pr[:, u % 4 + 1, P:384], r[:, 3:4],
                                           pr[:, u % 4, P:384], ALU.mult, ALU.add
                                           ).then_inc(pre["p"], 1)

                for u in range(16):
                    dve.wait_ge(pre["sc"], u0 + u + 1)
                    if u >= 3:
                        dve.wait_ge(pre["e"], u0 + u - 2)
                    s1 = s_[:, (u0 + u) % 3, :]
                    link(V.scalar_tensor_tensor(s1, ps[:, 3 + (u0 + u) % 3, 0:384], scale, add,
                                                ALU.mult, ALU.add))
                    V.tensor_reduce(st[:, 64 + 2 * u:65 + 2 * u], s1[:, 0:P], AX_X, ALU.max,
                                    negate=True)
                    V.tensor_reduce(st[:, 65 + 2 * u:66 + 2 * u], s1[:, P:384], AX_X, ALU.max,
                                    negate=True).then_inc(pre["s"], 1)
                    if diff:
                        if u % 2 and u >= 3:
                            combine(u // 2 - 1)
                            if u >= 5:
                                out(u // 2 - 2)
                    elif u >= 2:
                        h = u - 2
                        dve.wait_ge(pre["e"], u0 + h + 1)
                        link(V.reciprocal(st[:, 128 + 2 * h:130 + 2 * h], st[:, 96 + 2 * h:98 + 2 * h]))
                        if h:
                            out(h - 1)
                if diff:
                    combine(7)
                    out(6)
                    out(7)
                else:
                    for h in (14, 15):
                        dve.wait_ge(pre["e"], u0 + h + 1)
                        link(V.reciprocal(st[:, 128 + 2 * h:130 + 2 * h], st[:, 96 + 2 * h:98 + 2 * h]))
                        out(h - 1)
                    out(15)
                dve.wait_ge(pre["ov"], h0 + 16 // (2 if diff else 1))

            def rms_tiles(name, src, n, at, dst, scale=None):
                for t in range(NT):
                    ins = V.tensor_tensor_reduce(dst[:, t, :], src[:, t, :], src[:, t, :], 1.0, 0.0,
                                                 ALU.mult, ALU.add, st[:, at + t:at + t + 1])
                ins.then_inc(ss_rdy, 1)
                dve.wait_ge(sd_rdy, SD[name] + 1)
                link(V.reciprocal(st[:, at:at + 2], st[:, at + 2:at + 4]))
                for t in range(NT):
                    ins = V.tensor_scalar(dst[:, t, :], src[:, t, :], st[:, at + t:at + t + 1], None,
                                          ALU.mult)
                return ins

            def rotate(x1, x2, cos, sin, tmp, last=False):
                V.tensor_tensor(tmp[0], x1, cos, ALU.mult)
                V.tensor_tensor(tmp[1], x2, sin, ALU.mult)
                V.tensor_tensor(tmp[2], x1, sin, ALU.mult)
                link(V.tensor_tensor(tmp[3], x2, cos, ALU.mult))
                V.tensor_tensor(x1, tmp[0], tmp[1], ALU.subtract)
                ins = V.tensor_tensor(x2, tmp[2], tmp[3], ALU.add)
                if last:
                    ins.then_inc(pre["src"], 1)
                else:
                    link(ins)

            def quarters(buf, h, n):
                return [buf[:, i * h * n:(i + 1) * h * n].rearrange("p (h n) -> p h n", h=h)
                        for i in range(4)]

            norm("n1", 3)
            turned("n1", "g1_mix", "g_kv")
            dve.wait_ge(job_out, J["kvd"][0] + 2)
            rms_tiles("ckv", m_down[:, :, 0:KV_LORA], KV_LORA, 16, m_ckvn).then_inc(pre["tsm"], 1)
            cos1 = cst("cos1").rearrange("p (t n) -> p t n", t=2)
            sin1 = cst("sin1").rearrange("p (t n) -> p t n", t=2)
            rotate(m_down[:, :, 256:272], m_down[:, :, 272:288], cos1, sin1, quarters(m_rt, 2, 16))
            for t in range(NT):
                V.tensor_copy(m_k[:, t, :, 64:96], bc(m_down[:, t, 256:288], 1, H))
            dve.wait_ge(job_out, J["qd"][0] + 2)
            rms_tiles("cq", m_qd, Q_LORA, 20, m_cqn).then_inc(pre["tsm"], 1)
            dve.wait_ge(job_out, J["qu"][0] + 8)
            for t in range(NT):
                rotate(m_q[:, t, :, 64:80], m_q[:, t, :, 80:96], bc(cos1[:, t, :], 1, H),
                       bc(sin1[:, t, :], 1, H), quarters(m_rt, H, 16), last=(t == 1))
            dve.wait_ge(job_out, J["qk1"][0] + 16)
            attend(0, 64, m_soft, 1.0 / math.sqrt(QD), cst("amask"))
            turned("o1", None)
            res_norm(2, "g1_res")
            norm("nf1", 5)
            turned("nf1", "g1_ffn")
            ffn("ffn1", 1)
            res_norm(3, "g1_fres")

            def head_norm(name, parts, tmp):
                for i, (src, _g) in enumerate(parts):
                    s4 = src.rearrange("p t (h n) -> p t h n", h=H)
                    t4 = tmp[:, i * 2048:(i + 1) * 2048].rearrange("p (t h n) -> p t h n", t=2, h=H)
                    V.tensor_tensor(t4, s4, s4, ALU.mult).then_inc(pre["osq"], 1)
                n0 = {"dqk": 0, "sqk": 2}[name]
                dve.wait_ge(pre["osq"], n0 + 2)
                V.tensor_reduce(st[:, 128:192], tmp[:, 0:4096].rearrange("p (g n) -> p g n", n=64),
                                AX_X, ALU.add).then_inc(ss_rdy, 1)
                dve.wait_ge(sd_rdy, SD[name] + 1)
                link(V.reciprocal(st[:, 128:192], st[:, 192:256]))
                for i, (src, g) in enumerate(parts):
                    for t in range(NT):
                        s3 = src[:, t, :].rearrange("p (h n) -> p h n", h=H)
                        r = st[:, 128 + 32 * i + 16 * t:144 + 32 * i + 16 * t]
                        ins = V.tensor_tensor(s3, s3, bc(r, 2, 64), ALU.mult)
                link(ins)
                for i, (src, g) in enumerate(parts):
                    for t in range(NT):
                        s3 = src[:, t, :].rearrange("p (h n) -> p h n", h=H)
                        ins = V.tensor_tensor(s3, s3, bc(row(g), 1, H), ALU.mult)
                link(ins)

            def rope2(src, h, tmp, last=False):
                for t in range(NT):
                    s3 = src[:, t, :].rearrange("p (h n) -> p h n", h=h)
                    rotate(s3[:, :, 0:8], s3[:, :, 8:16], bc(cs2[:, 0, t, :], 1, h),
                           bc(cs2[:, 1, t, :], 1, h), quarters(tmp, h, 8), last and t == 1)

            norm("n2", 6)
            turned("n2", "n0_mix")
            a, _n = ROW["lam"]
            for i in range(2):
                last = V.tensor_tensor_reduce(d_rt[:, i * 64:(i + 1) * 64],
                                              rows[:, a + 128 * i:a + 128 * i + 64],
                                              rows[:, a + 128 * i + 64:a + 128 * i + 128], 1.0, 0.0,
                                              ALU.mult, ALU.add, d_lam[:, i:i + 1])
            last.then_inc(pre["src2"], 1)
            dve.wait_ge(job_out, J["din"][0] + 12)
            head_norm("dqk", [(d_p[:, 0], "dq"), (d_p[:, 1], "dk")], d_sq)
            dve.wait_ge(pre["osd"], 1)
            link(V.tensor_tensor(d_lam[:, 4:5], d_lam[:, 3:4], d_lam[:, 2:3], ALU.subtract))
            link(V.tensor_scalar(d_lam[:, 5:6], d_lam[:, 4:5], LAM_INIT, None, ALU.subtract))
            dve.wait_ge(wk["cs"], 1)
            rope2(d_p[:, 0], H, d_rt)
            rope2(d_p[:, 1], H, d_rt, last=True)
            attend(1, P, d_soft, HD ** -0.5, cst("amask"))
            link(V.tensor_tensor(d_sq[:, 0:2048], xnflat, xnflat, ALU.mult))
            V.tensor_reduce(st[:, 24:40], d_sq[:, 0:2048].rearrange("p (g n) -> p g n", n=P), AX_X,
                            ALU.add).then_inc(ss_rdy, 1)
            dve.wait_ge(sd_rdy, SD["dsub"] + 1)
            link(V.reciprocal(st[:, 24:40], st[:, 40:56]))
            link(V.tensor_scalar(st[:, 24:40], st[:, 24:40], 1.0 - LAM_INIT, None, ALU.mult))
            xg = xnflat.rearrange("p (g n) -> p g n", n=P)
            link(V.tensor_tensor(xg, xg, bc(st[:, 24:40], 2, P), ALU.mult))
            for t in range(NT):
                V.tensor_tensor(xg[:, 8 * t:8 * t + 8, :], xg[:, 8 * t:8 * t + 8, :],
                                bc(row("sub"), 1, 8), ALU.mult).then_inc(xn_rdy, 1)
            turned("o2", None)
            res_plain(4)
            norm("nm0", 8)
            turned("nm0", "n0_mlp")
            ffn("mlp0")
            res_plain(5)

            norm("n3", 9)
            turned("n3", "n1_mix")
            dve.wait_ge(job_out, J["sin"][0] + 10)
            rms_tiles("scq", s_p[:, :, 0:256], 256, 16, s_cqn).then_inc(pre["tsm"], 1)
            ki = s_ki[:, :, 0, :]
            link(rms_tiles("kidx", s_p[:, :, 2304:2368], 64, 20, ki))
            rope2(ki, 1, s_rt)
            V.tensor_copy(s_ki[:, :, 1, :], ki)
            link(V.tensor_scalar(s_p[:, :, 2368:2376], s_p[:, :, 2368:2376],
                                 IDX_H ** -0.5 * 64 ** -0.5, None, ALU.mult))
            dve.wait_ge(job_out, J["uq"][0] + 6)
            head_norm("sqk", [(s_q, "sq"), (s_p[:, :, 256:1280], "sk")], s_sq)
            rope2(s_q, H, s_rt)
            rope2(s_p[:, :, 256:1280], H, s_rt)
            rope2(s_qi, IDX_H, s_rt, last=True)
            for i in range(IDX_H):
                dve.wait_ge(pre["ixr"], i + 1)
                for t, (lo, hi) in enumerate(((0, P), (P, 384))):
                    w = s_p[:, t, 2368 + i:2369 + i]
                    r = s_ixr[:, i % 2, lo:hi]
                    if i == 0:
                        ins = V.tensor_scalar(s_acc[:, lo:hi], r, w, None, ALU.mult)
                    else:
                        ins = V.scalar_tensor_tensor(s_acc[:, lo:hi], r, w, s_acc[:, lo:hi],
                                                     ALU.mult, ALU.add)
                ins.then_inc(pre["ixs"], 1)
                dve.wait_ge(pre["ixs"], i + 1)
            link(V.tensor_tensor(s_w, s_acc, cst("amask"), ALU.add))
            m8 = st[:, 32:48]
            for r in range(TOPK // 8):
                for t, (lo, hi) in enumerate(((0, P), (P, 384))):
                    ins = V.max(m8[:, 8 * t:8 * t + 8], s_w[:, lo:hi])
                link(ins)
                for t, (lo, hi) in enumerate(((0, P), (P, 384))):
                    ins = V.match_replace(s_w[:, lo:hi], m8[:, 8 * t:8 * t + 8], s_w[:, lo:hi], TAKEN)
                link(ins)
            link(V.tensor_scalar(s_sel, s_w, TAKEN, -NEG, ALU.is_equal, ALU.mult))
            link(V.tensor_scalar(s_sel, s_sel, NEG, None, ALU.add))
            attend(2, 64, s_soft, HD ** -0.5, s_sel)
            turned("o3", None)
            res_plain(6)
            norm("nm1", 11)
            turned("nm1", "n1_mlp")
            ffn("mlp1")
            res_plain(7)


def constants():
    con, ncon = offsets(CONSTS)
    c = np.zeros((P, ncon), np.float32)

    def put(name, v):
        a, n = con[name]
        c[:, a:a + n] = v

    p = np.arange(P)
    put("ident", np.eye(P))
    put("blk1", (p[:, None] // 64 == p[None, :] // 64))
    put("sel2", (p[:, None] // 64 == np.arange(2)[None, :]))
    m = np.zeros((P, 384))
    m[:64, 64:128] = NEG
    m[:64, 320:384] = NEG
    put("amask", m)
    inv = (np.float32(1.0) / (np.float32(10000.0) ** (np.arange(0, QK_ROPE, 2, dtype=np.float32) / np.float32(QK_ROPE))))
    ang = np.arange(T, dtype=np.float32)[:, None] * inv[None, :].astype(np.float32)
    for name, f in (("cos1", np.cos), ("sin1", np.sin)):
        put(name, f(ang.astype(np.float64)).reshape(2, P, 16).transpose(1, 0, 2).reshape(P, 32))
    put("inv2", (np.float32(500000.0) ** (-np.arange(0, 16, 2, dtype=np.float32) / np.float32(16)))[None, :])
    put("eps", np.array([[EPS_NORM, EPS_LNX]]))
    put("ones", 1.0)
    a, b = p[:, None], p[None, :]
    ms = {"incl": a <= b, "strict": a < b, "dstrict": (a < b) & (a // 16 == b // 16),
          "dlow": (b < a) & (a // 16 == b // 16), "olow": (b < a) & (a // 16 != b // 16)}
    return c, np.concatenate([ms[n].astype(np.float32) for n in MASKS], axis=1)


def kernel(**inputs):
    import concourse.bacc as bacc
    from concourse.bass_utils import run_bass_kernel_spmd

    g = {k: np.asarray(v) for k, v in inputs.items()}

    def tiles(v):
        return np.ascontiguousarray(v.reshape(-1, P).T)

    parts = {"g0_mix": g["norm_g"][0, 0], "g0_ffn": g["norm_g"][0, 2], "g1_mix": g["norm_g"][1, 0],
             "g_kv": g["kv_norm_g"], "g1_ffn": g["norm_g"][1, 2], "n0_mix": g["norm_mix_2"][0],
             "n0_mlp": g["norm_mlp_2"][0], "n1_mix": g["norm_mix_2"][1], "n1_mlp": g["norm_mlp_2"][1],
             "mu": g["a_mu"][0], "w0": g["a_w0"], "a0": g["a_a0"], "k_k": g["a_k_k"],
             "k_a": g["a_k_a"], "r_k": g["a_r_k"], "kv_a": g["kv_a_norm_g"], "q_n": g["q_norm_g"],
             "cq_n": g["dsa_cq_norm_2"], "conv_w0": g["ffn_conv_w"][0], "conv_b0": g["ffn_conv_b"][0],
             "conv_w1": g["ffn_conv_w"][1], "conv_b1": g["ffn_conv_b"][1]}
    rws = {"g0_res": g["norm_g"][0, 1], "g0_fres": g["norm_g"][0, 3], "g1_res": g["norm_g"][1, 1],
           "g1_fres": g["norm_g"][1, 3], "lnx_w": g["a_lnx_w"], "lnx_b": g["a_lnx_b"],
           "dq": g["diff_q_norm_2"], "dk": g["diff_k_norm_2"], "sub": g["diff_subln_2"],
           "sq": g["dsa_q_norm_2"], "sk": g["dsa_k_norm_2"],
           "lam": np.concatenate([g[n].reshape(-1) for n in
                                  ("diff_lam_q1_2", "diff_lam_k1_2", "diff_lam_q2_2", "diff_lam_k2_2")])}
    con, masks = constants()
    arrays = {
        "x": g["x"][0], "positions": tiles(g["positions_2"]), "con": con, "masks": masks,
        "cols": np.concatenate([tiles(parts[n]) for n, _ in COLS], axis=1),
        "rows": np.concatenate([rws[n].reshape(1, -1) for n, _ in ROWS], axis=1),
        "w_r": g["a_w_rkv"][0, 0], "w_k": g["a_w_rkv"][0, 1], "w_v": g["a_w_rkv"][0, 2],
        "w_lora": np.concatenate([g["a_w1"][0], g["a_a1"][0], g["a_g1"][0]], axis=1),
        "a_w2": g["a_w2"][0], "a_a2": g["a_a2"][0], "a_g2": g["a_g2"][0], "a_w_o": g["a_w_o"][0],
        "kv_w_down": g["kv_w_down"], "kv_w_up": g["kv_w_up"], "q_w_down": g["q_w_down"][0],
        "q_w_up": g["q_w_up"][0], "o_w": g["o_w"][0], "diff_w_in": g["diff_w_in_2"][0],
        "diff_w_out": g["diff_w_out_2"][0], "dsa_w_in": g["dsa_w_in_2"][0],
        "w_uqi": np.concatenate([g["dsa_w_uq_2"][0], g["dsa_w_uq_idx_2"][0]], axis=1),
        "dsa_w_out": g["dsa_w_out_2"][0],
    }
    for n in range(2):
        arrays["ffn_w_in%d" % n] = g["ffn_w_in"][n]
        arrays["ffn_w_out%d" % n] = g["ffn_w_out"][n]
        arrays["mlp_w1_%d" % n] = g["mlp_w1_2"][n]
        arrays["mlp_w2_%d" % n] = g["mlp_w2_2"][n]
    arrays = {"in_" + k: np.ascontiguousarray(v) for k, v in arrays.items()}
    nc = bacc.Bacc("TRN2", target_bir_lowering=False, num_devices=1)
    d = {k[3:]: nc.dram_tensor(k, v.shape, mybir.dt.from_np(v.dtype), kind="ExternalInput").ap()
         for k, v in arrays.items()}
    out = nc.dram_tensor("out", (T, D), F32, kind="ExternalOutput").ap()
    program(nc, d, out)
    r = run_bass_kernel_spmd(nc, [arrays], core_ids=[0])
    return r.results[0]["out"].reshape(1, T, D)
```

```python
from contextlib import ExitStack
import math

import numpy as np
import concourse.bass as bass
from concourse import mybir

F32 = mybir.dt.float32
F32R = mybir.dt.float32r
I32 = mybir.dt.int32
ALU = mybir.AluOpType
ACT = mybir.ActivationFunctionType
AX_X = mybir.AxisListType.X

P = 128
T = 256
NT = T // P
D = 1024
KT = D // P
DFF = 2816
DFF2 = 4096
H = 16
HD = 64
LORA = 64
GLORA = 160
KV_LORA = 256
QK_ROPE = 32
QK_NOPE = 64
QD = QK_NOPE + QK_ROPE
Q_LORA = 384
TOPK = min(256, T // 4)
IDX_H = 8
EPS_NORM = 1e-6
EPS_LNX = 64e-5
NEG = -1e30
PAD = -3.0e38
TAKEN = -3.3e38
DSA_Q = 256
MAGIC = 1.5 * 2 ** 23
TWO_PI = (6.28125, 253 / 2 ** 17, 2 * math.pi - 6.28125 - 253 / 2 ** 17)
E05 = math.exp(-0.5)
LAM_INIT = 0.8 - 0.6 * math.exp(-0.3 * 0)

COLS = [("g0_mix", 8), ("g0_ffn", 8), ("g1_mix", 8), ("g_kv", 8), ("g1_ffn", 8), ("n0_mix", 8),
        ("n0_mlp", 8), ("n1_mix", 8), ("n1_mlp", 8), ("mu", 48), ("w0", 8), ("a0", 8), ("k_k", 8),
        ("k_a", 8), ("r_k", 8), ("kv_a", 2), ("q_n", 3), ("cq_n", 2), ("conv_w0", 66),
        ("conv_b0", 22), ("conv_w1", 66), ("conv_b1", 22)]
ROWS = [("g0_res", D), ("g0_fres", D), ("g1_res", D), ("g1_fres", D), ("lnx_w", D), ("lnx_b", D),
        ("dq", 64), ("dk", 64), ("sub", 128), ("sq", 64), ("sk", 64), ("lam", 256)]
CONSTS = [("ident", 128), ("blk1", 128), ("sel2", 2), ("amask", 384), ("cos1", 32), ("sin1", 32),
          ("inv2", 8), ("eps", 2), ("ones", 128)]
MASKS = ["incl", "strict", "dstrict", "dlow", "olow"]


def offsets(table):
    at, out = 0, {}
    for name, n in table:
        out[name] = (at, n)
        at += n
    return out, at


def program(nc, d, out_d):
    COL, NCOL = offsets(COLS)
    ROW, NROW = offsets(ROWS)
    CON, NCON = offsets(CONSTS)
    ctx = ExitStack()
    with ctx:
        place = {}
        free = [nc.sbuf_base + -nc.sbuf_base % 32]

        def sb(name, shape, dt=F32):
            place[name] = free[0]
            free[0] += 4 * math.prod(shape[1:]) + (-4 * math.prod(shape[1:])) % 32
            return nc.alloc_sbuf_tensor_at(name, shape, dt, offset=place[name])

        def over(name, base, at, shape, dt=F32R):
            return nc.alloc_sbuf_tensor_at(name, shape, dt, offset=place[base] + 4 * at)

        def sem(name):
            return ctx.enter_context(nc.semaphore(name))

        ps = ctx.enter_context(nc.psum_tensor("ps", [P, 8, 512], F32))
        ringA = sb("ringA", [P, 2, 4096])
        ringB = sb("ringB", [P, 2, 4096])
        x = sb("x", [P, NT, D])
        hT = sb("hT", [P, KT, T])
        xn = sb("xn", [P, NT, D])
        cols = sb("cols", [P, NCOL])
        rows = sb("rows", [P, NROW])
        con = sb("con", [P, NCON])
        masks = sb("masks", [P, len(MASKS), P])
        posi = sb("posi", [P, NT], I32)
        cs2 = sb("cs2", [P, 2, NT, 8])
        st = sb("st", [P, 256])
        NAR = 21640
        arena = sb("arena", [P, NAR])
        Ah = over("Ah", "arena", 0, [P, 2, 2048])
        Al = over("Al", "arena", 4096, [P, 2, 2048])
        Bh = over("Bh", "arena", 8192, [P, 2, 2048])
        Bl = over("Bl", "arena", 12288, [P, 2, 2048])
        hTl = over("hTl", "arena", 16384, [P, KT, T])
        hidh = over("hidh", "arena", 18432, [P, 2, 512])
        hidl = over("hidl", "arena", 19456, [P, 2, 512])
        hTh = over("hTh", "hT", 0, [P, KT, T])

        def col(name, k):
            return cols[:, COL[name][0] + k:COL[name][0] + k + 1]

        def colx(name, k):
            return cols[:, bass.ds(COL[name][0] + k, 1)]

        def row(name):
            a, n = ROW[name]
            return rows[:, a:a + n]

        def cst(name):
            a, n = CON[name]
            return con[:, a:a + n]

        ident = cst("ident")

        def mask(name):
            return masks[:, MASKS.index(name), :].bitcast(I32)

        class Carve:
            def __init__(self):
                self.at = 0

            def __call__(self, n):
                a = self.at
                self.at += n
                assert self.at <= NAR, self.at
                return arena[:, a:a + n]

        const_in = sem("const_in")
        x_in = sem("x_in")
        a_loaded = [sem("a_loaded0"), sem("a_loaded1")]
        b_loaded = [sem("b_loaded0"), sem("b_loaded1")]
        a_used = sem("a_used")
        ah_rdy = sem("ah_rdy")
        al_rdy = sem("al_rdy")
        bh_rdy = sem("bh_rdy")
        bl_rdy = sem("bl_rdy")
        b_used = sem("b_used")
        ht_rdy = sem("ht_rdy")
        out_done = sem("out_done")
        dve_c = sem("dve_c")
        act_c = sem("act_c")
        ss_rdy = sem("ss_rdy")
        sd_rdy = sem("sd_rdy")
        xn_rdy = sem("xn_rdy")
        tp_rdy = sem("tp_rdy")
        hv_rdy = sem("hv_rdy")
        ha_rdy = sem("ha_rdy")
        job_rdy = sem("job_rdy")
        job_out = sem("job_out")
        m_rdy = sem("m_rdy")
        msd_rdy = sem("msd_rdy")
        x_done = sem("x_done")
        f1_rdy = sem("f1_rdy")
        gc_rdy = sem("gc_rdy")
        ge_rdy = sem("ge_rdy")
        h_rdy = sem("h_rdy")
        xs_rdy = sem("xs_rdy")
        xs_used = sem("xs_used")
        wk = {n: sem("wk_" + n) for n in
              ["ang", "cs",
               "sq", "rkp",
               "lc", "kkn",
               "exp",
               "ops", "clr",
               "mm", "cpv", "cpa",
               "g", "cv"]}
        pre = {n: sem("at_" + n) for n in
               ["tsm", "src",
                "src2", "osd",
                "osq",
                "sc", "s", "e",
                "p",
                "pt", "pte",
                "o", "ov",
                "ix", "ixr", "ixs"]}

        def kview(name, w):
            return d[name].rearrange("(k p) n -> p k n", p=P)

        def std(name, n0, n):
            v = kview(name, n)
            return [(0, 4, n, v[:, 0:4, n0:n0 + n]), (4 * n, 4, n, v[:, 4:8, n0:n0 + n])]

        A = []
        a_at = {}

        def add(name, loads):
            a_at.setdefault(name, len(A))
            A.append(loads)

        for w in ("w_r", "w_k", "w_v"):
            for c in range(2):
                add("rkv", std(w, c * 512, 512))
        add("lora", std("w_lora", 0, 2 * LORA + GLORA))
        for c in range(2):
            add("wo0", std("a_w_o", c * 512, 512))
        a_at["ffn0"] = len(A)
        A += [None] * 11
        add("kvd", std("kv_w_down", 0, KV_LORA + QK_ROPE))
        v = kview("kv_w_up", 2048)
        add("kvu", [(0, 1, 2048, v[:, 0:1, :]), (2048, 1, 2048, v[:, 1:2, :])])
        add("qd", std("q_w_down", 0, Q_LORA))
        v = kview("q_w_up", 1536)
        for c in range(2):
            add("qu", [(0, 2, 768, v[:, 0:2, c * 768:(c + 1) * 768]),
                       (2 * 768, 1, 768, v[:, 2:3, c * 768:(c + 1) * 768])])
        for c in range(2):
            add("wo1", std("o_w", c * 512, 512))
        a_at["ffn1"] = len(A)
        A += [None] * 11
        for c in range(6):
            add("din", std("diff_w_in", c * 512, 512))
        for c in range(2):
            add("wo2", std("diff_w_out", c * 512, 512))
        a_at["mlp0"] = len(A)
        A += [None] * 8
        DSA_IN = 256 + 2048 + 64 + 8
        for c in range(5):
            add("sin", std("dsa_w_in", c * 512, min(512, DSA_IN - c * 512)))
        v = kview("w_uqi", 1536)
        add("uq", [(0, 1, 1536, v[:, 0:1, :]), (1536, 1, 1536, v[:, 1:2, :])])
        for c in range(2):
            add("wo3", std("dsa_w_out", c * 512, 512))
        a_at["mlp1"] = len(A)
        A += [None] * 8

        G0 = {"ffn0": 0, "ffn1": 11, "mlp0": 22, "mlp1": 30}
        NCH = {"ffn0": 11, "ffn1": 11, "mlp0": 8, "mlp1": 8}

        def chunk_walk(eng, name, step):
            n = NCH[name]
            step(0, 0)
            step(1, 1)
            pairs = (n - 3) // 2
            with eng.Fori(0, pairs) as i:
                step(i * 2 + 2, 0)
                step(i * 2 + 3, 1)
            for c in range(2 + 2 * pairs, n):
                step(c, c % 2)

        JOBS = [("rkv", 12), ("lora", 2), ("wz", 4), ("az", 4), ("kk", 4), ("bonus", 1), ("gg", 0),
                ("bk", 4), ("kvd", 2), ("ckv", 1), ("kvu", 8), ("qd", 2), ("cq", 2), ("qu", 8),
                ("qk1", 16), ("din", 12), ("qk2", 8), ("sin", 10), ("scq", 1), ("uq", 6), ("qk3", 8),
                ("ixt", 3), ("ixs", 0)]
        J, NJ = offsets(JOBS)

        def bank(j):
            return 4 + j % 4

        TI = {n: i for i, n in enumerate(["n0", "o0", "nf0", "n1", "o1", "nf1", "n2", "o2", "nm0",
                                          "n3", "o3", "nm1"])}
        XN = {n: i for i, n in enumerate([n for n in TI if n not in ("o1", "o3")])}
        MI = {n: i for i, n in enumerate(["o0", "ffn0", "o1", "ffn1", "o2", "mlp0", "o3", "mlp1"])}
        SD = {n: i for i, n in enumerate(
            ["n0", "lnx", "nf0", "n1", "ckv", "cq", "nf1", "n2", "dqk", "dsub", "nm0", "n3",
             "scq", "kidx", "sqk", "nm1"])}

        INST = ["ffn0", "ffn1", "mlp0", "mlp1"]
        a_last = {}

        def jobs_use(name, per_slot):
            def put(a0, n, j0):
                for s in range(n):
                    a_last[a0 + s] = (job_rdy, j0 + per_slot * (s + 1))
            return put

        jobs_use("rkv", 2)(a_at["rkv"], 6, J["rkv"][0])
        jobs_use("lora", 2)(a_at["lora"], 1, J["lora"][0])
        jobs_use("kvd", 2)(a_at["kvd"], 1, J["kvd"][0])
        jobs_use("kvu", 8)(a_at["kvu"], 1, J["kvu"][0])
        jobs_use("qd", 2)(a_at["qd"], 1, J["qd"][0])
        jobs_use("qu", 4)(a_at["qu"], 2, J["qu"][0])
        jobs_use("din", 2)(a_at["din"], 6, J["din"][0])
        jobs_use("sin", 2)(a_at["sin"], 5, J["sin"][0])
        jobs_use("uq", 6)(a_at["uq"], 1, J["uq"][0])
        for n, w in enumerate(["wo0", "wo1", "wo2", "wo3"]):
            a_last[a_at[w]] = (a_used, n + 1)
            a_last[a_at[w] + 1] = (m_rdy, 2 * (MI["o%d" % n] + 1))
        for w in INST:
            for c in range(NCH[w]):
                a_last[a_at[w] + c] = (al_rdy, 2 * (G0[w] + c) + 2)

        def b_used_at(w, ch, half):
            return ch * 2 + (2 * G0[w] - INST.index(w) + half + 1)

        def a_half(w, slot, half):
            if w.startswith("ffn"):
                return ringA[:, slot, :].rearrange("p (k j n) -> p k j n", k=KT, j=2)[
                    :, :, :, half * P:(half + 1) * P]
            return ringA[:, slot, :].rearrange("p (k n) -> p k n", k=KT)[
                :, :, half * T:(half + 1) * T]

        def a_split(w, buf, half):
            if w.startswith("ffn"):
                return buf[:, half, :].rearrange("p (k j n) -> p k j n", k=KT, j=2)
            return buf[:, half, :].rearrange("p (k n) -> p k n", k=KT)

        def b_len(w):
            return D if w.startswith("ffn") else 2 * D

        c = Carve()
        lo2 = c(4096)
        w2_sb, a2_sb = lo2[0:LORA, 0:1024], lo2[0:LORA, 1024:2048]
        g2a_sb, g2b_sb = lo2[:, 2048:3072], lo2[0:GLORA - P, 3072:4096]
        xx = c(2048)
        rT, kT_, vtok, zs, aT = c(2048), c(2048), c(2048), c(2048), c(2048)
        AR = c(4096).rearrange("p (k c j t) -> p k c j t", k=KT, c=2, j=2)
        sigg = c(512)
        lT = ringB[:, 1, 2048:2560]
        lm = c(16)
        cl = c(8)
        bon = c(32)
        Sst = c(512).rearrange("p (k v) -> p k v", k=KT)
        gs_ = c(64)
        xs = [ringB[:, 0, 0:2048], ringB[:, 0, 2048:4096]]
        kkb, Lc = xs[0], xs[1]
        btk = ringB[:, 1, 0:2048].rearrange("p (j c) -> p j c", j=2)
        eN = ringB[:, 1, 2048:4096]
        hflat = hT[:, :, :].rearrange("p k t -> p (k t)")
        xnflat = xn[:, :, :].rearrange("p t n -> p (t n)")
        eQ, eP = xnflat, hflat
        k2 = xx
        bT = aT
        ytok = hflat
        lanes = []
        for pool in ([rT, kT_, zs], [kkb, Lc, eN]):
            bufs = [r[:, 512 * i:512 * i + 512] for r in pool for i in range(4)]
            n = len(lanes)
            names = ["NdT", "rb", "ak", "rk", "Nd", "No", "N2", "N2T", "N4", "N4T", "N8", "E"]
            lane = dict(zip(names, bufs))
            lane.update(M=lane["N2T"], MT=lane["N4T"], M2=lane["N2"], M2T=lane["N4"], M4T=lane["N8"])
            for i, r in enumerate(["R", "u0", "u1"]):
                lane[r] = lo2[:, n * 768 + i * 256:n * 768 + i * 256 + 256]
            lanes.append(lane)

        ht = xnflat[:, 0:512]
        gc = xnflat[:, 512:1024].rearrange("p (g n) -> p g n", g=2)
        ge = xnflat[:, 1024:1536].rearrange("p (g n) -> p g n", g=2)
        rl = xnflat[:, 512:1536].rearrange("p (g n) -> p g n", g=2)

        c = Carve()
        m_down = c(576).rearrange("p (t n) -> p t n", t=2)
        m_ckvn = c(512).rearrange("p (t n) -> p t n", t=2)
        m_ckvT = c(512).rearrange("p (k n) -> p k n", k=2)
        m_qd = c(768).rearrange("p (t n) -> p t n", t=2)
        m_cqn = c(768).rearrange("p (t n) -> p t n", t=2)
        m_cqT = c(768).rearrange("p (k n) -> p k n", k=3)
        m_k = c(3072).rearrange("p (t h n) -> p t h n", t=2, h=H)
        m_q = c(3072).rearrange("p (t h n) -> p t h n", t=2, h=H)
        m_rt = c(1024)
        m_KT = c(4096).rearrange("p (h t) -> p h t", h=H)
        m_QT = c(4096).rearrange("p (h t) -> p h t", h=H)
        hT2 = m_QT.rearrange("p h t -> p (h t)")[:, 0:2048].rearrange("p (k t) -> p k t", k=KT)
        m_v = rows[:, ROW["lnx_w"][0]:ROW["lnx_w"][0] + 2048].rearrange("p (t n) -> p t n", t=2)
        c2 = Carve()
        m_soft = c2(3456)

        c = Carve()
        d_p = c(6144).rearrange("p (j t n) -> p j t n", j=3, t=2)
        d_QT = c(2048).rearrange("p (k t) -> p k t", k=8)
        d_KT = c(2048).rearrange("p (k t) -> p k t", k=8)
        d_sq = c(4096)
        d_rt = c(1024)
        d_soft = c(3456)
        d_lam = c(8)

        c = Carve()
        s_p = c(2 * DSA_IN).rearrange("p (t n) -> p t n", t=2)
        s_q = c(2048).rearrange("p (t n) -> p t n", t=2)
        s_qi = c(1024).rearrange("p (t n) -> p t n", t=2)
        s_cqn = c(512).rearrange("p (t n) -> p t n", t=2)
        s_cqT = c(512).rearrange("p (k n) -> p k n", k=2)
        s_ki = c(256).rearrange("p (t j n) -> p t j n", t=2, j=2)
        s_QIT = c(1024).rearrange("p (k t) -> p k t", k=4)
        s_KIT = c(256)
        qk_at = c(4096)
        s_QT = qk_at[:, 0:2048].rearrange("p (k t) -> p k t", k=8)
        s_KT = qk_at[:, 2048:4096].rearrange("p (k t) -> p k t", k=8)
        s_sq = qk_at
        s_rt = c(512)
        s_ixr = c(768).rearrange("p (j n) -> p j n", j=2)
        s_acc = c(384)
        s_w = c(384)
        s_sel = c(384)
        s_soft = c(3456)

        def soft(r):
            return (r[:, 0:1152].rearrange("p (j n) -> p j n", j=3),
                    r[:, 1152:2688].rearrange("p (j n) -> p j n", j=4),
                    r[:, 2688:3456].rearrange("p (j n) -> p j n", j=2))

        def fm(ap):
            return ap.rearrange("p (k t) -> p k t", k=KT)

        def bc(ap, axis, n):
            shape = list(ap.shape)
            shape.insert(axis, n)
            return ap.unsqueeze(axis).to_broadcast(shape)

        STEPS = [("sb", "v"), ("sk", "v"), ("sn", "v"), ("N2", "a"), ("N2T", "a"), ("E2", "v"),
                 ("N4", "a"), ("N4T", "a"), ("E3", "v"), ("N8", "a"), ("E4", "v"), ("M", "a"),
                 ("MT", "v"), ("M2", "a"), ("M2T", "a"), ("M4T", "v"), ("rhs", "a"), ("y0", "a"),
                 ("y1", "v"), ("y2", "v"), ("U", "v"), ("Y", "a"), ("S", "v")]
        BANKS = {"sb": (0, 1), "sk": (2, 3), "sn": (0, 1), "N2": (2,), "N2T": (3,), "E2": (0,),
                 "N4": (1,), "N4T": (2,), "E3": (3,), "N8": (0,), "E4": (1,), "M": (2,), "MT": (3,),
                 "M2": (0,), "M2T": (1,), "M4T": (2,), "rhs": (3, 0), "y0": (1,), "y1": (2,),
                 "y2": (3,), "U": (0,), "Y": (1, 2), "S": (3,)}
        ORDER = [(u, name, e) for pair in range(4) for name, e in STEPS
                 for u in (2 * pair, 2 * pair + 1) if name != "S" or u < 4]
        PE_N = {(u, name): n + 1 for n, (u, name, _) in enumerate(ORDER)}
        EV_N = {}
        for e in "va":
            for n, (u, name, _) in enumerate([o for o in ORDER if o[2] == e]):
                EV_N[u, name] = (wk["cpv"] if e == "v" else wk["cpa"], n + 1)

        def heads_of(u):
            g = u % 4
            return u // 4, [(0, 2 * g, 0), (1, 2 * g + 1, 0), (2, 2 * g, 64), (3, 2 * g + 1, 64)]

        def lane_bank(u, name, i=0):
            return 4 * (u % 2) + BANKS[name][i]

        block = ctx.enter_context(nc.Block())

        @block.sync
        def _(sp):
            cons = [(cols[:, :], d["cols"]), (con[:, :], d["con"]),
                    (masks[:, :, :], d["masks"].rearrange("p (m t) -> p m t", m=len(MASKS))),
                    (rows[:, :], d["rows"].to_broadcast([P, NROW])),
                    (posi[:, :], d["positions"]),
                    (w2_sb, d["a_w2"]), (a2_sb, d["a_a2"]), (g2a_sb, d["a_g2"][0:P, :]),
                    (g2b_sb, d["a_g2"][P:GLORA, :])]
            sp.dma_start(x[:, :, :], d["x"].rearrange("(t p) n -> p t n", p=P)).then_inc(x_in, 16)
            for dst, src in cons:
                sp.dma_start(dst, src).then_inc(const_in, 16)

            def load_a(i):
                if i >= 2:
                    s, v = a_last[i - 2]
                    sp.wait_ge(s, v)
                for off, k, n, src in A[i]:
                    dst = ringA[:, i % 2, off:off + k * n].rearrange("p (k n) -> p k n", k=k)
                    sp.dma_start(dst, src).then_inc(a_loaded[i % 2], 16)

            def ffn_loads(w, gate_up):
                n = INST.index(w)

                def step(ch, par):
                    a0, g0 = a_at[w], G0[w]
                    ap, bp = (a0 + par) % 2, (g0 + par) % 2
                    if isinstance(ch, int):
                        s, v = a_last[a0 + ch - 2]
                        sp.wait_ge(s, v)
                    else:
                        sp.wait_ge(al_rdy, ch * 2 + (2 * g0 - 2))
                    dst = ringA[:, ap, :].rearrange("p (k j n) -> p k j n", k=KT, j=2)
                    if gate_up:
                        wi = d["ffn_w_in%d" % n].rearrange("(k p) m -> p k m", p=P)
                        for j in range(2):
                            sp.dma_start(dst[:, :, j, :], wi[:, :, bass.ds(ch * 256 + j * DFF, 256)]
                                         ).then_inc(a_loaded[ap], 16)
                    else:
                        wi = d["mlp_w1_%d" % (n - 2)].rearrange("(k p) m -> p k m", p=P)
                        dst = ringA[:, ap, :].rearrange("p (k n) -> p k n", k=KT)
                        for j in range(2):
                            sp.dma_start(dst[:, 4 * j:4 * j + 4, :],
                                         wi[:, 4 * j:4 * j + 4, bass.ds(ch * 512, 512)]
                                         ).then_inc(a_loaded[ap], 16)
                    if w == "ffn0" and isinstance(ch, int) and ch == 0:
                        sp.wait_ge(m_rdy, 2)
                    elif isinstance(ch, int) and ch < 2 and w == "ffn0":
                        pass
                    else:
                        sp.wait_ge(bl_rdy, ch * 2 + (2 * g0 - 2))
                    if gate_up:
                        wo, kk_ = d["ffn_w_out%d" % n], 1
                    else:
                        wo, kk_ = d["mlp_w2_%d" % (n - 2)], 2
                    dst = ringB[:, bp, 0:2048 * kk_].rearrange("p (j k n) -> p j k n", j=2, k=kk_)
                    for j in range(2):
                        src = wo[bass.ds((ch * 2 + j) * kk_ * P, kk_ * P), :].rearrange(
                            "(k p) m -> p k m", p=P)
                        sp.dma_start(dst[:, j], src).then_inc(b_loaded[bp], 16)

                chunk_walk(sp, w, step)

            for i in range(0, a_at["ffn0"]):
                load_a(i)
            ffn_loads("ffn0", True)
            for i in range(a_at["kvd"], a_at["ffn1"]):
                load_a(i)
            ffn_loads("ffn1", True)
            for i in range(a_at["din"], a_at["mlp0"]):
                load_a(i)
            ffn_loads("mlp0", False)
            for i in range(a_at["sin"], a_at["mlp1"]):
                load_a(i)
            ffn_loads("mlp1", False)
            for t in range(NT):
                sp.wait_ge(x_done, 14 + t + 1)
                sp.dma_start(out_d.rearrange("(t p) n -> p t n", p=P)[:, t, :], x[:, t, :]
                             ).then_inc(out_done, 16)
            sp.wait_ge(out_done, 32)

        @block.tensor
        def _(pe):
            mm = nc.tensor.matmul

            def wait_a(i):
                pe.wait_ge(a_loaded[i % 2], 32 * (i // 2 + 1))

            def turn16(name):
                if name in XN:
                    pe.wait_ge(xn_rdy, 2 * (XN[name] + 1))
                else:
                    pe.wait_ge(pre["ov"], {"o1": 16, "o3": 40}[name])
                for b in range(4):
                    for k in (2 * b, 2 * b + 1):
                        for t in range(NT):
                            last = nc.tensor.transpose(
                                ps[:, 4 + b, (k % 2) * T + t * P:(k % 2) * T + t * P + P],
                                xn[:, t, k * P:(k + 1) * P], ident)
                    last.then_inc(tp_rdy, 1)

            def wait_hT(name):
                pe.wait_ge(hv_rdy, 4 * (TI[name] + 1))
                pe.wait_ge(ha_rdy, 4 * (TI[name] + 1))

            def job_bank(j):
                if j >= 4:
                    pe.wait_ge(job_out, j - 3)
                return bank(j)

            def token_jobs(a, j0, src, kts, chunks):
                wait_a(a)
                w = sum(chunks)
                j, off = j0, 0
                for n in chunks:
                    for t in range(NT):
                        b = job_bank(j)
                        for k in range(kts):
                            last = mm(ps[:, b, 0:n], src[:, k, t * P:(t + 1) * P],
                                      ringA[:, a % 2, k * w + off:k * w + off + n],
                                      start=(k == 0), stop=(k == kts - 1))
                        last.then_inc(job_rdy, 1)
                        j += 1
                    off += n

            def out_proj(n):
                a = a_at["wo%d" % n]
                mi = MI["o%d" % n]
                wait_hT("o%d" % n)
                if mi:
                    pe.wait_ge(x_done, 2 * mi)
                for half in range(2):
                    wait_a(a + half)
                    for t in range(NT):
                        for k in range(KT):
                            last = mm(ps[:, 2 * t + half, :], hT[:, k, t * P:(t + 1) * P],
                                      ringA[:, (a + half) % 2, k * 512:(k + 1) * 512],
                                      start=(k == 0), stop=(k == KT - 1))
                        if half == 1:
                            last.then_inc(m_rdy, 1)
                        elif t == 1:
                            last.then_inc(a_used, 1)

            def ffn(w, nf):
                n = INST.index(w)
                g0 = G0[w]

                def first(ch, half, first_one=False):
                    if not isinstance(ch, int) or g0 + ch >= 1:
                        pe.wait_ge(h_rdy, ch * 2 + (2 * g0 + half - 1))
                    for j in range(2):
                        o = ps[:, 4 + half, j * T:(j + 1) * T]
                        if j == 0:
                            pe.wait_ge(ah_rdy, ch * 2 + (2 * g0 + half + 1))
                        for k in range(KT):
                            if first_one and j == 0 and k % 2 == 0:
                                pe.wait_ge(ha_rdy, 4 * TI[n_in] + k // 2 + 1)
                                if k == 0:
                                    pe.wait_ge(hv_rdy, 4 * TI[n_in] + 1)
                            mm(o, Ah[:, half, k * T + j * P:k * T + j * P + P], hTh[:, k, :],
                               start=(k == 0), stop=False)
                        for k in range(KT):
                            if first_one and j == 0 and k % 2 == 0:
                                pe.wait_ge(hv_rdy, 4 * TI[n_in] + k // 2 + 1)
                            mm(o, Ah[:, half, k * T + j * P:k * T + j * P + P], hTl[:, k, :],
                               start=False, stop=False)
                        if j == 0:
                            pe.wait_ge(al_rdy, ch * 2 + (2 * g0 + half + 1))
                        for k in range(KT):
                            last = mm(o, Al[:, half, k * T + j * P:k * T + j * P + P], hTh[:, k, :],
                                      start=False, stop=(k == KT - 1))
                    last.then_inc(f1_rdy, 1)

                def second(ch, half, first_one=False, last_one=False):
                    pe.wait_ge(bl_rdy, ch * 2 + (2 * g0 + half + 1))
                    pe.wait_ge(h_rdy, ch * 2 + (2 * g0 + half + 1))
                    if first_one and MI[w]:
                        pe.wait_ge(x_done, 2 * MI[w])
                    for t in range(NT):
                        for f in range(nf):
                            for i, (hb, wb) in enumerate(((hidh, Bh), (hidh, Bl), (hidl, Bh))):
                                for c_ in range(2):
                                    o = f * D + c_ * 512
                                    last = mm(ps[:, 2 * t + c_, :],
                                              hb[:, half, f * T + t * P:f * T + t * P + P],
                                              wb[:, half, o:o + 512],
                                              start=(first_one and f == 0 and i == 0),
                                              stop=(last_one and f == nf - 1 and i == 2))
                        if last_one:
                            last.then_inc(m_rdy, 1)
                    if not last_one:
                        last.then_inc(b_used, 1)

                n_in = {"ffn0": "nf0", "ffn1": "nf1", "mlp0": "nm0", "mlp1": "nm1"}[w]
                first(0, 0, first_one=True)
                first(0, 1)
                second(0, 0, first_one=True)

                def step(ch, par):
                    if isinstance(ch, int) and ch == 0:
                        return
                    first(ch, 0)
                    second(ch + -1, 1)
                    first(ch, 1)
                    second(ch, 0)

                chunk_walk(pe, w, step)
                second(NCH[w] - 1, 1, last_one=True)

            pe.wait_ge(const_in, 16 * 9)
            turn16("n0")
            j = J["rkv"][0]
            for i in range(3):
                pe.wait_ge(xs_rdy, i + 1)
                xi = fm(xs[i % 2])
                for s in range(2):
                    a = 2 * i + s
                    if i == 2:
                        token_jobs(a, j, xi, KT, [512])
                        j += 2
                        continue
                    wait_a(a)
                    for jj in range(2):
                        b = job_bank(j)
                        for q in range(2):
                            for k in range(KT):
                                o = k * 512 + (2 * jj + q) * P
                                last = mm(ps[:, b, q * T:(q + 1) * T], ringA[:, a % 2, o:o + P],
                                          xi[:, k, :], start=(k == 0), stop=(k == KT - 1))
                        last.then_inc(job_rdy, 1)
                        j += 1
            a = a_at["lora"]
            wait_a(a)
            wl = 2 * LORA + GLORA
            b = job_bank(j)
            for i in range(2):
                pe.wait_ge(xs_rdy, 4 + i)
                xi = fm(xs[(3 + i) % 2])
                for k in range(KT):
                    o = k * wl + i * LORA
                    last = mm(ps[0:LORA, b, i * T:(i + 1) * T], ringA[:, a % 2, o:o + LORA],
                              xi[:, k, :], start=(k == 0), stop=(k == KT - 1))
            last.then_inc(job_rdy, 1)
            j += 1
            b = job_bank(j)
            pe.wait_ge(xs_rdy, 6)
            xi = fm(xs[1])
            for q, (o0, n) in enumerate([(2 * LORA, P), (2 * LORA + P, GLORA - P)]):
                for k in range(KT):
                    o = k * wl + o0
                    last = mm(ps[0:n, b, q * T:(q + 1) * T], ringA[:, a % 2, o:o + n],
                              xi[:, k, :], start=(k == 0), stop=(k == KT - 1))
            last.then_inc(job_rdy, 1)
            j += 1
            pe.wait_ge(job_out, J["lora"][0] + 1)
            for i, wsb in enumerate((w2_sb, a2_sb)):
                for jj in range(4):
                    b = job_bank(j)
                    for q in range(2):
                        k = 2 * jj + q
                        last = mm(ps[:, b, q * T:(q + 1) * T], wsb[:, k * P:(k + 1) * P],
                                  lT[0:LORA, i * T:(i + 1) * T], start=True, stop=True)
                    last.then_inc(job_rdy, 1)
                    j += 1
            pe.wait_ge(wk["sq"], 1)
            for jj in range(4):
                b = job_bank(j)
                last = mm(ps[:, b, :], cst("blk1"), xnflat[:, jj * 512:(jj + 1) * 512],
                          start=True, stop=True)
                last.then_inc(job_rdy, 1)
                j += 1
            pe.wait_ge(wk["rkp"], 1)
            b = job_bank(j)
            for t in range(NT):
                for k in range(KT):
                    last = mm(ps[:, b, t * H + 2 * k:t * H + 2 * k + 2],
                              fm(hflat)[:, k, t * P:(t + 1) * P], cst("sel2"), start=True, stop=True)
            last.then_inc(job_rdy, 1)
            j += 1
            pe.wait_ge(wk["ops"], 1)
            for m, src in enumerate((bT, k2)):
                for jj in range(2):
                    b = job_bank(j)
                    for q in range(4):
                        k = 4 * jj + q
                        last = nc.tensor.transpose(ps[:, b, q * P:(q + 1) * P],
                                                   fm(src)[:, k, 0:P], ident)
                    last.then_inc(job_rdy, 1)
                    j += 1
            pe.wait_ge(job_out, j)
            pe.wait_ge(wk["clr"], 1)

            def need(u, *names):
                for n in names:
                    pe.wait_ge(*EV_N[u, n])

            BEFORE = {"sn": "sb", "N2": "sk", "N2T": "sk", "E2": "sn", "N4": "sn", "N4T": "N2",
                      "E3": "N2T", "N8": "E2", "E4": "N4", "M": "N4T", "MT": "E3", "M2": "N8",
                      "M2T": "E4", "M4T": "M", "rhs": "MT", "y0": "M2T", "y1": "M4T", "y2": "rhs",
                      "U": "rhs", "Y": "y0", "S": "y2"}
            PROD = {"N2": ("NdT", "Nd"), "N2T": ("Nd", "NdT"), "E2": ("N2", "E"),
                    "N4": ("N2T", "N2"), "N4T": ("N2", "N2T"), "E3": ("N4", "E"),
                    "N8": ("N4T", "N4"), "E4": ("N8", "E"), "M": ("E", "No"), "MT": ("No", "E"),
                    "M2": ("MT", "M"), "M2T": ("M", "MT"), "M4T": ("M2", "M2T"),
                    "y0": ("E", "R"), "y1": ("M4T", "u0"), "y2": ("M2T", "u1"), "U": ("MT", "u0")}
            FROM = {"N2": ("sb", "sn"), "N2T": (), "E2": ("N2",), "N4": ("N2T",), "N4T": (),
                    "E3": ("N4", "E2"), "N8": ("N4T",), "E4": ("N8", "E3"), "M": ("E4",), "MT": (),
                    "M2": ("MT", "M"), "M2T": (), "M4T": ("M2", "M2T"), "y0": ("rhs",),
                    "y1": ("y0", "M4T"), "y2": ("y1",), "U": ("y2",)}
            for u, name, _e in ORDER:
                ch, hs = heads_of(u)
                L = lanes[u % 2]
                if name in BEFORE:
                    need(u, BEFORE[name])
                elif name == "sb" and u >= 2:
                    need(u - 2, "U", "Y")
                elif name == "sk" and u >= 2:
                    need(u - 2, "Y", "S" if u - 2 < 4 else "y2")
                if name == "Y":
                    need(u, "y1", "U")
                if name in PROD:
                    need(u, *FROM[name])
                    lhs, rhs = PROD[name]
                    w = 64 if rhs in ("R", "u0", "u1") else P
                    b = lane_bank(u, name)
                    for q in range(4):
                        last = mm(ps[:, b, q * w:(q + 1) * w], L[lhs][:, q * P:(q + 1) * P],
                                  L[rhs][:, q * w:(q + 1) * w], start=True, stop=True)
                elif name in ("sb", "sk", "sn"):
                    for s, k, p0 in hs:
                        b = lane_bank(u, name, s // 2)
                        rowsl = slice(p0, p0 + 64)
                        toks = slice(ch * P, (ch + 1) * P)
                        if name == "sn":
                            last = mm(ps[:, b, (s % 2) * P:(s % 2) * P + P],
                                      AR[rowsl, k, ch, 0, :], fm(bT)[rowsl, k, toks],
                                      start=True, stop=True)
                        else:
                            src = bT if name == "sb" else k2
                            last = mm(ps[:, b, (s % 2) * T:(s % 2) * T + T], fm(src)[rowsl, k, toks],
                                      AR[rowsl, k, ch, :, :].rearrange("p j t -> p (j t)"),
                                      start=True, stop=True)
                elif name == "rhs":
                    need(u, "sk", "M2")
                    if ch:
                        need(u - 4, "S")
                    for s, k, p0 in hs:
                        b = lane_bank(u, name, s // 2)
                        o = ps[:, b, (s % 2) * 64:(s % 2) * 64 + 64]
                        hv = k * P + p0
                        last = mm(o, L["ak"][:, s * P:(s + 1) * P],
                                  vtok[:, ch * D + hv:ch * D + hv + 64], start=True, stop=(ch == 0))
                        if ch:
                            last = mm(o, AR[p0:p0 + 64, k, ch, 0, :], Sst[p0:p0 + 64, k, :],
                                      start=False, stop=True)
                elif name == "Y":
                    for s, k, p0 in hs:
                        b = lane_bank(u, name, s // 2)
                        o = ps[:, b, (s % 2) * 64:(s % 2) * 64 + 64]
                        hv = k * P + p0
                        mm(o, L["rk"][:, s * P:(s + 1) * P], vtok[:, ch * D + hv:ch * D + hv + 64],
                           start=True, stop=False)
                        last = mm(o, L["rb"][:, s * P:(s + 1) * P], L["u1"][:, s * 64:(s + 1) * 64],
                                  start=False, stop=(ch == 0))
                        if ch:
                            last = mm(o, AR[p0:p0 + 64, k, ch, 1, :], Sst[p0:p0 + 64, k, :],
                                      start=False, stop=True)
                else:
                    b = lane_bank(u, name)
                    uv = L["u1"].rearrange("p (j q v) -> p q j v", j=2, q=2)
                    for q in range(2):
                        k = hs[q][1]
                        o = ps[:, b, q * P:(q + 1) * P]
                        mm(o, btk[:, 1, k * P:(k + 1) * P], vtok[:, k * P:(k + 1) * P],
                           start=True, stop=False)
                        last = mm(o, btk[:, 0, k * P:(k + 1) * P], uv[:, q, :, :],
                                  start=False, stop=True)
                last.then_inc(wk["mm"], 1)
            need(6, "U", "Y", "y2")
            for t in range(NT):
                for half in range(2):
                    o = ps[:, 2 * t + half, :]
                    mm(o, sigg[:, t * P:(t + 1) * P], g2a_sb[:, half * 512:(half + 1) * 512],
                       start=True, stop=False)
                    last = mm(o, sigg[0:GLORA - P, T + t * P:T + (t + 1) * P],
                              g2b_sb[:, half * 512:(half + 1) * 512], start=False, stop=True)
            last.then_inc(wk["g"], 1)
            need(7, "U", "Y", "y2")
            turn16("o0")
            out_proj(0)

            turn16("nf0")
            ffn("ffn0", 1)

            def small_turn(j0, src, kts, n):
                pe.wait_ge(pre["tsm"], n)
                for jj in range((kts + 1) // 2):
                    b = job_bank(j0 + jj)
                    for k in range(2 * jj, min(2 * jj + 2, kts)):
                        for t in range(NT):
                            last = nc.tensor.transpose(
                                ps[:, b, (k % 2) * T + t * P:(k % 2) * T + t * P + P],
                                src[:, t, k * P:(k + 1) * P], ident)
                    last.then_inc(job_rdy, 1)

            def turn_blocks(j0, blocks):
                for jj in range((len(blocks) + 1) // 2):
                    b = job_bank(j0 + jj)
                    for i in range(2 * jj, min(2 * jj + 2, len(blocks))):
                        src, w = blocks[i]
                        for t in range(NT):
                            o = (i % 2) * T + t * P
                            last = nc.tensor.transpose(ps[0:w, b, o:o + P], src(t), ident)
                    last.then_inc(job_rdy, 1)

            def attend(layer, qt, kt, v, dv, softs):
                _, pr, pT = soft(softs)
                diff = layer == 1
                per = 2 if diff else 1
                u0, h0 = 16 * layer, [0, 16, 24][layer]

                def scores(u):
                    if u0 + u >= 3:
                        pe.wait_ge(pre["s"], u0 + u - 2)
                    b = 3 + (u0 + u) % 3
                    q, k = qt(u), kt(u)
                    mm(ps[:, b, 0:P], q[:, 0:P], k[:, 0:P], start=True, stop=True)
                    mm(ps[:, b, P:3 * P], q[:, P:T], k[:, :], start=True, stop=True
                       ).then_inc(pre["sc"], 1)

                def turn(h):
                    if diff:
                        pe.wait_ge(pre["p"], h + 1)
                    else:
                        pe.wait_ge(pre["e"], u0 + h + 1)
                    if h0 + h >= 2:
                        pe.wait_ge(pre["pte"], h0 + h - 1)
                    b = 6 + (h0 + h) % 2
                    for i in range(3):
                        last = nc.tensor.transpose(ps[:, b, i * P:(i + 1) * P],
                                                   pr[:, (per * h) % 4, i * P:(i + 1) * P], ident)
                    last.then_inc(pre["pt"], 1)

                def out(h):
                    pe.wait_ge(pre["pte"], h0 + h + 1)
                    if h0 + h >= 2:
                        pe.wait_ge(pre["ov"], h0 + h - 1)
                    b = (h0 + h) % 2
                    w = pT[:, (h0 + h) % 2, :]
                    mm(ps[:, b, 0:dv], w[:, 0:P], v(0, h), start=True, stop=True)
                    mm(ps[:, b, dv:2 * dv], w[:, P:2 * P], v(0, h), start=True, stop=False)
                    mm(ps[:, b, dv:2 * dv], w[:, 2 * P:3 * P], v(1, h), start=False, stop=True
                       ).then_inc(pre["o"], 1)

                heads = 16 // per
                for u in range(min(2 * per, 16)):
                    scores(u)
                for h in range(heads):
                    turn(h)
                    for u in range(per * (h + 2), min(per * (h + 3), 16)):
                        scores(u)
                    if h:
                        out(h - 1)
                out(heads - 1)

            turn16("n1")
            wait_hT("n1")
            token_jobs(a_at["kvd"], J["kvd"][0], hT2, KT, [KV_LORA + QK_ROPE])
            small_turn(J["ckv"][0], m_ckvn, 2, 1)
            pe.wait_ge(job_out, J["ckv"][0] + 1)
            token_jobs(a_at["kvu"], J["kvu"][0], m_ckvT, 2, [512] * 4)
            token_jobs(a_at["qd"], J["qd"][0], hT, KT, [Q_LORA])
            small_turn(J["cq"][0], m_cqn, 3, 2)
            pe.wait_ge(job_out, J["cq"][0] + 2)
            for s in range(2):
                token_jobs(a_at["qu"] + s, J["qu"][0] + 4 * s, m_cqT, 3, [384, 384])
            pe.wait_ge(job_out, J["qk1"][0])
            pe.wait_ge(pre["src"], 1)
            turn_blocks(J["qk1"][0], [((lambda t, s=s, h=h: s[:, t, h, :]), QD)
                                      for s in (m_q, m_k) for h in range(H)])
            pe.wait_ge(job_out, J["qk1"][0] + 16)
            attend(0, lambda u: m_QT[0:QD, u, :], lambda u: m_KT[0:QD, u, :],
                   lambda t, h: m_v[:, t, h * 64:(h + 1) * 64], 64, m_soft)
            turn16("o1")
            out_proj(1)
            turn16("nf1")
            ffn("ffn1", 1)

            turn16("n2")
            wait_hT("n2")
            for s in range(6):
                token_jobs(a_at["din"] + s, J["din"][0] + 2 * s, hT, KT, [512])
            pe.wait_ge(pre["src"], 2)
            turn_blocks(J["qk2"][0], [((lambda t, i=i, k=k: d_p[:, i, t, k * P:(k + 1) * P]), P)
                                      for i in range(2) for k in range(8)])
            pe.wait_ge(job_out, J["qk2"][0] + 8)

            def half(ap, u):
                return ap[64 * (u % 2):64 * (u % 2) + 64, u // 2, :]

            attend(1, lambda u: half(d_QT, u), lambda u: half(d_KT, u),
                   lambda t, h: d_p[:, 2, t, h * P:(h + 1) * P], P, d_soft)
            turn16("o2")
            out_proj(2)
            turn16("nm0")
            ffn("mlp0", 2)

            turn16("n3")
            wait_hT("n3")
            for s in range(5):
                token_jobs(a_at["sin"] + s, J["sin"][0] + 2 * s, hT, KT,
                           [min(512, DSA_IN - 512 * s)])
            small_turn(J["scq"][0], s_cqn, 2, 3)
            pe.wait_ge(job_out, J["scq"][0] + 1)
            token_jobs(a_at["uq"], J["uq"][0], s_cqT, 2, [512] * 3)
            pe.wait_ge(pre["src"], 3)
            turn_blocks(J["qk3"][0], [((lambda t, s=s, k=k: s[:, t, k * P:(k + 1) * P]), P)
                                      for s in (s_q, s_p[:, :, 256:1280]) for k in range(8)])
            turn_blocks(J["ixt"][0], [((lambda t, k=k: s_qi[:, t, k * P:(k + 1) * P]), P)
                                      for k in range(4)] +
                        [((lambda t: s_ki[:, t, :, :].rearrange("p j n -> p (j n)")), P)])
            pe.wait_ge(job_out, J["ixt"][0] + 3)
            for i in range(IDX_H):
                if i >= 3:
                    pe.wait_ge(pre["ixr"], i - 2)
                b = 3 + i % 3
                q = half(s_QIT, i)
                kx = s_KIT[64 * (i % 2):64 * (i % 2) + 64, :]
                mm(ps[:, b, 0:P], q[:, 0:P], kx[:, 0:P], start=True, stop=True)
                mm(ps[:, b, P:3 * P], q[:, P:T], kx, start=True, stop=True).then_inc(pre["ix"], 1)
            pe.wait_ge(pre["ixr"], 8)
            attend(2, lambda u: half(s_QT, u), lambda u: half(s_KT, u),
                   lambda t, h: s_p[:, t, 1280 + h * 64:1280 + (h + 1) * 64], 64, s_soft)
            turn16("o3")
            out_proj(3)
            turn16("nm1")
            ffn("mlp1", 2)

        @block.scalar
        def _(act):
            chain = [0]
            A_ = nc.scalar.activation

            def link(ins):
                chain[0] += 1
                ins.then_inc(act_c, 1)
                act.wait_ge(act_c, chain[0])

            eps = con[:, CON["eps"][0]:CON["eps"][0] + 1]
            eps_l = con[:, CON["eps"][0] + 1:CON["eps"][0] + 2]

            def root(name, out, in_, n, e):
                act.wait_ge(ss_rdy, SD[name] + 1)
                if e is None:
                    ins = A_(out, in_, ACT.Sqrt, scale=1.0 / n)
                else:
                    ins = A_(out, in_, ACT.Sqrt, bias=e, scale=1.0 / n)
                ins.then_inc(sd_rdy, 1)

            def norm(name):
                root(name, st[:, 2:4], st[:, 0:2], D, eps)

            def turned(name, gain, gain2=None):
                n = TI[name]
                for k in range(4, 8):
                    act.wait_ge(tp_rdy, 4 * n + k // 2 + 1)
                    src = ps[:, 4 + k // 2, (k % 2) * T:(k % 2) * T + T]
                    if gain2:
                        A_(hT2[:, k, :], src, ACT.Copy, scale=col(gain2, k))
                    if gain:
                        A_(hT[:, k, :], src, ACT.Copy, scale=col(gain, k)).then_inc(ha_rdy, 1)
                    else:
                        nc.scalar.copy(hT[:, k, :], src).then_inc(ha_rdy, 1)

            def res_root(mi):
                for t in range(NT):
                    act.wait_ge(m_rdy, 2 * mi + t + 1)
                    link(A_(xn[:, t, :], ps[:, 2 * t:2 * t + 2, :].rearrange("p b n -> p (b n)"),
                            ACT.Square, accum_out=st[:, 8 + t:9 + t]))
                    A_(st[:, 10 + t:11 + t], st[:, 8 + t:9 + t], ACT.Sqrt, bias=eps, scale=1.0 / D
                       ).then_inc(msd_rdy, 1)

            def job(j, *copies):
                act.wait_ge(job_rdy, j + 1)
                for f in copies:
                    last = f(ps[:, bank(j), :])
                last.then_inc(job_out, 1)

            def turned_split(name, gain):
                n = TI[name]
                for b in range(4):
                    act.wait_ge(tp_rdy, 4 * n + b + 1)
                    for k in (2 * b, 2 * b + 1):
                        last = A_(hTh[:, k, :], ps[:, 4 + b, (k % 2) * T:(k % 2) * T + T], ACT.Copy,
                                  scale=col(gain, k))
                    last.then_inc(ha_rdy, 1)

            def round_a(w, ch, par, half):
                a0, g0 = a_at[w], G0[w]
                ap = (a0 + par) % 2
                act.wait_ge(a_loaded[ap], ch * 16 + (32 * ((a0 + par) // 2 + 1) - 16 * par))
                if not isinstance(ch, int) or ch >= 1:
                    act.wait_ge(f1_rdy, ch * 2 + (2 * g0 + half - 1))
                nc.scalar.copy(a_split(w, Ah, half), a_half(w, ap, half)).then_inc(ah_rdy, 1)

            def round_b(w, ch, par, half):
                g0 = G0[w]
                bp, n = (g0 + par) % 2, b_len(w)
                act.wait_ge(b_loaded[bp], ch * 16 + (32 * ((g0 + par) // 2 + 1) - 16 * par))
                if not isinstance(ch, int) or ch >= 1:
                    act.wait_ge(b_used, b_used_at(w, ch + -1, half))
                nc.scalar.copy(Bh[:, half, 0:n], ringB[:, bp, half * n:(half + 1) * n]
                               ).then_inc(bh_rdy, 1)

            def ffn_start(w):
                act.wait_ge(m_rdy, 2 * MI[w])
                for half in range(2):
                    round_a(w, 0, 0, half)

            def ffn(w, gelu):
                g0 = G0[w]
                round_b(w, 0, 0, 0)

                def step(ch, par):
                    last = isinstance(ch, int) and ch == NCH[w] - 1
                    for half in range(2):
                        n = ch * 2 + (2 * g0 + half + 1)
                        if not last:
                            round_a(w, ch + 1, 1 - par, half)
                        if gelu:
                            act.wait_ge(gc_rdy, n)
                            A_(ge[:, half, :], gc[:, half, :], ACT.Gelu_apprx_tanh
                               ).then_inc(ge_rdy, 1)
                        else:
                            act.wait_ge(f1_rdy, n)
                            act.wait_ge(h_rdy, n + -2)
                            A_(rl[:, half, :], ps[:, 4 + half, :], ACT.Relu).then_inc(ge_rdy, 1)
                        if half == 0:
                            round_b(w, ch, par, 1)
                        elif not last:
                            round_b(w, ch + 1, 1 - par, 0)

                chunk_walk(act, w, step)

            act.wait_ge(const_in, 16 * 9)
            act.wait_ge(wk["ang"], 1)
            A_(cs2[:, :, :, :], cs2[:, :, :, :], ACT.Sin).then_inc(wk["cs"], 1)
            norm("n0")
            turned("n0", "g0_mix")
            j = J["rkv"][0]
            for dst in (fm(rT), fm(kT_)):
                for s in range(4):
                    o = dst[:, 2 * s:2 * s + 2, :].rearrange("p k t -> p (k t)")
                    job(j, lambda p, o=o: nc.scalar.copy(o, p))
                    j += 1
            for half in range(2):
                for t in range(NT):
                    o = vtok[:, t * D + half * 512:t * D + half * 512 + 512]
                    job(j, lambda p, o=o: nc.scalar.copy(o, p))
                    j += 1
            job(j, lambda p: A_(lT[0:LORA, 0:T], p[0:LORA, 0:T], ACT.Tanh),
                lambda p: nc.scalar.copy(lT[0:LORA, T:2 * T], p[0:LORA, T:2 * T]))
            job(j + 1, lambda p: A_(sigg[:, 0:T], p[:, 0:T], ACT.Sigmoid),
                lambda p: A_(sigg[0:GLORA - P, T:2 * T], p[0:GLORA - P, T:2 * T], ACT.Sigmoid))
            j += 2
            for dst, bias in ((zs, "w0"), (aT, "a0")):
                for s in range(4):
                    job(j, *[lambda p, q=q: A_(fm(dst)[:, 2 * s + q, :], p[:, q * T:(q + 1) * T],
                                               ACT.Sigmoid, bias=col(bias, 2 * s + q))
                             for q in range(2)])
                    j += 1
            for s in range(4):
                job(j, lambda p: A_(xnflat[:, s * 512:(s + 1) * 512], p, ACT.Sqrt))
                j += 1
            job(j, lambda p: nc.scalar.copy(bon, p[:, 0:32]))
            j += 1
            act.wait_ge(wk["lc"], 1)
            act.wait_ge(wk["kkn"], 1)
            A_(eQ, zs, ACT.Exp).then_inc(wk["exp"], 1)
            A_(eN, Lc, ACT.Exp, scale=-1.0).then_inc(wk["exp"], 1)
            A_(eP, Lc, ACT.Exp).then_inc(wk["exp"], 1)
            A_(cl, cl, ACT.Exp).then_inc(wk["exp"], 1)
            for m in range(2):
                for s in range(2):
                    o = btk[:, m, s * 512:(s + 1) * 512]
                    job(j, lambda p, o=o: nc.scalar.copy(o, p))
                    j += 1
            for u, name, e in ORDER:
                if e != "a":
                    continue
                ch, hs = heads_of(u)
                L = lanes[u % 2]
                act.wait_ge(wk["mm"], PE_N[u, name])
                if name == "rhs":
                    for i in range(2):
                        last = nc.scalar.copy(L["R"][:, i * P:(i + 1) * P],
                                              ps[:, lane_bank(u, name, i), 0:P])
                elif name == "y0":
                    last = nc.scalar.copy(L["u0"], ps[:, lane_bank(u, name), 0:T])
                elif name == "Y":
                    for i in range(2):
                        yv = ytok.rearrange("p (c k i v) -> p c k i v", c=2, k=KT, i=2)
                        k = hs[0][1]
                        last = nc.scalar.copy(yv[:, ch, k:k + 2, i, :],
                                              ps[:, lane_bank(u, name, i), 0:P].rearrange(
                                                  "p (k v) -> p k v", k=2))
                else:
                    last = nc.scalar.copy(L[name], ps[:, lane_bank(u, name), :])
                last.then_inc(wk["cpa"], 1)
            root("lnx", gs_[:, 32:64], gs_[:, 0:32], HD, eps_l)
            turned("o0", None)
            res_root(0)
            ffn_start("ffn0")
            norm("nf0")
            turned_split("nf0", "g0_ffn")
            ffn("ffn0", True)
            res_root(1)

            def attend(layer, softs):
                s_, pr, pT = soft(softs)
                diff = layer == 1
                per = 2 if diff else 1
                u0, h0 = 16 * layer, [0, 16, 24][layer]

                def turned_p(h):
                    act.wait_ge(pre["pt"], h0 + h + 1)
                    nc.scalar.copy(pT[:, (h0 + h) % 2, :], ps[:, 6 + (h0 + h) % 2, 0:384]
                                   ).then_inc(pre["pte"], 1)

                for u in range(16):
                    act.wait_ge(pre["s"], u0 + u + 1)
                    nm = st[:, 64 + 2 * u:66 + 2 * u]
                    sm = st[:, 96 + 2 * u:98 + 2 * u]
                    i = u % 4
                    A_(pr[:, i, 0:P], s_[:, (u0 + u) % 3, 0:P], ACT.Exp, bias=nm[:, 0:1],
                       accum_out=sm[:, 0:1])
                    A_(pr[:, i, P:384], s_[:, (u0 + u) % 3, P:384], ACT.Exp, bias=nm[:, 1:2],
                       accum_out=sm[:, 1:2]).then_inc(pre["e"], 1)
                    if diff and u % 2 and u >= 3:
                        turned_p(u // 2 - 1)
                    if not diff and u:
                        turned_p(u - 1)
                turned_p(16 // per - 1)

            norm("n1")
            turned("n1", "g1_mix", "g_kv")
            j = J["kvd"][0]
            for t in range(NT):
                job(j + t, lambda p: nc.scalar.copy(m_down[:, t, :], p[:, 0:288]))
            root("ckv", st[:, 18:20], st[:, 16:18], KV_LORA, eps)
            j = J["ckv"][0]
            job(j, *[lambda p, k=k: A_(m_ckvT[:, k, :], p[:, k * T:(k + 1) * T], ACT.Copy,
                                       scale=col("kv_a", k)) for k in range(2)])
            j = J["kvu"][0]
            for q in range(4):
                for t in range(NT):
                    def kpart(p):
                        return nc.scalar.copy(m_k[:, t, 4 * q:4 * q + 4, 0:64],
                                              p.rearrange("p (h n) -> p h n", h=4)[:, :, 0:64])

                    def vpart(p):
                        return nc.scalar.copy(
                            m_v[:, t, q * 256:(q + 1) * 256].rearrange("p (h n) -> p h n", h=4),
                            p.rearrange("p (h n) -> p h n", h=4)[:, :, 64:128])
                    job(j, kpart, vpart)
                    j += 1
            for t in range(NT):
                job(J["qd"][0] + t, lambda p: nc.scalar.copy(m_qd[:, t, :], p[:, 0:Q_LORA]))
            root("cq", st[:, 22:24], st[:, 20:22], Q_LORA, eps)
            j = J["cq"][0]
            job(j, *[lambda p, k=k: A_(m_cqT[:, k, :], p[:, k * T:(k + 1) * T], ACT.Copy,
                                       scale=col("q_n", k)) for k in range(2)])
            job(j + 1, lambda p: A_(m_cqT[:, 2, :], p[:, 0:T], ACT.Copy, scale=col("q_n", 2)))
            j = J["qu"][0]
            for q in range(4):
                for t in range(NT):
                    job(j, lambda p: nc.scalar.copy(m_q[:, t, 4 * q:4 * q + 4, :],
                                                    p[:, 0:384].rearrange("p (h n) -> p h n", h=4)))
                    j += 1
            j = J["qk1"][0]
            for dst in (m_QT, m_KT):
                for s in range(8):
                    job(j, lambda p: nc.scalar.copy(
                        dst[0:QD, 2 * s:2 * s + 2, :].rearrange("p h t -> p (h t)"), p[0:QD, :]))
                    j += 1
            attend(0, m_soft)
            turned("o1", None)
            res_root(2)
            ffn_start("ffn1")
            norm("nf1")
            turned_split("nf1", "g1_ffn")
            ffn("ffn1", True)
            res_root(3)

            norm("n2")
            turned("n2", "n0_mix")
            j = J["din"][0]
            for i in range(3):
                for half in range(2):
                    for t in range(NT):
                        job(j, lambda p: nc.scalar.copy(d_p[:, i, t, half * 512:half * 512 + 512], p))
                        j += 1
            act.wait_ge(pre["src2"], 1)
            A_(d_lam[:, 2:4], d_lam[:, 0:2], ACT.Exp).then_inc(pre["osd"], 1)
            root("dqk", st[:, 192:256], st[:, 128:192], HD, eps)
            j = J["qk2"][0]
            for dst in (d_QT, d_KT):
                for s in range(4):
                    job(j, lambda p: nc.scalar.copy(
                        dst[:, 2 * s:2 * s + 2, :].rearrange("p h t -> p (h t)"), p))
                    j += 1
            attend(1, d_soft)
            root("dsub", st[:, 40:56], st[:, 24:40], 2 * HD, eps)
            turned("o2", None)
            ffn_start("mlp0")
            norm("nm0")
            turned_split("nm0", "n0_mlp")
            ffn("mlp0", False)

            norm("n3")
            turned("n3", "n1_mix")
            j = J["sin"][0]
            for s in range(5):
                w = min(512, DSA_IN - 512 * s)
                for t in range(NT):
                    job(j, lambda p: nc.scalar.copy(s_p[:, t, s * 512:s * 512 + w], p[:, 0:w]))
                    j += 1
            root("scq", st[:, 18:20], st[:, 16:18], DSA_Q, eps)
            job(J["scq"][0], *[lambda p, k=k: A_(s_cqT[:, k, :], p[:, k * T:(k + 1) * T], ACT.Copy,
                                                 scale=col("cq_n", k)) for k in range(2)])
            root("kidx", st[:, 22:24], st[:, 20:22], 64, eps)
            j = J["uq"][0]
            for q in range(3):
                for t in range(NT):
                    dst = s_q[:, t, q * 512:(q + 1) * 512] if q < 2 else s_qi[:, t, :]
                    job(j, lambda p: nc.scalar.copy(dst, p))
                    j += 1
            root("sqk", st[:, 192:256], st[:, 128:192], HD, eps)
            j = J["qk3"][0]
            for dst in (s_QT, s_KT):
                for s in range(4):
                    job(j, lambda p: nc.scalar.copy(
                        dst[:, 2 * s:2 * s + 2, :].rearrange("p h t -> p (h t)"), p))
                    j += 1
            for s in range(2):
                job(j, lambda p: nc.scalar.copy(
                    s_QIT[:, 2 * s:2 * s + 2, :].rearrange("p h t -> p (h t)"), p))
                j += 1
            job(j, lambda p: nc.scalar.copy(s_KIT, p[:, 0:T]))
            for i in range(IDX_H):
                act.wait_ge(pre["ix"], i + 1)
                if i >= 2:
                    act.wait_ge(pre["ixs"], i - 1)
                A_(s_ixr[:, i % 2, :], ps[:, 3 + i % 3, 0:384], ACT.Relu).then_inc(pre["ixr"], 1)
            attend(2, s_soft)
            turned("o3", None)
            ffn_start("mlp1")
            norm("nm1")
            turned_split("nm1", "n1_mlp")
            ffn("mlp1", False)

        @block.vector
        def _(dve):
            chain = [0]
            V = nc.vector

            def link(ins):
                chain[0] += 1
                ins.then_inc(dve_c, 1)
                dve.wait_ge(dve_c, chain[0])

            def norm(name, inst):
                for t in range(NT):
                    ins = V.tensor_tensor_reduce(xn[:, t, :], x[:, t, :], x[:, t, :], 1.0, 0.0,
                                                 ALU.mult, ALU.add, st[:, t:t + 1])
                ins.then_inc(ss_rdy, 1)
                dve.wait_ge(sd_rdy, SD[name] + 1)
                link(V.reciprocal(st[:, 4:6], st[:, 2:4]))
                for t in range(NT):
                    V.tensor_scalar(xn[:, t, :], x[:, t, :], st[:, 4 + t:5 + t], None, ALU.mult
                                    ).then_inc(xn_rdy, 1)

            def turned(name, gain, gain2=None):
                n = TI[name]
                for k in range(4):
                    dve.wait_ge(tp_rdy, 4 * n + k // 2 + 1)
                    src = ps[:, 4 + k // 2, (k % 2) * T:(k % 2) * T + T]
                    if gain2:
                        V.tensor_scalar(hT2[:, k, :], src, col(gain2, k), None, ALU.mult)
                    if gain:
                        ins = V.tensor_scalar(hT[:, k, :], src, col(gain, k), None, ALU.mult)
                    else:
                        ins = V.tensor_copy(hT[:, k, :], src)
                    ins.then_inc(hv_rdy, 1)

            def mview(t):
                return ps[:, 2 * t:2 * t + 2, :].rearrange("p b n -> p (b n)")

            def res_norm(mi, gain):
                for t in range(NT):
                    dve.wait_ge(msd_rdy, 2 * mi + t + 1)
                    link(V.reciprocal(st[:, 12 + t:13 + t], st[:, 10 + t:11 + t]))
                    link(V.scalar_tensor_tensor(xn[:, t, :], mview(t), st[:, 12 + t:13 + t], row(gain),
                                                ALU.mult, ALU.mult))
                    V.tensor_tensor(x[:, t, :], x[:, t, :], xn[:, t, :], ALU.add).then_inc(x_done, 1)
                dve.wait_ge(x_done, 2 * mi + 2)

            def res_plain(mi):
                for t in range(NT):
                    dve.wait_ge(m_rdy, 2 * mi + t + 1)
                    V.tensor_tensor(x[:, t, :], x[:, t, :], mview(t), ALU.add).then_inc(x_done, 1)
                dve.wait_ge(x_done, 2 * mi + 2)

            def turned_split(name, gain):
                n = TI[name]
                for b in range(4):
                    dve.wait_ge(ha_rdy, 4 * n + b + 1)
                    for k in (2 * b, 2 * b + 1):
                        last = V.scalar_tensor_tensor(
                            hTl[:, k, :], ps[:, 4 + b, (k % 2) * T:(k % 2) * T + T], col(gain, k),
                            hTh[:, k, :].bitcast(F32), ALU.mult, ALU.subtract)
                    last.then_inc(hv_rdy, 1)

            def rest_a(w, ch, par, half):
                dve.wait_ge(ah_rdy, ch * 2 + (2 * G0[w] + half + 1))
                V.tensor_tensor(a_split(w, Al, half), a_half(w, (a_at[w] + par) % 2, half),
                                a_split(w, Ah, half).bitcast(F32), ALU.subtract).then_inc(al_rdy, 1)

            def rest_b(w, ch, par, half):
                n = b_len(w)
                dve.wait_ge(bh_rdy, ch * 2 + (2 * G0[w] + half + 1))
                V.tensor_tensor(Bl[:, half, 0:n], ringB[:, (G0[w] + par) % 2, half * n:(half + 1) * n],
                                Bh[:, half, 0:n].bitcast(F32), ALU.subtract).then_inc(bl_rdy, 1)

            def ffn_start(w):
                for half in range(2):
                    rest_a(w, 0, 0, half)

            def ffn(w, layer=None):
                g0 = G0[w]
                F = DFF // P
                rest_b(w, 0, 0, 0)

                def conv(ch, half):
                    cw, cb = "conv_w%d" % layer, "conv_b%d" % layer
                    f = ch * 2 + half
                    gate, o = ps[:, 4 + half, 0:T], gc[:, half, :]
                    n = ch * 4 + (4 * g0 + 2 * half + 1)
                    dve.wait_ge(f1_rdy, ch * 2 + (2 * g0 + half + 1))
                    V.tensor_scalar(o, gate, colx(cw, f + 2 * F), colx(cb, f), ALU.mult, ALU.add
                                    ).then_inc(wk["cv"], 1)
                    dve.wait_ge(wk["cv"], n)
                    V.scalar_tensor_tensor(o[:, 1:T], gate[:, 0:T - 1], colx(cw, f + F), o[:, 1:T],
                                           ALU.mult, ALU.add).then_inc(wk["cv"], 1)
                    dve.wait_ge(wk["cv"], n + 1)
                    V.scalar_tensor_tensor(o[:, 2:T], gate[:, 0:T - 2], colx(cw, f), o[:, 2:T],
                                           ALU.mult, ALU.add).then_inc(gc_rdy, 1)

                def step(ch, par):
                    last = isinstance(ch, int) and ch == NCH[w] - 1
                    for half in range(2):
                        if layer is not None:
                            conv(ch, half)
                        if not last:
                            rest_a(w, ch + 1, 1 - par, half)
                        n = ch * 2 + (2 * g0 + half + 1)
                        m = ch * 4 + (4 * g0 + 2 * half + 1)
                        dve.wait_ge(ge_rdy, n)
                        if not isinstance(ch, int) or n >= 2:
                            dve.wait_ge(h_rdy, n + -1)
                        if layer is None:
                            wid = 2 * T
                            V.tensor_tensor(ht, rl[:, half, :], rl[:, half, :], ALU.mult
                                            ).then_inc(ht_rdy, 1)
                        else:
                            wid = T
                            V.tensor_tensor(ht[:, 0:T], ge[:, half, :], ps[:, 4 + half, T:2 * T],
                                            ALU.mult).then_inc(ht_rdy, 1)
                        if not isinstance(ch, int) or ch >= 1:
                            dve.wait_ge(b_used, b_used_at(w, ch + -1, half))
                        dve.wait_ge(ht_rdy, m)
                        V.tensor_copy(hidh[:, half, 0:wid], ht[:, 0:wid]).then_inc(ht_rdy, 1)
                        dve.wait_ge(ht_rdy, m + 1)
                        V.tensor_tensor(hidl[:, half, 0:wid], ht[:, 0:wid],
                                        hidh[:, half, 0:wid].bitcast(F32), ALU.subtract
                                        ).then_inc(h_rdy, 1)
                        if half == 0:
                            rest_b(w, ch, par, 1)
                        elif not last:
                            rest_b(w, ch + 1, 1 - par, 0)

                chunk_walk(dve, w, step)

            dve.wait_ge(const_in, 16 * 9)
            inv = con[:, CON["inv2"][0]:CON["inv2"][0] + 8]
            posf, ang = gs_[:, 0:2], st[:, 128:144].rearrange("p (t n) -> p t n", t=2)
            cnt = st[:, 144:176].rearrange("p (j t n) -> p j t n", j=2, t=2)
            link(V.tensor_copy(posf, posi[:, :]))
            for t in range(NT):
                ins = V.tensor_scalar(ang[:, t, :], inv, posf[:, t:t + 1], None, ALU.mult)
            link(ins)
            V.tensor_scalar(cnt[:, 0], ang, 1.0 / (2 * math.pi), 0.25, ALU.mult, ALU.add)
            link(V.tensor_scalar(cnt[:, 1], ang, 1.0 / (2 * math.pi), None, ALU.mult))
            link(V.tensor_scalar(cnt, cnt, MAGIC, None, ALU.add))
            link(V.tensor_scalar(cnt, cnt, -MAGIC, None, ALU.add))
            for j in range(2):
                ins = V.scalar_tensor_tensor(cs2[:, j], cnt[:, j], -TWO_PI[0], ang, ALU.mult, ALU.add)
            link(ins)
            link(V.scalar_tensor_tensor(cs2[:, :, :, :].rearrange("p j t n -> p (j t n)"),
                                        st[:, 144:176], -TWO_PI[1],
                                        cs2[:, :, :, :].rearrange("p j t n -> p (j t n)"),
                                        ALU.mult, ALU.add))
            link(V.scalar_tensor_tensor(cs2[:, :, :, :].rearrange("p j t n -> p (j t n)"),
                                        st[:, 144:176], -TWO_PI[2],
                                        cs2[:, :, :, :].rearrange("p j t n -> p (j t n)"),
                                        ALU.mult, ALU.add))
            link(V.tensor_scalar(cs2[:, 0], cs2[:, 0], math.pi / 2, None, ALU.add))
            V.tensor_scalar(cs2[:, :, :, :], cs2[:, :, :, :], 3.1415925, -3.1415925, ALU.min, ALU.max
                            ).then_inc(wk["ang"], 1)

            dve.wait_ge(x_in, 16)
            norm("n0", 0)
            turned("n0", "g0_mix")
            dve.wait_ge(hv_rdy, 4)
            dve.wait_ge(ha_rdy, 4)
            xf = fm(xx)
            V.tensor_scalar(xf[:, :, 0:1], hT[:, :, 0:1], -1.0, None, ALU.mult)
            link(V.tensor_tensor(xf[:, :, 1:T], hT[:, :, 0:T - 1], hT[:, :, 1:T], ALU.subtract))
            for i in range(6):
                if i >= 2:
                    dve.wait_ge(job_rdy, [4, 8, 12, 13][i - 2])
                for k in range(KT):
                    last = V.scalar_tensor_tensor(fm(xs[i % 2])[:, k, :], xf[:, k, :],
                                                  col("mu", 8 * i + k), hT[:, k, :],
                                                  ALU.mult, ALU.add)
                last.then_inc(xs_rdy, 1)
            dve.wait_ge(job_rdy, J["lora"][0] + 2)
            for k in range(KT):
                ins = V.tensor_scalar(fm(kkb)[:, k, :], fm(kT_)[:, k, :], col("k_k", k), None, ALU.mult)
            link(ins)
            V.tensor_tensor(xnflat, kkb, kkb, ALU.mult).then_inc(wk["sq"], 1)
            dve.wait_ge(job_out, J["az"][0] + 4)
            for k in range(KT):
                ins = V.tensor_scalar(fm(k2)[:, k, :], fm(aT)[:, k, :], 1.0, col("k_a", k),
                                      ALU.subtract, ALU.mult)
            link(ins)
            link(V.scalar_tensor_tensor(k2, k2, 1.0, kT_, ALU.add, ALU.mult))
            for k in range(KT):
                last = V.scalar_tensor_tensor(hT[:, k, :], fm(rT)[:, k, :], col("r_k", k),
                                              fm(k2)[:, k, :], ALU.mult, ALU.mult)
            last.then_inc(wk["rkp"], 1)
            link(V.tensor_scalar(zs, zs, -E05, None, ALU.mult))
            ones = cst("ones")
            for s in range(2 * KT):
                ins = V.tensor_tensor_scan(Lc[:, s * P:(s + 1) * P], ones, zs[:, s * P:(s + 1) * P],
                                           0.0, ALU.mult, ALU.add)
            link(ins)
            L3 = Lc.rearrange("p (s t) -> p s t", t=P)
            link(V.tensor_copy(lm, L3[:, :, P // 2 - 1]))
            link(V.tensor_tensor(L3, L3, bc(lm, 2, P), ALU.subtract))
            V.tensor_tensor(zs, Lc, zs, ALU.subtract)
            lms = lm.rearrange("p (k c) -> p k c", c=2)
            L4 = Lc.rearrange("p (k c t) -> p k c t", c=2, t=P)
            V.tensor_tensor(cl, L4[:, :, 0, P - 1], lms[:, :, 1], ALU.add).then_inc(wk["lc"], 1)
            dve.wait_ge(job_out, J["kk"][0] + 4)
            link(V.tensor_scalar(xnflat, xnflat, 1e-12, None, ALU.max))
            link(V.reciprocal(xnflat, xnflat))
            V.tensor_tensor(kkb, kkb, xnflat, ALU.mult).then_inc(wk["kkn"], 1)
            dve.wait_ge(wk["kkn"], 1)
            dve.wait_ge(wk["exp"], 1)
            a5 = AR[:, :, :, 0, :]
            r5 = AR[:, :, :, 1, :]

            def v4(ap):
                return ap.rearrange("p (k c t) -> p k c t", c=2, t=P)

            for c_ in range(2):
                V.scalar_tensor_tensor(a5[:, :, c_, :], v4(kkb)[:, :, c_, :], -1.0, v4(eQ)[:, :, c_, :],
                                       ALU.mult, ALU.mult)
            link(V.tensor_tensor(aT, aT, kkb, ALU.mult))
            dve.wait_ge(wk["exp"], 2)
            V.tensor_tensor(aT, aT, eN, ALU.mult)
            V.tensor_tensor(k2, k2, eN, ALU.mult)
            dve.wait_ge(wk["exp"], 4)
            for c_ in range(2):
                last = V.tensor_tensor(r5[:, :, c_, :], v4(rT)[:, :, c_, :], v4(eP)[:, :, c_, :],
                                       ALU.mult)
            last.then_inc(wk["ops"], 1)
            dve.wait_ge(wk["ops"], 1)
            for L in lanes:
                for n_ in ("NdT", "rb", "ak", "rk", "Nd", "No"):
                    last = V.memset(L[n_], 0.0)
            last.then_inc(wk["clr"], 1)
            dve.wait_ge(wk["clr"], 1)

            def h4(ap, i):
                return ap.rearrange("p (q t) -> p q t", q=4)[:, 2 * i:2 * i + 2, :]

            for u, name, e in ORDER:
                if e != "v":
                    continue
                ch, hs = heads_of(u)
                L = lanes[u % 2]
                dve.wait_ge(wk["mm"], PE_N[u, name])
                if name in ("sb", "sk"):
                    for i in range(2):
                        p4 = ps[:, lane_bank(u, name, i), :].rearrange("p (q j t) -> p q j t", q=2, j=2)
                        for j, (dst, m) in enumerate((("NdT", "dstrict"), ("rb", "incl"))
                                                     if name == "sb" else
                                                     (("ak", "strict"), ("rk", "incl"))):
                            last = V.copy_predicated(h4(L[dst], i), bc(mask(m), 1, 2), p4[:, :, j, :])
                elif name == "sn":
                    for i in range(2):
                        p4 = ps[:, lane_bank(u, name, i), 0:T].rearrange("p (q t) -> p q t", q=2)
                        V.copy_predicated(h4(L["Nd"], i), bc(mask("dlow"), 1, 2), p4)
                        V.copy_predicated(h4(L["No"], i), bc(mask("olow"), 1, 2), p4)
                    last = V.tensor_tensor(L["E"].rearrange("p (q t) -> p q t", q=4),
                                           L["NdT"].rearrange("p (q t) -> p q t", q=4),
                                           bc(ident, 1, 4), ALU.add)
                elif name in ("E2", "E3", "E4"):
                    last = V.tensor_tensor(L["E"], L["E"], ps[:, lane_bank(u, name), :], ALU.add)
                elif name in ("MT", "M4T"):
                    last = V.tensor_copy(L[name], ps[:, lane_bank(u, name), :])
                elif name in ("y1", "y2", "U"):
                    src, dst = ("u1", "u0") if name == "y2" else ("u0", "u1")
                    last = V.tensor_tensor(L[dst], L[src], ps[:, lane_bank(u, name), 0:T], ALU.add)
                else:
                    b = lane_bank(u, name)
                    for q in range(2):
                        k = hs[q][1]
                        for p0 in (0, 64):
                            o = q * P + p0
                            last = V.tensor_scalar(Sst[p0:p0 + 64, k, :], ps[p0:p0 + 64, b, o:o + 64],
                                                   cl[p0:p0 + 64, k:k + 1], None, ALU.mult)
                last.then_inc(wk["cpv"], 1)

            dve.wait_ge(*EV_N[7, "Y"])
            y3 = ytok.rearrange("p (g v) -> p g v", v=64)
            x3 = xnflat.rearrange("p (g v) -> p g v", v=64)
            v3 = vtok.rearrange("p (g v) -> p g v", v=64)
            link(V.tensor_reduce(gs_[:, 0:32], y3, AX_X, ALU.add))
            link(V.tensor_scalar(gs_[:, 0:32], gs_[:, 0:32], 1.0 / HD, None, ALU.mult))
            link(V.tensor_tensor(y3, y3, bc(gs_[:, 0:32], 2, 64), ALU.subtract))
            link(V.tensor_tensor(xnflat, ytok, ytok, ALU.mult))
            V.tensor_reduce(gs_[:, 0:32], x3, AX_X, ALU.add).then_inc(ss_rdy, 1)
            dve.wait_ge(sd_rdy, SD["lnx"] + 1)
            link(V.reciprocal(gs_[:, 0:32], gs_[:, 32:64]))
            link(V.tensor_tensor(y3, y3, bc(gs_[:, 0:32], 2, 64), ALU.mult))
            yt = ytok.rearrange("p (t n) -> p t n", t=2)
            link(V.tensor_tensor(yt, yt, bc(row("lnx_w"), 1, 2), ALU.mult))
            V.tensor_tensor(x3, v3, bc(bon, 2, 64), ALU.mult)
            link(V.tensor_tensor(yt, yt, bc(row("lnx_b"), 1, 2), ALU.add))
            link(V.tensor_tensor(ytok, ytok, xnflat, ALU.add))
            dve.wait_ge(wk["g"], 1)
            for t in range(NT):
                V.tensor_tensor(xn[:, t, :], yt[:, t, :], mview(t), ALU.mult).then_inc(xn_rdy, 1)
            turned("o0", None)
            res_norm(0, "g0_res")
            norm("nf0", 2)
            ffn_start("ffn0")
            turned_split("nf0", "g0_ffn")
            ffn("ffn0", 0)
            res_norm(1, "g0_fres")

            def attend(layer, dv, softs, scale, add):
                s_, pr, _ = soft(softs)
                diff = layer == 1
                u0, h0 = 16 * layer, [0, 16, 24][layer]

                def out(h):
                    dve.wait_ge(pre["o"], h0 + h + 1)
                    b = (h0 + h) % 2
                    for t in range(NT):
                        dst = xn[:, t, h * dv:(h + 1) * dv]
                        src = ps[:, b, t * dv:(t + 1) * dv]
                        if diff:
                            ins = V.tensor_copy(dst, src)
                        else:
                            ins = V.tensor_scalar(dst, src, st[:, 128 + 2 * h + t:129 + 2 * h + t],
                                                  None, ALU.mult)
                    ins.then_inc(pre["ov"], 1)

                def combine(h):
                    u = 2 * h
                    dve.wait_ge(pre["e"], u0 + u + 2)
                    r = st[:, 128 + 4 * h:132 + 4 * h]
                    link(V.reciprocal(r, st[:, 96 + 2 * u:100 + 2 * u]))
                    V.tensor_scalar(pr[:, u % 4, 0:P], pr[:, u % 4, 0:P], r[:, 0:1], None, ALU.mult)
                    V.tensor_scalar(pr[:, u % 4, P:384], pr[:, u % 4, P:384], r[:, 1:2], None, ALU.mult)
                    link(V.tensor_scalar(r[:, 2:4], r[:, 2:4], d_lam[:, 5:6], None, ALU.mult))
                    V.scalar_tensor_tensor(pr[:, u % 4, 0:P], pr[:, u % 4 + 1, 0:P], r[:, 2:3],
                                           pr[:, u % 4, 0:P], ALU.mult, ALU.add)
                    V.scalar_tensor_tensor(pr[:, u % 4, P:384], pr[:, u % 4 + 1, P:384], r[:, 3:4],
                                           pr[:, u % 4, P:384], ALU.mult, ALU.add
                                           ).then_inc(pre["p"], 1)

                for u in range(16):
                    dve.wait_ge(pre["sc"], u0 + u + 1)
                    if u >= 3:
                        dve.wait_ge(pre["e"], u0 + u - 2)
                    s1 = s_[:, (u0 + u) % 3, :]
                    link(V.scalar_tensor_tensor(s1, ps[:, 3 + (u0 + u) % 3, 0:384], scale, add,
                                                ALU.mult, ALU.add))
                    V.tensor_reduce(st[:, 64 + 2 * u:65 + 2 * u], s1[:, 0:P], AX_X, ALU.max,
                                    negate=True)
                    V.tensor_reduce(st[:, 65 + 2 * u:66 + 2 * u], s1[:, P:384], AX_X, ALU.max,
                                    negate=True).then_inc(pre["s"], 1)
                    if diff:
                        if u % 2 and u >= 3:
                            combine(u // 2 - 1)
                            if u >= 5:
                                out(u // 2 - 2)
                    elif u >= 2:
                        h = u - 2
                        dve.wait_ge(pre["e"], u0 + h + 1)
                        link(V.reciprocal(st[:, 128 + 2 * h:130 + 2 * h], st[:, 96 + 2 * h:98 + 2 * h]))
                        if h:
                            out(h - 1)
                if diff:
                    combine(7)
                    out(6)
                    out(7)
                else:
                    for h in (14, 15):
                        dve.wait_ge(pre["e"], u0 + h + 1)
                        link(V.reciprocal(st[:, 128 + 2 * h:130 + 2 * h], st[:, 96 + 2 * h:98 + 2 * h]))
                        out(h - 1)
                    out(15)
                dve.wait_ge(pre["ov"], h0 + 16 // (2 if diff else 1))

            def rms_tiles(name, src, n, at, dst, scale=None):
                for t in range(NT):
                    ins = V.tensor_tensor_reduce(dst[:, t, :], src[:, t, :], src[:, t, :], 1.0, 0.0,
                                                 ALU.mult, ALU.add, st[:, at + t:at + t + 1])
                ins.then_inc(ss_rdy, 1)
                dve.wait_ge(sd_rdy, SD[name] + 1)
                link(V.reciprocal(st[:, at:at + 2], st[:, at + 2:at + 4]))
                for t in range(NT):
                    ins = V.tensor_scalar(dst[:, t, :], src[:, t, :], st[:, at + t:at + t + 1], None,
                                          ALU.mult)
                return ins

            def rotate(x1, x2, cos, sin, tmp, last=False):
                V.tensor_tensor(tmp[0], x1, cos, ALU.mult)
                V.tensor_tensor(tmp[1], x2, sin, ALU.mult)
                V.tensor_tensor(tmp[2], x1, sin, ALU.mult)
                link(V.tensor_tensor(tmp[3], x2, cos, ALU.mult))
                V.tensor_tensor(x1, tmp[0], tmp[1], ALU.subtract)
                ins = V.tensor_tensor(x2, tmp[2], tmp[3], ALU.add)
                if last:
                    ins.then_inc(pre["src"], 1)
                else:
                    link(ins)

            def quarters(buf, h, n):
                return [buf[:, i * h * n:(i + 1) * h * n].rearrange("p (h n) -> p h n", h=h)
                        for i in range(4)]

            norm("n1", 3)
            turned("n1", "g1_mix", "g_kv")
            dve.wait_ge(job_out, J["kvd"][0] + 2)
            rms_tiles("ckv", m_down[:, :, 0:KV_LORA], KV_LORA, 16, m_ckvn).then_inc(pre["tsm"], 1)
            cos1 = cst("cos1").rearrange("p (t n) -> p t n", t=2)
            sin1 = cst("sin1").rearrange("p (t n) -> p t n", t=2)
            rotate(m_down[:, :, 256:272], m_down[:, :, 272:288], cos1, sin1, quarters(m_rt, 2, 16))
            for t in range(NT):
                V.tensor_copy(m_k[:, t, :, 64:96], bc(m_down[:, t, 256:288], 1, H))
            dve.wait_ge(job_out, J["qd"][0] + 2)
            rms_tiles("cq", m_qd, Q_LORA, 20, m_cqn).then_inc(pre["tsm"], 1)
            dve.wait_ge(job_out, J["qu"][0] + 8)
            for t in range(NT):
                rotate(m_q[:, t, :, 64:80], m_q[:, t, :, 80:96], bc(cos1[:, t, :], 1, H),
                       bc(sin1[:, t, :], 1, H), quarters(m_rt, H, 16), last=(t == 1))
            dve.wait_ge(job_out, J["qk1"][0] + 16)
            attend(0, 64, m_soft, 1.0 / math.sqrt(QD), cst("amask"))
            turned("o1", None)
            res_norm(2, "g1_res")
            norm("nf1", 5)
            ffn_start("ffn1")
            turned_split("nf1", "g1_ffn")
            ffn("ffn1", 1)
            res_norm(3, "g1_fres")

            def head_norm(name, parts, tmp):
                for i, (src, _g) in enumerate(parts):
                    s4 = src.rearrange("p t (h n) -> p t h n", h=H)
                    t4 = tmp[:, i * 2048:(i + 1) * 2048].rearrange("p (t h n) -> p t h n", t=2, h=H)
                    V.tensor_tensor(t4, s4, s4, ALU.mult).then_inc(pre["osq"], 1)
                n0 = {"dqk": 0, "sqk": 2}[name]
                dve.wait_ge(pre["osq"], n0 + 2)
                V.tensor_reduce(st[:, 128:192], tmp[:, 0:4096].rearrange("p (g n) -> p g n", n=64),
                                AX_X, ALU.add).then_inc(ss_rdy, 1)
                dve.wait_ge(sd_rdy, SD[name] + 1)
                link(V.reciprocal(st[:, 128:192], st[:, 192:256]))
                for i, (src, g) in enumerate(parts):
                    for t in range(NT):
                        s3 = src[:, t, :].rearrange("p (h n) -> p h n", h=H)
                        r = st[:, 128 + 32 * i + 16 * t:144 + 32 * i + 16 * t]
                        ins = V.tensor_tensor(s3, s3, bc(r, 2, 64), ALU.mult)
                link(ins)
                for i, (src, g) in enumerate(parts):
                    for t in range(NT):
                        s3 = src[:, t, :].rearrange("p (h n) -> p h n", h=H)
                        ins = V.tensor_tensor(s3, s3, bc(row(g), 1, H), ALU.mult)
                link(ins)

            def rope2(src, h, tmp, last=False):
                for t in range(NT):
                    s3 = src[:, t, :].rearrange("p (h n) -> p h n", h=h)
                    rotate(s3[:, :, 0:8], s3[:, :, 8:16], bc(cs2[:, 0, t, :], 1, h),
                           bc(cs2[:, 1, t, :], 1, h), quarters(tmp, h, 8), last and t == 1)

            norm("n2", 6)
            turned("n2", "n0_mix")
            a, _n = ROW["lam"]
            for i in range(2):
                last = V.tensor_tensor_reduce(d_rt[:, i * 64:(i + 1) * 64],
                                              rows[:, a + 128 * i:a + 128 * i + 64],
                                              rows[:, a + 128 * i + 64:a + 128 * i + 128], 1.0, 0.0,
                                              ALU.mult, ALU.add, d_lam[:, i:i + 1])
            last.then_inc(pre["src2"], 1)
            dve.wait_ge(job_out, J["din"][0] + 12)
            head_norm("dqk", [(d_p[:, 0], "dq"), (d_p[:, 1], "dk")], d_sq)
            dve.wait_ge(pre["osd"], 1)
            link(V.tensor_tensor(d_lam[:, 4:5], d_lam[:, 3:4], d_lam[:, 2:3], ALU.subtract))
            link(V.tensor_scalar(d_lam[:, 5:6], d_lam[:, 4:5], LAM_INIT, None, ALU.subtract))
            dve.wait_ge(wk["cs"], 1)
            rope2(d_p[:, 0], H, d_rt)
            rope2(d_p[:, 1], H, d_rt, last=True)
            attend(1, P, d_soft, HD ** -0.5, cst("amask"))
            link(V.tensor_tensor(d_sq[:, 0:2048], xnflat, xnflat, ALU.mult))
            V.tensor_reduce(st[:, 24:40], d_sq[:, 0:2048].rearrange("p (g n) -> p g n", n=P), AX_X,
                            ALU.add).then_inc(ss_rdy, 1)
            dve.wait_ge(sd_rdy, SD["dsub"] + 1)
            link(V.reciprocal(st[:, 24:40], st[:, 40:56]))
            link(V.tensor_scalar(st[:, 24:40], st[:, 24:40], 1.0 - LAM_INIT, None, ALU.mult))
            xg = xnflat.rearrange("p (g n) -> p g n", n=P)
            link(V.tensor_tensor(xg, xg, bc(st[:, 24:40], 2, P), ALU.mult))
            for t in range(NT):
                V.tensor_tensor(xg[:, 8 * t:8 * t + 8, :], xg[:, 8 * t:8 * t + 8, :],
                                bc(row("sub"), 1, 8), ALU.mult).then_inc(xn_rdy, 1)
            turned("o2", None)
            res_plain(4)
            norm("nm0", 8)
            ffn_start("mlp0")
            turned_split("nm0", "n0_mlp")
            ffn("mlp0")
            res_plain(5)

            norm("n3", 9)
            turned("n3", "n1_mix")
            dve.wait_ge(job_out, J["sin"][0] + 10)
            rms_tiles("scq", s_p[:, :, 0:256], 256, 16, s_cqn).then_inc(pre["tsm"], 1)
            ki = s_ki[:, :, 0, :]
            link(rms_tiles("kidx", s_p[:, :, 2304:2368], 64, 20, ki))
            rope2(ki, 1, s_rt)
            V.tensor_copy(s_ki[:, :, 1, :], ki)
            link(V.tensor_scalar(s_p[:, :, 2368:2376], s_p[:, :, 2368:2376],
                                 IDX_H ** -0.5 * 64 ** -0.5, None, ALU.mult))
            dve.wait_ge(job_out, J["uq"][0] + 6)
            head_norm("sqk", [(s_q, "sq"), (s_p[:, :, 256:1280], "sk")], s_sq)
            rope2(s_q, H, s_rt)
            rope2(s_p[:, :, 256:1280], H, s_rt)
            rope2(s_qi, IDX_H, s_rt, last=True)
            for i in range(IDX_H):
                dve.wait_ge(pre["ixr"], i + 1)
                for t, (lo, hi) in enumerate(((0, P), (P, 384))):
                    w = s_p[:, t, 2368 + i:2369 + i]
                    r = s_ixr[:, i % 2, lo:hi]
                    if i == 0:
                        ins = V.tensor_scalar(s_acc[:, lo:hi], r, w, None, ALU.mult)
                    else:
                        ins = V.scalar_tensor_tensor(s_acc[:, lo:hi], r, w, s_acc[:, lo:hi],
                                                     ALU.mult, ALU.add)
                ins.then_inc(pre["ixs"], 1)
                dve.wait_ge(pre["ixs"], i + 1)
            link(V.tensor_tensor(s_w, s_acc, cst("amask"), ALU.add))
            m8 = st[:, 32:48]
            for r in range(TOPK // 8):
                for t, (lo, hi) in enumerate(((0, P), (P, 384))):
                    ins = V.max(m8[:, 8 * t:8 * t + 8], s_w[:, lo:hi])
                link(ins)
                for t, (lo, hi) in enumerate(((0, P), (P, 384))):
                    ins = V.match_replace(s_w[:, lo:hi], m8[:, 8 * t:8 * t + 8], s_w[:, lo:hi], TAKEN)
                link(ins)
            link(V.tensor_scalar(s_sel, s_w, TAKEN, -NEG, ALU.is_equal, ALU.mult))
            link(V.tensor_scalar(s_sel, s_sel, NEG, None, ALU.add))
            attend(2, 64, s_soft, HD ** -0.5, s_sel)
            turned("o3", None)
            res_plain(6)
            norm("nm1", 11)
            ffn_start("mlp1")
            turned_split("nm1", "n1_mlp")
            ffn("mlp1")
            res_plain(7)


def constants():
    con, ncon = offsets(CONSTS)
    c = np.zeros((P, ncon), np.float32)

    def put(name, v):
        a, n = con[name]
        c[:, a:a + n] = v

    p = np.arange(P)
    put("ident", np.eye(P))
    put("blk1", (p[:, None] // 64 == p[None, :] // 64))
    put("sel2", (p[:, None] // 64 == np.arange(2)[None, :]))
    m = np.zeros((P, 384))
    m[:64, 64:128] = NEG
    m[:64, 320:384] = NEG
    put("amask", m)
    inv = (np.float32(1.0) / (np.float32(10000.0) ** (np.arange(0, QK_ROPE, 2, dtype=np.float32) / np.float32(QK_ROPE))))
    ang = np.arange(T, dtype=np.float32)[:, None] * inv[None, :].astype(np.float32)
    for name, f in (("cos1", np.cos), ("sin1", np.sin)):
        put(name, f(ang.astype(np.float64)).reshape(2, P, 16).transpose(1, 0, 2).reshape(P, 32))
    put("inv2", (np.float32(500000.0) ** (-np.arange(0, 16, 2, dtype=np.float32) / np.float32(16)))[None, :])
    put("eps", np.array([[EPS_NORM, EPS_LNX]]))
    put("ones", 1.0)
    a, b = p[:, None], p[None, :]
    ms = {"incl": a <= b, "strict": a < b, "dstrict": (a < b) & (a // 16 == b // 16),
          "dlow": (b < a) & (a // 16 == b // 16), "olow": (b < a) & (a // 16 != b // 16)}
    return c, np.concatenate([ms[n].astype(np.float32) for n in MASKS], axis=1)


def kernel(**inputs):
    import concourse.bacc as bacc
    from concourse.bass_utils import run_bass_kernel_spmd

    g = {k: np.asarray(v) for k, v in inputs.items()}

    def tiles(v):
        return np.ascontiguousarray(v.reshape(-1, P).T)

    parts = {"g0_mix": g["norm_g"][0, 0], "g0_ffn": g["norm_g"][0, 2], "g1_mix": g["norm_g"][1, 0],
             "g_kv": g["kv_norm_g"], "g1_ffn": g["norm_g"][1, 2], "n0_mix": g["norm_mix_2"][0],
             "n0_mlp": g["norm_mlp_2"][0], "n1_mix": g["norm_mix_2"][1], "n1_mlp": g["norm_mlp_2"][1],
             "mu": g["a_mu"][0], "w0": g["a_w0"], "a0": g["a_a0"], "k_k": g["a_k_k"],
             "k_a": g["a_k_a"], "r_k": g["a_r_k"], "kv_a": g["kv_a_norm_g"], "q_n": g["q_norm_g"],
             "cq_n": g["dsa_cq_norm_2"], "conv_w0": g["ffn_conv_w"][0], "conv_b0": g["ffn_conv_b"][0],
             "conv_w1": g["ffn_conv_w"][1], "conv_b1": g["ffn_conv_b"][1]}
    rws = {"g0_res": g["norm_g"][0, 1], "g0_fres": g["norm_g"][0, 3], "g1_res": g["norm_g"][1, 1],
           "g1_fres": g["norm_g"][1, 3], "lnx_w": g["a_lnx_w"], "lnx_b": g["a_lnx_b"],
           "dq": g["diff_q_norm_2"], "dk": g["diff_k_norm_2"], "sub": g["diff_subln_2"],
           "sq": g["dsa_q_norm_2"], "sk": g["dsa_k_norm_2"],
           "lam": np.concatenate([g[n].reshape(-1) for n in
                                  ("diff_lam_q1_2", "diff_lam_k1_2", "diff_lam_q2_2", "diff_lam_k2_2")])}
    con, masks = constants()
    arrays = {
        "x": g["x"][0], "positions": tiles(g["positions_2"]), "con": con, "masks": masks,
        "cols": np.concatenate([tiles(parts[n]) for n, _ in COLS], axis=1),
        "rows": np.concatenate([rws[n].reshape(1, -1) for n, _ in ROWS], axis=1),
        "w_r": g["a_w_rkv"][0, 0], "w_k": g["a_w_rkv"][0, 1], "w_v": g["a_w_rkv"][0, 2],
        "w_lora": np.concatenate([g["a_w1"][0], g["a_a1"][0], g["a_g1"][0]], axis=1),
        "a_w2": g["a_w2"][0], "a_a2": g["a_a2"][0], "a_g2": g["a_g2"][0], "a_w_o": g["a_w_o"][0],
        "kv_w_down": g["kv_w_down"], "kv_w_up": g["kv_w_up"], "q_w_down": g["q_w_down"][0],
        "q_w_up": g["q_w_up"][0], "o_w": g["o_w"][0], "diff_w_in": g["diff_w_in_2"][0],
        "diff_w_out": g["diff_w_out_2"][0], "dsa_w_in": g["dsa_w_in_2"][0],
        "w_uqi": np.concatenate([g["dsa_w_uq_2"][0], g["dsa_w_uq_idx_2"][0]], axis=1),
        "dsa_w_out": g["dsa_w_out_2"][0],
    }
    for n in range(2):
        arrays["ffn_w_in%d" % n] = g["ffn_w_in"][n]
        arrays["ffn_w_out%d" % n] = g["ffn_w_out"][n]
        arrays["mlp_w1_%d" % n] = g["mlp_w1_2"][n]
        arrays["mlp_w2_%d" % n] = g["mlp_w2_2"][n]
    arrays = {"in_" + k: np.ascontiguousarray(v) for k, v in arrays.items()}
    nc = bacc.Bacc("TRN2", target_bir_lowering=False, num_devices=1)
    d = {k[3:]: nc.dram_tensor(k, v.shape, mybir.dt.from_np(v.dtype), kind="ExternalInput").ap()
         for k, v in arrays.items()}
    out = nc.dram_tensor("out", (T, D), F32, kind="ExternalOutput").ap()
    program(nc, d, out)
    r = run_bass_kernel_spmd(nc, [arrays], core_ids=[0])
    return r.results[0]["out"].reshape(1, T, D)
```

```python
from contextlib import ExitStack
import math

import numpy as np
import concourse.bass as bass
from concourse import mybir

F32 = mybir.dt.float32
F32R = mybir.dt.float32r
I32 = mybir.dt.int32
ALU = mybir.AluOpType
ACT = mybir.ActivationFunctionType
AX_X = mybir.AxisListType.X

P = 128
T = 256
NT = T // P
D = 1024
KT = D // P
DFF = 2816
DFF2 = 4096
H = 16
HD = 64
LORA = 64
GLORA = 160
KV_LORA = 256
QK_ROPE = 32
QK_NOPE = 64
QD = QK_NOPE + QK_ROPE
Q_LORA = 384
TOPK = min(256, T // 4)
IDX_H = 8
EPS_NORM = 1e-6
EPS_LNX = 64e-5
NEG = -1e30
PAD = -3.0e38
TAKEN = -3.3e38
DSA_Q = 256
MAGIC = 1.5 * 2 ** 23
TWO_PI = (6.28125, 253 / 2 ** 17, 2 * math.pi - 6.28125 - 253 / 2 ** 17)
E05 = math.exp(-0.5)
LAM_INIT = 0.8 - 0.6 * math.exp(-0.3 * 0)

COLS = [("g0_mix", 8), ("g0_ffn", 8), ("g1_mix", 8), ("g_kv", 8), ("g1_ffn", 8), ("n0_mix", 8),
        ("n0_mlp", 8), ("n1_mix", 8), ("n1_mlp", 8), ("mu", 48), ("w0", 8), ("a0", 8), ("k_k", 8),
        ("k_a", 8), ("r_k", 8), ("kv_a", 2), ("q_n", 3), ("cq_n", 2), ("conv_w0", 66),
        ("conv_b0", 22), ("conv_w1", 66), ("conv_b1", 22), ("sub", 1)]
ROWS = [("g0_res", D), ("g0_fres", D), ("g1_res", D), ("g1_fres", D), ("lnx_w", D), ("lnx_b", D),
        ("dq", 64), ("dk", 64), ("sq", 64), ("sk", 64), ("lam", 256)]
CONSTS = [("ident", 128), ("blk1", 128), ("sel2", 2), ("amask", 384), ("cos1", 32), ("sin1", 32),
          ("inv2", 8), ("eps", 2), ("ones", 128)]
MASKS = ["incl", "strict", "dstrict", "dlow", "olow"]


def offsets(table):
    at, out = 0, {}
    for name, n in table:
        out[name] = (at, n)
        at += n
    return out, at


def program(nc, d, out_d):
    COL, NCOL = offsets(COLS)
    ROW, NROW = offsets(ROWS)
    CON, NCON = offsets(CONSTS)
    ctx = ExitStack()
    with ctx:
        place = {}
        free = [nc.sbuf_base + -nc.sbuf_base % 32]

        def sb(name, shape, dt=F32):
            place[name] = free[0]
            free[0] += 4 * math.prod(shape[1:]) + (-4 * math.prod(shape[1:])) % 32
            return nc.alloc_sbuf_tensor_at(name, shape, dt, offset=place[name])

        def over(name, base, at, shape, dt=F32R):
            return nc.alloc_sbuf_tensor_at(name, shape, dt, offset=place[base] + 4 * at)

        def sem(name):
            return ctx.enter_context(nc.semaphore(name))

        ps = ctx.enter_context(nc.psum_tensor("ps", [P, 8, 512], F32))
        ringA = sb("ringA", [P, 2, 4096])
        ringB = sb("ringB", [P, 2, 4096])
        x = sb("x", [P, NT, D])
        hT = sb("hT", [P, KT, T])
        xn = sb("xn", [P, NT, D])
        cols = sb("cols", [P, NCOL])
        rows = sb("rows", [P, NROW])
        con = sb("con", [P, NCON])
        masks = sb("masks", [P, len(MASKS), P])
        posi = sb("posi", [P, NT], I32)
        cs2 = sb("cs2", [P, 2, NT, 8])
        st = sb("st", [P, 256])
        NAR = 21640
        arena = sb("arena", [P, NAR])
        Ah = over("Ah", "arena", 0, [P, 2, 2048])
        Al = over("Al", "arena", 4096, [P, 2, 2048])
        Bh = over("Bh", "arena", 8192, [P, 2, 2048])
        Bl = over("Bl", "arena", 12288, [P, 2, 2048])
        hTl = over("hTl", "arena", 16384, [P, KT, T])
        hidh = over("hidh", "arena", 18432, [P, 2, 512])
        hidl = over("hidl", "arena", 19456, [P, 2, 512])
        hTh = over("hTh", "hT", 0, [P, KT, T])

        def col(name, k):
            return cols[:, COL[name][0] + k:COL[name][0] + k + 1]

        def gcol(name, k):
            return col(name, 0 if name == "sub" else k)

        def colx(name, k):
            return cols[:, bass.ds(COL[name][0] + k, 1)]

        def row(name):
            a, n = ROW[name]
            return rows[:, a:a + n]

        def cst(name):
            a, n = CON[name]
            return con[:, a:a + n]

        ident = cst("ident")

        def mask(name):
            return masks[:, MASKS.index(name), :].bitcast(I32)

        class Carve:
            def __init__(self, at=0):
                self.at = at

            def __call__(self, n):
                a = self.at
                self.at += n
                assert self.at <= NAR, self.at
                return arena[:, a:a + n]

        con_in = sem("con_in")
        const_in = sem("const_in")
        x_in = sem("x_in")
        a_loaded = [sem("a_loaded0"), sem("a_loaded1")]
        b_loaded = [sem("b_loaded0"), sem("b_loaded1")]
        a_used = sem("a_used")
        ah_rdy = sem("ah_rdy")
        al_rdy = sem("al_rdy")
        bh_rdy = sem("bh_rdy")
        bl_rdy = sem("bl_rdy")
        b_used = sem("b_used")
        ht_rdy = sem("ht_rdy")
        out_done = sem("out_done")
        dve_c = sem("dve_c")
        act_c = sem("act_c")
        ss_rdy = sem("ss_rdy")
        sd_rdy = sem("sd_rdy")
        rms_rdy = sem("rms_rdy")
        xn_rdy = sem("xn_rdy")
        tp_rdy = sem("tp_rdy")
        hv_rdy = sem("hv_rdy")
        ha_rdy = sem("ha_rdy")
        job_rdy = sem("job_rdy")
        job_out = sem("job_out")
        m_rdy = sem("m_rdy")
        msd_rdy = sem("msd_rdy")
        x_done = sem("x_done")
        f1_rdy = sem("f1_rdy")
        gc_rdy = sem("gc_rdy")
        ge_rdy = sem("ge_rdy")
        h_rdy = sem("h_rdy")
        xs_rdy = sem("xs_rdy")
        wk = {n: sem("wk_" + n) for n in
              ["ang", "cs",
               "sq", "rkp",
               "lc", "kkn",
               "exp",
               "ops", "clr",
               "mm", "cpv", "cpa",
               "g", "cv"]}
        pool_c = sem("pool_c")
        hd_go = sem("hd_go")
        hd_rdy = sem("hd_rdy")
        pre = {n: sem("at_" + n) for n in
               ["tsm", "src",
                "src2", "osd",
                "osq",
                "sc", "s", "e",
                "p",
                "pt", "pte",
                "o", "ov",
                "ix", "ixr", "ixs"]}

        def kview(name, w):
            return d[name].rearrange("(k p) n -> p k n", p=P)

        def std(name, n0, n):
            v = kview(name, n)
            return [(0, 4, n, v[:, 0:4, n0:n0 + n]), (4 * n, 4, n, v[:, 4:8, n0:n0 + n])]

        A = []
        a_at = {}

        def add(name, loads):
            a_at.setdefault(name, len(A))
            A.append(loads)

        add("lora", std("w_lora", 0, 2 * LORA + GLORA))
        for w in ("w_k", "w_r", "w_v"):
            for c in range(2):
                add(w, std(w, c * 512, 512))
        for c in range(2):
            add("wo0", std("a_w_o", c * 512, 512))
        a_at["ffn0"] = len(A)
        A += [None] * 11
        add("kvd", std("kv_w_down", 0, KV_LORA + QK_ROPE))
        add("qd", std("q_w_down", 0, Q_LORA))
        v = kview("kv_w_up", 2048)
        add("kvu", [(0, 1, 2048, v[:, 0:1, :]), (2048, 1, 2048, v[:, 1:2, :])])
        v = kview("q_w_up", 1536)
        for c in range(2):
            add("qu", [(0, 2, 768, v[:, 0:2, c * 768:(c + 1) * 768]),
                       (2 * 768, 1, 768, v[:, 2:3, c * 768:(c + 1) * 768])])
        for c in range(2):
            add("wo1", std("o_w", c * 512, 512))
        a_at["ffn1"] = len(A)
        A += [None] * 11
        for c in range(6):
            add("din", std("diff_w_in", c * 512, 512))
        for c in range(2):
            add("wo2", std("diff_w_out", c * 512, 512))
        a_at["mlp0"] = len(A)
        A += [None] * 8
        DSA_IN = 256 + 2048 + 64 + 8
        for c in range(5):
            add("sin", std("dsa_w_in", c * 512, min(512, DSA_IN - c * 512)))
        v = kview("w_uqi", 1536)
        add("uq", [(0, 1, 1536, v[:, 0:1, :]), (1536, 1, 1536, v[:, 1:2, :])])
        for c in range(2):
            add("wo3", std("dsa_w_out", c * 512, 512))
        a_at["mlp1"] = len(A)
        A += [None] * 8

        G0 = {"ffn0": 0, "ffn1": 11, "mlp0": 22, "mlp1": 30}
        NCH = {"ffn0": 11, "ffn1": 11, "mlp0": 8, "mlp1": 8}

        def chunk_walk(eng, name, step):
            n = NCH[name]
            step(0, 0)
            step(1, 1)
            pairs = (n - 3) // 2
            with eng.Fori(0, pairs) as i:
                step(i * 2 + 2, 0)
                step(i * 2 + 3, 1)
            for c in range(2 + 2 * pairs, n):
                step(c, c % 2)

        JOBS = [("lora", 2), ("k", 4), ("wz", 4), ("az", 4), ("r", 4), ("kk", 4), ("v", 2),
                ("bonus", 1), ("v2", 2), ("bk", 4), ("kvd", 2), ("qd", 2), ("ckv", 1), ("kvu", 8), ("cq", 2), ("qu", 8),
                ("qk1", 16), ("din", 12), ("qk2", 8), ("sin", 10), ("scq", 1), ("uq", 6), ("ixt", 3),
                ("qk3", 8)]
        J, NJ = offsets(JOBS)

        def bank(j):
            return 4 + j % 4

        def tbank(name, i):
            if name == "n0":
                return i
            return 4 + (i + {"n2": J["din"][0], "n3": J["sin"][0]}.get(name, 0)) % 4

        TI = {n: i for i, n in enumerate(["n0", "o0", "nf0", "n1", "o1", "nf1", "n2", "o2", "nm0",
                                          "n3", "o3", "nm1"])}
        XN = {n: i for i, n in enumerate([n for n in TI if n not in ("o1", "o3")])}
        MI = {n: i for i, n in enumerate(["o0", "ffn0", "o1", "ffn1", "o2", "mlp0", "o3", "mlp1"])}
        SD = {n: i for i, n in enumerate(
            ["lnx0", "lnx1", "ckv", "cq", "dq", "dk", "scq", "sk", "kidx", "sq"])}
        NI = {n: i for i, n in enumerate(["n0", "nf0", "n1", "nf1", "n2", "nm0", "n3", "nm1"])}

        INST = ["ffn0", "ffn1", "mlp0", "mlp1"]
        a_last = {}

        def jobs_use(name, per_slot):
            def put(a0, n, j0):
                for s in range(n):
                    a_last[a0 + s] = (job_rdy, j0 + per_slot * (s + 1))
            return put

        jobs_use("w_k", 2)(a_at["w_k"], 2, J["k"][0])
        jobs_use("w_r", 2)(a_at["w_r"], 2, J["r"][0])
        jobs_use("w_v", 2)(a_at["w_v"], 1, J["v"][0])
        jobs_use("w_v", 2)(a_at["w_v"] + 1, 1, J["v2"][0])
        jobs_use("lora", 2)(a_at["lora"], 1, J["lora"][0])
        jobs_use("kvd", 2)(a_at["kvd"], 1, J["kvd"][0])
        jobs_use("kvu", 8)(a_at["kvu"], 1, J["kvu"][0])
        jobs_use("qd", 2)(a_at["qd"], 1, J["qd"][0])
        jobs_use("qu", 4)(a_at["qu"], 2, J["qu"][0])
        jobs_use("uq", 6)(a_at["uq"], 1, J["uq"][0])
        SPLIT, a_free = {}, []
        used = 0
        for w, n in [("wo0", 2), ("ffn0", 11), ("wo1", 2), ("ffn1", 11), ("din", 6), ("wo2", 2),
                     ("mlp0", 8), ("sin", 5), ("wo3", 2), ("mlp1", 8)]:
            for c in range(n):
                SPLIT[a_at[w] + c] = len(SPLIT)
                a_last[a_at[w] + c] = (al_rdy, 2 * len(SPLIT))
                if w in INST:
                    a_free += [(f1_rdy, 2 * (G0[w] + c) + half + 1) for half in range(2)]
                    continue
                used += 1
                a_free.append((a_used, used))
                if w in ("din", "sin"):
                    a_free.append((job_rdy, J[w][0] + 2 * c + 2))
                elif c == 0:
                    used += 1
                    a_free.append((a_used, used))
                else:
                    a_free.append((m_rdy, 2 * (MI["o" + w[2]] + 1)))
        S0 = {w: 2 * SPLIT[a_at[w]] for w in INST}

        def k_half(ap, a, half):
            n = A[a][0][2] * 4
            return ap[:, 0:n] if ap.shape[-1] == 2048 else ap[:, half * n:(half + 1) * n]

        def b_used_at(w, ch, half):
            return ch * 2 + (2 * G0[w] - INST.index(w) + half + 1)

        def a_half(w, slot, half):
            if w.startswith("ffn"):
                return ringA[:, slot, :].rearrange("p (k j n) -> p k j n", k=KT, j=2)[
                    :, :, :, half * P:(half + 1) * P]
            return ringA[:, slot, :].rearrange("p (k n) -> p k n", k=KT)[
                :, :, half * T:(half + 1) * T]

        def a_split(w, buf, half):
            if w.startswith("ffn"):
                return buf[:, half, :].rearrange("p (k j n) -> p k j n", k=KT, j=2)
            return buf[:, half, :].rearrange("p (k n) -> p k n", k=KT)

        def b_len(w):
            return D if w.startswith("ffn") else 2 * D

        c = Carve()
        lo2 = c(4096)
        w2_sb, a2_sb = lo2[0:LORA, 0:1024], lo2[0:LORA, 1024:2048]
        g2a_sb, g2b_sb = lo2[:, 2048:3072], lo2[0:GLORA - P, 3072:4096]
        xx = c(2048)
        rT, kT_, vtok, zs, aT = c(2048), c(2048), c(2048), c(2048), c(2048)
        ARf = c(4096)
        AR = ARf.rearrange("p (k c j t) -> p k c j t", k=KT, c=2, j=2)
        sigg = c(512)
        lm = c(16)
        cl = c(8)
        bon = c(32)
        Sst = c(512).rearrange("p (k v) -> p k v", k=KT)
        gs_ = c(64)
        diag = Sst.rearrange("p k v -> p (k v)")[:, 0:T].rearrange("p (t n) -> p t n", t=NT)
        lT = Sst.rearrange("p k v -> p (k v)")
        R = [ringB[:, i // 2, 2048 * (i % 2):2048 * (i % 2) + 2048] for i in range(4)]
        MIXES = [(3, R[0]), (4, R[1]), (5, ARf[:, 0:2048]), (1, ARf[:, 2048:4096]), (0, R[2]),
                 (2, R[0])]
        Lc, kkb = R[1], R[3]
        btk = R[2].rearrange("p (j c) -> p j c", j=2)
        eN = kT_
        hflat = hT[:, :, :].rearrange("p k t -> p (k t)")
        xnflat = xn[:, :, :].rearrange("p t n -> p (t n)")
        eQ, eP = xnflat, hflat
        k2 = xx
        bT = aT
        ytok = hflat
        lanes = []
        for pool in ([rT, kT_, zs], [R[0], Lc, kkb]):
            bufs = [r[:, 512 * i:512 * i + 512] for r in pool for i in range(4)]
            n = len(lanes)
            names = ["NdT", "rb", "ak", "rk", "Nd", "No", "N2", "N2T", "N4", "N4T", "N8", "E"]
            lane = dict(zip(names, bufs))
            lane.update(M=lane["N2T"], MT=lane["N4T"], M2=lane["N2"], M2T=lane["N4"], M4T=lane["N8"])
            for i, r in enumerate(["R", "u0", "u1"]):
                lane[r] = lo2[:, n * 768 + i * 256:n * 768 + i * 256 + 256]
            lanes.append(lane)

        ht = xnflat[:, 0:512]
        gc = xnflat[:, 512:1024].rearrange("p (g n) -> p g n", g=2)
        ge = xnflat[:, 1024:1536].rearrange("p (g n) -> p g n", g=2)
        rl = xnflat[:, 512:1536].rearrange("p (g n) -> p g n", g=2)

        c = Carve()
        m_down = c(576).rearrange("p (t n) -> p t n", t=2)
        m_ckvn = c(512).rearrange("p (t n) -> p t n", t=2)
        m_ckvT = c(512).rearrange("p (k n) -> p k n", k=2)
        m_qd = c(768).rearrange("p (t n) -> p t n", t=2)
        m_cqn = c(768).rearrange("p (t n) -> p t n", t=2)
        m_cqT = c(768).rearrange("p (k n) -> p k n", k=3)
        m_k = c(3072).rearrange("p (t h n) -> p t h n", t=2, h=H)
        m_q = c(3072).rearrange("p (t h n) -> p t h n", t=2, h=H)
        m_rt = c(1024)
        m_KT = ringB[:, 0, :].rearrange("p (h t) -> p h t", h=H)
        m_QT = ringB[:, 1, :].rearrange("p (h t) -> p h t", h=H)
        hT2 = m_QT.rearrange("p h t -> p (h t)")[:, 0:2048].rearrange("p (k t) -> p k t", k=KT)
        m_v = rows[:, ROW["lnx_w"][0]:ROW["lnx_w"][0] + 2048].rearrange("p (t n) -> p t n", t=2)
        m_soft = c(3456)

        c = Carve(8192)
        d_p = c(6144).rearrange("p (j t n) -> p j t n", j=3, t=2)
        d_soft = c(3456)
        c.at = 18432
        d_rt = c(1024)
        d_lam = c(8)
        d_QT = ringB[:, 0, 0:2048].rearrange("p (k t) -> p k t", k=8)
        d_KT = ringB[:, 0, 2048:4096].rearrange("p (k t) -> p k t", k=8)
        d_sq = ringB[:, 1, :]

        c = Carve(8192)
        s_p = c(2 * DSA_IN).rearrange("p (t n) -> p t n", t=2)
        s_cqn = c(512).rearrange("p (t n) -> p t n", t=2)
        s_cqT = c(512).rearrange("p (k n) -> p k n", k=2)
        s_ki = c(256).rearrange("p (t j n) -> p t j n", t=2, j=2)
        s_KIT = c(256)
        s_rt = c(512)
        s_rtp = d_rt[:, 0:512]
        s_acc = c(384)
        s_w = c(384)
        s_sel = c(384)
        assert c.at <= 16384
        c.at = 16384
        s_soft = c(3456)
        s_ixr = c(768).rearrange("p (j n) -> p j n", j=2)
        s_q = ringB[:, 0, 0:2048].rearrange("p (t n) -> p t n", t=2)
        s_qi = ringB[:, 0, 2048:3072].rearrange("p (t n) -> p t n", t=2)
        s_QIT = ringB[:, 0, 3072:4096].rearrange("p (k t) -> p k t", k=4)
        qk_at = ringB[:, 1, :]
        s_QT = qk_at[:, 0:2048].rearrange("p (k t) -> p k t", k=8)
        s_KT = qk_at[:, 2048:4096].rearrange("p (k t) -> p k t", k=8)
        s_sq = qk_at

        def soft(r):
            return (r[:, 0:1152].rearrange("p (j n) -> p j n", j=3),
                    r[:, 1152:2688].rearrange("p (j n) -> p j n", j=4),
                    r[:, 2688:3456].rearrange("p (j n) -> p j n", j=2))

        def fm(ap):
            return ap.rearrange("p (k t) -> p k t", k=KT)

        def bc(ap, axis, n):
            shape = list(ap.shape)
            shape.insert(axis, n)
            return ap.unsqueeze(axis).to_broadcast(shape)

        STEPS = [("sb", "v"), ("sk", "v"), ("sn", "v"), ("N2", "a"), ("N2T", "a"), ("E2", "v"),
                 ("N4", "a"), ("N4T", "a"), ("E3", "v"), ("N8", "a"), ("E4", "v"), ("M", "a"),
                 ("MT", "v"), ("M2", "a"), ("M2T", "a"), ("M4T", "v"), ("rhs", "a"), ("y0", "a"),
                 ("y1", "v"), ("y2", "v"), ("U", "v"), ("Y", "a"), ("S", "v")]
        BANKS = {"sb": (0, 1), "sk": (2, 3), "sn": (0, 1), "N2": (2,), "N2T": (3,), "E2": (0,),
                 "N4": (1,), "N4T": (2,), "E3": (3,), "N8": (0,), "E4": (1,), "M": (2,), "MT": (3,),
                 "M2": (0,), "M2T": (1,), "M4T": (2,), "rhs": (3, 0), "y0": (1,), "y1": (2,),
                 "y2": (3,), "U": (0,), "Y": (1, 2), "S": (3,)}
        ORDER = [(u, name, e) for pair in range(4) for name, e in STEPS
                 for u in (2 * pair, 2 * pair + 1) if name != "S" or u < 4]
        PE_N = {(u, name): n + 1 for n, (u, name, _) in enumerate(ORDER)}
        EV_N = {}
        for e in "va":
            for n, (u, name, _) in enumerate([o for o in ORDER if o[2] == e]):
                EV_N[u, name] = (wk["cpv"] if e == "v" else wk["cpa"], n + 1)

        def heads_of(u):
            g = u % 4
            return u // 4, [(0, 2 * g, 0), (1, 2 * g + 1, 0), (2, 2 * g, 64), (3, 2 * g + 1, 64)]

        def lane_bank(u, name, i=0):
            return 4 * (u % 2) + BANKS[name][i]

        block = ctx.enter_context(nc.Block())

        @block.sync
        def _(sp):
            sp.dma_start(x[:, :, :], d["x"].rearrange("(t p) n -> p t n", p=P)).then_inc(x_in, 16)
            sp.dma_start(con[:, :], d["con"]).then_inc(con_in, 16)
            sp.dma_start(cols[:, :], d["cols"]).then_inc(con_in, 16)

            def load_a(i):
                if i >= 2:
                    s, v = a_last[i - 2]
                    sp.wait_ge(s, v)
                for off, k, n, src in A[i]:
                    dst = ringA[:, i % 2, off:off + k * n].rearrange("p (k n) -> p k n", k=k)
                    sp.dma_start(dst, src).then_inc(a_loaded[i % 2], 16)

            def ffn_loads(w, gate_up):
                n = INST.index(w)
                a0, g0 = a_at[w], G0[w]

                def load_a(ch, par=None):
                    par = ch if par is None else par
                    ap = (a0 + par) % 2
                    if isinstance(ch, int):
                        s, v = a_last[a0 + ch - 2]
                        sp.wait_ge(s, v)
                    else:
                        sp.wait_ge(al_rdy, ch * 2 + (S0[w] - 2))
                    dst = ringA[:, ap, :].rearrange("p (k j n) -> p k j n", k=KT, j=2)
                    if gate_up:
                        wi = d["ffn_w_in%d" % n].rearrange("(k p) m -> p k m", p=P)
                        for j in range(2):
                            sp.dma_start(dst[:, :, j, :], wi[:, :, bass.ds(ch * 256 + j * DFF, 256)]
                                         ).then_inc(a_loaded[ap], 16)
                    else:
                        wi = d["mlp_w1_%d" % (n - 2)].rearrange("(k p) m -> p k m", p=P)
                        dst = ringA[:, ap, :].rearrange("p (k n) -> p k n", k=KT)
                        for j in range(2):
                            sp.dma_start(dst[:, 4 * j:4 * j + 4, :],
                                         wi[:, 4 * j:4 * j + 4, bass.ds(ch * 512, 512)]
                                         ).then_inc(a_loaded[ap], 16)

                def step(ch, par):
                    bp = (g0 + par) % 2
                    if isinstance(ch, int) and ch < 2:
                        if ch == 0:
                            load_a(0)
                            load_a(1)
                            sp.wait_ge(m_rdy, 2 * MI[w])
                    else:
                        load_a(ch, par)
                        sp.wait_ge(bl_rdy, ch * 2 + (2 * g0 - 2))
                    if gate_up:
                        wo, kk_ = d["ffn_w_out%d" % n], 1
                    else:
                        wo, kk_ = d["mlp_w2_%d" % (n - 2)], 2
                    dst = ringB[:, bp, 0:2048 * kk_].rearrange("p (j k n) -> p j k n", j=2, k=kk_)
                    for j in range(2):
                        src = wo[bass.ds((ch * 2 + j) * kk_ * P, kk_ * P), :].rearrange(
                            "(k p) m -> p k m", p=P)
                        sp.dma_start(dst[:, j], src).then_inc(b_loaded[bp], 16)

                chunk_walk(sp, w, step)

            load_a(0)
            load_a(1)
            for dst, src in [(w2_sb, d["a_w2"]), (a2_sb, d["a_a2"]), (g2a_sb, d["a_g2"][0:P, :]),
                             (g2b_sb, d["a_g2"][P:GLORA, :]), (posi[:, :], d["positions"]),
                             (masks[:, :, :], d["masks"].rearrange("p (m t) -> p m t", m=len(MASKS))),
                             (rows[:, :], d["rows"].to_broadcast([P, NROW]))]:
                sp.dma_start(dst, src).then_inc(const_in, 16)
            for i in range(2, a_at["ffn0"]):
                load_a(i)
            ffn_loads("ffn0", True)
            for i in range(a_at["kvd"], a_at["ffn1"]):
                load_a(i)
            ffn_loads("ffn1", True)
            for i in range(a_at["din"], a_at["mlp0"]):
                load_a(i)
            ffn_loads("mlp0", False)
            for i in range(a_at["sin"], a_at["mlp1"]):
                load_a(i)
            ffn_loads("mlp1", False)
            for t in range(NT):
                sp.wait_ge(x_done, 14 + t + 1)
                sp.dma_start(out_d.rearrange("(t p) n -> p t n", p=P)[:, t, :], x[:, t, :]
                             ).then_inc(out_done, 16)
            sp.wait_ge(out_done, 32)

        @block.tensor
        def _(pe):
            mm = nc.tensor.matmul

            def wait_a(i):
                pe.wait_ge(a_loaded[i % 2], 32 * (i // 2 + 1))

            def turn16(name):
                if name in ("o1", "o3"):
                    pe.wait_ge(pre["ov"], {"o1": 16, "o3": 40}[name])
                for t in range(NT):
                    if name in XN:
                        pe.wait_ge(xn_rdy, 2 * XN[name] + t + 1)
                    for k in range(KT):
                        o = (k % 2) * T + t * P
                        dst = ps[:, tbank(name, k // 2), o:o + P]
                        if name in NI:
                            last = mm(dst, x[:, t, k * P:(k + 1) * P], diag[:, t, :],
                                      start=True, stop=True)
                        else:
                            last = nc.tensor.transpose(dst, xn[:, t, k * P:(k + 1) * P], ident)
                        if t == 1 and k % 2:
                            last.then_inc(tp_rdy, 1)

            def wait_hT(name):
                pe.wait_ge(hv_rdy, 4 * (TI[name] + 1))
                pe.wait_ge(ha_rdy, 4 * (TI[name] + 1))

            def job_bank(j):
                if j >= 4:
                    pe.wait_ge(job_out, j - 3)
                return bank(j)

            def token_jobs(a, j0, src, kts, chunks):
                wait_a(a)
                w = sum(chunks)
                j, off = j0, 0
                for n in chunks:
                    for t in range(NT):
                        b = job_bank(j)
                        for k in range(kts):
                            last = mm(ps[:, b, 0:n], src[:, k, t * P:(t + 1) * P],
                                      ringA[:, a % 2, k * w + off:k * w + off + n],
                                      start=(k == 0), stop=(k == kts - 1))
                        last.then_inc(job_rdy, 1)
                        j += 1
                    off += n

            def split_slot(a, banks, name=None, done=None):
                n = A[a][0][2]
                for half in range(2):
                    ks = range(4 * half, 4 * half + 4)
                    pe.wait_ge(ah_rdy, 2 * SPLIT[a] + half + 1)

                    def product(t, left, right, start=False, stop=False, ready=None):
                        for k in ks:
                            if ready is not None and name and t == 0 and k % 2 == 0:
                                pe.wait_ge(ready, 4 * TI[name] + k // 2 + 1)
                            if start and k == 0 and name in ("n2", "n3"):
                                pe.wait_ge(hv_rdy, 4 * TI[name] + t + 1)
                            ins = mm(ps[:, banks[t], 0:n], left[:, k, t * P:(t + 1) * P],
                                     right[:, half, (k % 4) * n:(k % 4) * n + n],
                                     start=(start and k == 0), stop=(stop and k == KT - 1))
                        return ins

                    if done is m_rdy and half == 1:
                        pe.wait_ge(al_rdy, 2 * SPLIT[a] + half + 1)
                        for t in range(NT):
                            product(t, hTh, Ah)
                            product(t, hTl, Ah)
                            product(t, hTh, Al, stop=True).then_inc(m_rdy, 1)
                        continue
                    for t in range(NT):
                        product(t, hTh, Ah, start=True, ready=ha_rdy)
                    for t in range(NT):
                        product(t, hTl, Ah, ready=hv_rdy)
                    pe.wait_ge(al_rdy, 2 * SPLIT[a] + half + 1)
                    for t in range(NT):
                        last = product(t, hTh, Al, stop=True)
                        if half == 1 and done is not None:
                            last.then_inc(done, 1)
                    if half == 0 or done is None:
                        last.then_inc(a_used, 1)

            def out_proj(n):
                a = a_at["wo%d" % n]
                mi = MI["o%d" % n]
                if mi:
                    pe.wait_ge(x_done, 2 * mi)
                split_slot(a, (0, 2), name="o%d" % n)
                split_slot(a + 1, (1, 3), done=m_rdy)

            def split_jobs(a, j0, name=None):
                split_slot(a, (job_bank(j0), job_bank(j0 + 1)), name, job_rdy)

            def ffn(w, nf):
                n = INST.index(w)
                g0 = G0[w]

                def first(ch, half, first_one=False):
                    if not isinstance(ch, int) or g0 + ch >= 1:
                        pe.wait_ge(h_rdy, ch * 2 + (2 * g0 + half - 1))
                    for j in range(2):
                        o = ps[:, 4 + half, j * T:(j + 1) * T]
                        if j == 0:
                            pe.wait_ge(ah_rdy, ch * 2 + (S0[w] + half + 1))
                        for k in range(KT):
                            if first_one and j == 0 and k % 2 == 0:
                                pe.wait_ge(ha_rdy, 4 * TI[n_in] + k // 2 + 1)
                                if k == 0:
                                    pe.wait_ge(hv_rdy, 4 * TI[n_in] + 1)
                            mm(o, Ah[:, half, k * T + j * P:k * T + j * P + P], hTh[:, k, :],
                               start=(k == 0), stop=False)
                        for k in range(KT):
                            if first_one and j == 0 and k % 2 == 0:
                                pe.wait_ge(hv_rdy, 4 * TI[n_in] + k // 2 + 1)
                            mm(o, Ah[:, half, k * T + j * P:k * T + j * P + P], hTl[:, k, :],
                               start=False, stop=False)
                        if j == 0:
                            pe.wait_ge(al_rdy, ch * 2 + (S0[w] + half + 1))
                        for k in range(KT):
                            last = mm(o, Al[:, half, k * T + j * P:k * T + j * P + P], hTh[:, k, :],
                                      start=False, stop=(k == KT - 1))
                    last.then_inc(f1_rdy, 1)

                def second(ch, half, first_one=False, last_one=False):
                    pe.wait_ge(bl_rdy, ch * 2 + (2 * g0 + half + 1))
                    pe.wait_ge(h_rdy, ch * 2 + (2 * g0 + half + 1))
                    if first_one and MI[w]:
                        pe.wait_ge(x_done, 2 * MI[w])
                    for t in range(NT):
                        for f in range(nf):
                            for i, (hb, wb) in enumerate(((hidh, Bh), (hidh, Bl), (hidl, Bh))):
                                for c_ in range(2):
                                    o = f * D + c_ * 512
                                    last = mm(ps[:, 2 * t + c_, :],
                                              hb[:, half, f * T + t * P:f * T + t * P + P],
                                              wb[:, half, o:o + 512],
                                              start=(first_one and f == 0 and i == 0),
                                              stop=(last_one and f == nf - 1 and i == 2))
                        if last_one:
                            last.then_inc(m_rdy, 1)
                    if not last_one:
                        last.then_inc(b_used, 1)

                n_in = {"ffn0": "nf0", "ffn1": "nf1", "mlp0": "nm0", "mlp1": "nm1"}[w]
                first(0, 0, first_one=True)
                first(0, 1)
                second(0, 0, first_one=True)

                def step(ch, par):
                    if isinstance(ch, int) and ch == 0:
                        return
                    first(ch, 0)
                    second(ch + -1, 1)
                    first(ch, 1)
                    second(ch, 0)

                chunk_walk(pe, w, step)
                second(NCH[w] - 1, 1, last_one=True)

            def feature_jobs(a0, j, xi):
                for a in (a0, a0 + 1):
                    wait_a(a)
                    for jj in range(2):
                        b = job_bank(j)
                        for q in range(2):
                            for k in range(KT):
                                o = k * 512 + (2 * jj + q) * P
                                last = mm(ps[:, b, q * T:(q + 1) * T], ringA[:, a % 2, o:o + P],
                                          xi[:, k, :], start=(k == 0), stop=(k == KT - 1))
                        last.then_inc(job_rdy, 1)
                        j += 1

            pe.wait_ge(con_in, 32)
            turn16("n0")
            a = a_at["lora"]
            wait_a(a)
            wl = 2 * LORA + GLORA
            j = J["lora"][0]
            b = job_bank(j)
            for i in range(2):
                pe.wait_ge(xs_rdy, 1 + i)
                xi = fm(MIXES[i][1])
                for k in range(KT):
                    o = k * wl + i * LORA
                    last = mm(ps[0:LORA, b, i * T:(i + 1) * T], ringA[:, a % 2, o:o + LORA],
                              xi[:, k, :], start=(k == 0), stop=(k == KT - 1))
            last.then_inc(job_rdy, 1)
            b = job_bank(j + 1)
            pe.wait_ge(xs_rdy, 3)
            xi = fm(MIXES[2][1])
            for q, (o0, n) in enumerate([(2 * LORA, P), (2 * LORA + P, GLORA - P)]):
                for k in range(KT):
                    o = k * wl + o0
                    last = mm(ps[0:n, b, q * T:(q + 1) * T], ringA[:, a % 2, o:o + n],
                              xi[:, k, :], start=(k == 0), stop=(k == KT - 1))
            last.then_inc(job_rdy, 1)
            pe.wait_ge(xs_rdy, 4)
            feature_jobs(a_at["w_k"], J["k"][0], fm(MIXES[3][1]))
            pe.wait_ge(const_in, 16 * 7)
            pe.wait_ge(job_out, J["lora"][0] + 1)
            j = J["wz"][0]
            for i, wsb in enumerate((w2_sb, a2_sb)):
                for jj in range(4):
                    b = job_bank(j)
                    for q in range(2):
                        k = 2 * jj + q
                        last = mm(ps[:, b, q * T:(q + 1) * T], wsb[:, k * P:(k + 1) * P],
                                  lT[0:LORA, i * T:(i + 1) * T], start=True, stop=True)
                    last.then_inc(job_rdy, 1)
                    j += 1
            pe.wait_ge(xs_rdy, 5)
            feature_jobs(a_at["w_r"], J["r"][0], fm(MIXES[4][1]))
            pe.wait_ge(wk["sq"], 1)
            j = J["kk"][0]
            for jj in range(4):
                b = job_bank(j)
                last = mm(ps[:, b, :], cst("blk1"), xnflat[:, jj * 512:(jj + 1) * 512],
                          start=True, stop=True)
                last.then_inc(job_rdy, 1)
                j += 1
            pe.wait_ge(xs_rdy, 6)
            token_jobs(a_at["w_v"], J["v"][0], fm(MIXES[5][1]), KT, [512])
            pe.wait_ge(wk["rkp"], 1)
            b = job_bank(J["bonus"][0])
            for t in range(NT):
                for k in range(KT):
                    last = mm(ps[:, b, t * H + 2 * k:t * H + 2 * k + 2],
                              fm(hflat)[:, k, t * P:(t + 1) * P], cst("sel2"), start=True, stop=True)
            last.then_inc(job_rdy, 1)
            token_jobs(a_at["w_v"] + 1, J["v2"][0], fm(MIXES[5][1]), KT, [512])
            j = J["bk"][0]
            pe.wait_ge(wk["ops"], 1)
            for m, src in enumerate((bT, k2)):
                for jj in range(2):
                    b = job_bank(j)
                    for q in range(4):
                        k = 4 * jj + q
                        last = nc.tensor.transpose(ps[:, b, q * P:(q + 1) * P],
                                                   fm(src)[:, k, 0:P], ident)
                    last.then_inc(job_rdy, 1)
                    j += 1
            pe.wait_ge(job_out, j)
            pe.wait_ge(wk["clr"], 1)

            def need(u, *names):
                for n in names:
                    pe.wait_ge(*EV_N[u, n])

            BEFORE = {"sn": "sb", "N2": "sk", "N2T": "sk", "E2": "sn", "N4": "sn", "N4T": "N2",
                      "E3": "N2T", "N8": "E2", "E4": "N4", "M": "N4T", "MT": "E3", "M2": "N8",
                      "M2T": "E4", "M4T": "M", "rhs": "MT", "y0": "M2T", "y1": "M4T", "y2": "rhs",
                      "U": "rhs", "Y": "y0", "S": "y2"}
            PROD = {"N2": ("NdT", "Nd"), "N2T": ("Nd", "NdT"), "E2": ("N2", "E"),
                    "N4": ("N2T", "N2"), "N4T": ("N2", "N2T"), "E3": ("N4", "E"),
                    "N8": ("N4T", "N4"), "E4": ("N8", "E"), "M": ("E", "No"), "MT": ("No", "E"),
                    "M2": ("MT", "M"), "M2T": ("M", "MT"), "M4T": ("M2", "M2T"),
                    "y0": ("E", "R"), "y1": ("M4T", "u0"), "y2": ("M2T", "u1"), "U": ("MT", "u0")}
            FROM = {"N2": ("sb", "sn"), "N2T": (), "E2": ("N2",), "N4": ("N2T",), "N4T": (),
                    "E3": ("N4", "E2"), "N8": ("N4T",), "E4": ("N8", "E3"), "M": ("E4",), "MT": (),
                    "M2": ("MT", "M"), "M2T": (), "M4T": ("M2", "M2T"), "y0": ("rhs",),
                    "y1": ("y0", "M4T"), "y2": ("y1",), "U": ("y2",)}
            for u, name, _e in ORDER:
                ch, hs = heads_of(u)
                L = lanes[u % 2]
                if name in BEFORE:
                    need(u, BEFORE[name])
                elif name == "sb" and u >= 2:
                    need(u - 2, "U", "Y")
                elif name == "sk" and u >= 2:
                    need(u - 2, "Y", "S" if u - 2 < 4 else "y2")
                if name == "Y":
                    need(u, "y1", "U")
                if name in PROD:
                    need(u, *FROM[name])
                    lhs, rhs = PROD[name]
                    w = 64 if rhs in ("R", "u0", "u1") else P
                    b = lane_bank(u, name)
                    for q in range(4):
                        last = mm(ps[:, b, q * w:(q + 1) * w], L[lhs][:, q * P:(q + 1) * P],
                                  L[rhs][:, q * w:(q + 1) * w], start=True, stop=True)
                elif name in ("sb", "sk", "sn"):
                    for s, k, p0 in hs:
                        b = lane_bank(u, name, s // 2)
                        rowsl = slice(p0, p0 + 64)
                        toks = slice(ch * P, (ch + 1) * P)
                        if name == "sn":
                            last = mm(ps[:, b, (s % 2) * P:(s % 2) * P + P],
                                      AR[rowsl, k, ch, 0, :], fm(bT)[rowsl, k, toks],
                                      start=True, stop=True)
                        else:
                            src = bT if name == "sb" else k2
                            last = mm(ps[:, b, (s % 2) * T:(s % 2) * T + T], fm(src)[rowsl, k, toks],
                                      AR[rowsl, k, ch, :, :].rearrange("p j t -> p (j t)"),
                                      start=True, stop=True)
                elif name == "rhs":
                    need(u, "sk", "M2")
                    if ch:
                        need(u - 4, "S")
                    for s, k, p0 in hs:
                        b = lane_bank(u, name, s // 2)
                        o = ps[:, b, (s % 2) * 64:(s % 2) * 64 + 64]
                        hv = k * P + p0
                        last = mm(o, L["ak"][:, s * P:(s + 1) * P],
                                  vtok[:, ch * D + hv:ch * D + hv + 64], start=True, stop=(ch == 0))
                        if ch:
                            last = mm(o, AR[p0:p0 + 64, k, ch, 0, :], Sst[p0:p0 + 64, k, :],
                                      start=False, stop=True)
                elif name == "Y":
                    for s, k, p0 in hs:
                        b = lane_bank(u, name, s // 2)
                        o = ps[:, b, (s % 2) * 64:(s % 2) * 64 + 64]
                        hv = k * P + p0
                        mm(o, L["rk"][:, s * P:(s + 1) * P], vtok[:, ch * D + hv:ch * D + hv + 64],
                           start=True, stop=False)
                        last = mm(o, L["rb"][:, s * P:(s + 1) * P], L["u1"][:, s * 64:(s + 1) * 64],
                                  start=False, stop=(ch == 0))
                        if ch:
                            last = mm(o, AR[p0:p0 + 64, k, ch, 1, :], Sst[p0:p0 + 64, k, :],
                                      start=False, stop=True)
                else:
                    b = lane_bank(u, name)
                    uv = L["u1"].rearrange("p (j q v) -> p q j v", j=2, q=2)
                    for q in range(2):
                        k = hs[q][1]
                        o = ps[:, b, q * P:(q + 1) * P]
                        mm(o, btk[:, 1, k * P:(k + 1) * P], vtok[:, k * P:(k + 1) * P],
                           start=True, stop=False)
                        last = mm(o, btk[:, 0, k * P:(k + 1) * P], uv[:, q, :, :],
                                  start=False, stop=True)
                last.then_inc(wk["mm"], 1)
            need(6, "U", "Y", "y2")
            for t in range(NT):
                for half in range(2):
                    o = ps[:, 2 * t + half, :]
                    mm(o, sigg[:, t * P:(t + 1) * P], g2a_sb[:, half * 512:(half + 1) * 512],
                       start=True, stop=False)
                    last = mm(o, sigg[0:GLORA - P, T + t * P:T + (t + 1) * P],
                              g2b_sb[:, half * 512:(half + 1) * 512], start=False, stop=True)
            last.then_inc(wk["g"], 1)
            need(7, "U", "Y", "y2")
            turn16("o0")
            out_proj(0)

            turn16("nf0")
            ffn("ffn0", 1)

            def small_turn(j0, src, kts, n):
                pe.wait_ge(pre["tsm"], n)
                for jj in range((kts + 1) // 2):
                    b = job_bank(j0 + jj)
                    for k in range(2 * jj, min(2 * jj + 2, kts)):
                        for t in range(NT):
                            last = nc.tensor.transpose(
                                ps[:, b, (k % 2) * T + t * P:(k % 2) * T + t * P + P],
                                src[:, t, k * P:(k + 1) * P], ident)
                    last.then_inc(job_rdy, 1)

            def turn_blocks(j0, blocks):
                for jj in range((len(blocks) + 1) // 2):
                    b = job_bank(j0 + jj)
                    for i in range(2 * jj, min(2 * jj + 2, len(blocks))):
                        src, w = blocks[i]
                        for t in range(NT):
                            o = (i % 2) * T + t * P
                            last = nc.tensor.transpose(ps[0:w, b, o:o + P], src(t), ident)
                    last.then_inc(job_rdy, 1)

            def attend(layer, qt, kt, v, dv, softs):
                _, pr, pT = soft(softs)
                diff = layer == 1
                per = 2 if diff else 1
                u0, h0 = 16 * layer, [0, 16, 24][layer]

                def scores(u):
                    if u0 + u >= 4:
                        pe.wait_ge(pre["s"], u0 + u - 3)
                    b = 2 + (u0 + u) % 4
                    q, k = qt(u), kt(u)
                    mm(ps[:, b, 0:P], q[:, 0:P], k[:, 0:P], start=True, stop=True)
                    mm(ps[:, b, P:3 * P], q[:, P:T], k[:, :], start=True, stop=True
                       ).then_inc(pre["sc"], 1)

                def turn(h):
                    if diff:
                        pe.wait_ge(pre["p"], h + 1)
                    else:
                        pe.wait_ge(pre["e"], u0 + h + 1)
                    if h0 + h >= 2:
                        pe.wait_ge(pre["pte"], h0 + h - 1)
                    b = 6 + (h0 + h) % 2
                    for i in range(3):
                        last = nc.tensor.transpose(ps[:, b, i * P:(i + 1) * P],
                                                   pr[:, (per * h) % 4, i * P:(i + 1) * P], ident)
                    last.then_inc(pre["pt"], 1)

                def out(h):
                    pe.wait_ge(pre["pte"], h0 + h + 1)
                    if h0 + h >= 2:
                        pe.wait_ge(pre["ov"], h0 + h - 1)
                    b = (h0 + h) % 2
                    w = pT[:, (h0 + h) % 2, :]
                    mm(ps[:, b, 0:dv], w[:, 0:P], v(0, h), start=True, stop=True)
                    mm(ps[:, b, dv:2 * dv], w[:, P:2 * P], v(0, h), start=True, stop=False)
                    mm(ps[:, b, dv:2 * dv], w[:, 2 * P:3 * P], v(1, h), start=False, stop=True
                       ).then_inc(pre["o"], 1)

                heads = 16 // per
                for u in range(3 * per):
                    scores(u)
                for h in range(heads):
                    turn(h)
                    if h:
                        out(h - 1)
                    for u in range(per * (h + 3), min(per * (h + 4), 16)):
                        scores(u)
                out(heads - 1)

            turn16("n1")
            wait_hT("n1")
            token_jobs(a_at["kvd"], J["kvd"][0], hT2, KT, [KV_LORA + QK_ROPE])
            token_jobs(a_at["qd"], J["qd"][0], hT, KT, [Q_LORA])
            small_turn(J["ckv"][0], m_ckvn, 2, 1)
            pe.wait_ge(job_out, J["ckv"][0] + 1)
            token_jobs(a_at["kvu"], J["kvu"][0], m_ckvT, 2, [512] * 4)
            small_turn(J["cq"][0], m_cqn, 3, 2)
            pe.wait_ge(job_out, J["cq"][0] + 2)
            for s in range(2):
                token_jobs(a_at["qu"] + s, J["qu"][0] + 4 * s, m_cqT, 3, [384, 384])
            pe.wait_ge(job_out, J["qk1"][0])
            pe.wait_ge(pre["src"], 1)
            turn_blocks(J["qk1"][0], [((lambda t, s=s, h=h: s[:, t, h, :]), QD)
                                      for s in (m_q, m_k) for h in range(H)])
            pe.wait_ge(job_out, J["qk1"][0] + 16)
            attend(0, lambda u: m_QT[0:QD, u, :], lambda u: m_KT[0:QD, u, :],
                   lambda t, h: m_v[:, t, h * 64:(h + 1) * 64], 64, m_soft)
            turn16("o1")
            out_proj(1)
            turn16("nf1")
            ffn("ffn1", 1)

            turn16("n2")
            for s in range(6):
                split_jobs(a_at["din"] + s, J["din"][0] + 2 * s, "n2" if s == 0 else None)
            pe.wait_ge(pre["src"], 2)
            pe.wait_ge(hd_rdy, 1)
            turn_blocks(J["qk2"][0], [((lambda t, i=i, k=k: d_p[:, i, t, k * P:(k + 1) * P]), P)
                                      for i in range(2) for k in range(8)])
            pe.wait_ge(job_out, J["qk2"][0] + 8)

            def half(ap, u):
                return ap[64 * (u % 2):64 * (u % 2) + 64, u // 2, :]

            attend(1, lambda u: half(d_QT, u), lambda u: half(d_KT, u),
                   lambda t, h: d_p[:, 2, t, h * P:(h + 1) * P], P, d_soft)
            turn16("o2")
            out_proj(2)
            turn16("nm0")
            ffn("mlp0", 2)

            turn16("n3")
            for s in range(5):
                split_jobs(a_at["sin"] + s, J["sin"][0] + 2 * s, "n3" if s == 0 else None)
            small_turn(J["scq"][0], s_cqn, 2, 3)
            pe.wait_ge(job_out, J["scq"][0] + 1)
            token_jobs(a_at["uq"], J["uq"][0], s_cqT, 2, [512] * 3)
            pe.wait_ge(pre["src"], 3)
            turn_blocks(J["ixt"][0], [((lambda t, k=k: s_qi[:, t, k * P:(k + 1) * P]), P)
                                      for k in range(4)] +
                        [((lambda t: s_ki[:, t, :, :].rearrange("p j n -> p (j n)")), P)])
            pe.wait_ge(job_out, J["ixt"][0] + 3)
            for i in range(IDX_H):
                if i >= 3:
                    pe.wait_ge(pre["ixr"], i - 2)
                b = 3 + i % 3
                q = half(s_QIT, i)
                kx = s_KIT[64 * (i % 2):64 * (i % 2) + 64, :]
                mm(ps[:, b, 0:P], q[:, 0:P], kx[:, 0:P], start=True, stop=True)
                mm(ps[:, b, P:3 * P], q[:, P:T], kx, start=True, stop=True).then_inc(pre["ix"], 1)
            pe.wait_ge(pre["ixr"], 8)
            pe.wait_ge(hd_rdy, 3)
            turn_blocks(J["qk3"][0], [((lambda t, s=s, k=k: s[:, t, k * P:(k + 1) * P]), P)
                                      for s in (s_q, s_p[:, :, 256:1280]) for k in range(8)])
            pe.wait_ge(job_out, J["qk3"][0] + 8)
            attend(2, lambda u: half(s_QT, u), lambda u: half(s_KT, u),
                   lambda t, h: s_p[:, t, 1280 + h * 64:1280 + (h + 1) * 64], 64, s_soft)
            turn16("o3")
            out_proj(3)
            turn16("nm1")
            ffn("mlp1", 2)

        @block.scalar
        def _(act):
            chain = [0]
            A_ = nc.scalar.activation

            def link(ins):
                chain[0] += 1
                ins.then_inc(act_c, 1)
                act.wait_ge(act_c, chain[0])

            eps = con[:, CON["eps"][0]:CON["eps"][0] + 1]
            eps_l = con[:, CON["eps"][0] + 1:CON["eps"][0] + 2]

            def root(name, out, in_, n, e):
                act.wait_ge(ss_rdy, SD[name] + 1)
                if e is None:
                    ins = A_(out, in_, ACT.Sqrt, scale=1.0 / n)
                else:
                    ins = A_(out, in_, ACT.Sqrt, bias=e, scale=1.0 / n)
                ins.then_inc(sd_rdy, 1)

            primed = [56]

            def prime(func):
                A_(st[:, primed[0]:primed[0] + 1], eps, func)
                primed[0] += 1

            def norm(name):
                n = NI[name]
                for t in range(NT):
                    if n:
                        act.wait_ge(x_done, 2 * (n - 1) + t + 1)
                    else:
                        act.wait_ge(x_in, 16)
                    link(A_(xn[:, t, :], x[:, t, :], ACT.Square, accum_out=st[:, t:t + 1]))
                    A_(st[:, 2 + t:3 + t], st[:, t:t + 1], ACT.Sqrt, bias=eps, scale=1.0 / D
                       ).then_inc(rms_rdy, 1)

            def turned(name, gain, gain2=None):
                n = TI[name]
                for k in range(4, 8):
                    act.wait_ge(tp_rdy, 4 * n + k // 2 + 1)
                    src = ps[:, tbank(name, k // 2), (k % 2) * T:(k % 2) * T + T]
                    if gain2:
                        A_(hT2[:, k, :], src, ACT.Copy, scale=col(gain2, k))
                    if gain:
                        A_(hT[:, k, :], src, ACT.Copy, scale=col(gain, k)).then_inc(ha_rdy, 1)
                    else:
                        nc.scalar.copy(hT[:, k, :], src).then_inc(ha_rdy, 1)

            def head_root(name, i):
                root(name, st[:, 192 + 32 * i:224 + 32 * i], st[:, 128 + 32 * i:160 + 32 * i], HD, eps)

            def res_root(mi):
                for t in range(NT):
                    act.wait_ge(m_rdy, 2 * mi + t + 1)
                    link(A_(xn[:, t, :], ps[:, 2 * t:2 * t + 2, :].rearrange("p b n -> p (b n)"),
                            ACT.Square, accum_out=st[:, 8 + t:9 + t]))
                    A_(st[:, 10 + t:11 + t], st[:, 8 + t:9 + t], ACT.Sqrt, bias=eps, scale=1.0 / D
                       ).then_inc(msd_rdy, 1)

            def job(j, *copies):
                act.wait_ge(job_rdy, j + 1)
                for f in copies:
                    last = f(ps[:, bank(j), :])
                last.then_inc(job_out, 1)

            def turned_split(name, gain=None):
                n = TI[name]
                for b in range(4):
                    act.wait_ge(tp_rdy, 4 * n + b + 1)
                    if gain is None:
                        last = nc.scalar.copy(hTh[:, 2 * b:2 * b + 2, :].rearrange("p k t -> p (k t)"),
                                              ps[:, tbank(name, b), :])
                    for k in (2 * b, 2 * b + 1) if gain else ():
                        last = A_(hTh[:, k, :], ps[:, tbank(name, b), (k % 2) * T:(k % 2) * T + T],
                                  ACT.Copy, scale=gcol(gain, k))
                    last.then_inc(ha_rdy, 1)

            def round_slot(a, half):
                act.wait_ge(a_loaded[a % 2], 32 * (a // 2 + 1))
                n = 2 * SPLIT[a] + half
                if n >= 2:
                    act.wait_ge(*a_free[n - 2])
                nc.scalar.copy(k_half(Ah[:, half, :], a, 0), k_half(ringA[:, a % 2, :], a, half)
                               ).then_inc(ah_rdy, 1)

            def round_a(w, ch, par, half):
                a0, g0 = a_at[w], G0[w]
                ap = (a0 + par) % 2
                act.wait_ge(a_loaded[ap], ch * 16 + (32 * ((a0 + par) // 2 + 1) - 16 * par))
                if not isinstance(ch, int) or ch >= 1:
                    act.wait_ge(f1_rdy, ch * 2 + (2 * g0 + half - 1))
                nc.scalar.copy(a_split(w, Ah, half), a_half(w, ap, half)).then_inc(ah_rdy, 1)

            def round_b(w, ch, par, half):
                g0 = G0[w]
                bp, n = (g0 + par) % 2, b_len(w)
                act.wait_ge(b_loaded[bp], ch * 16 + (32 * ((g0 + par) // 2 + 1) - 16 * par))
                if not isinstance(ch, int) or ch >= 1:
                    act.wait_ge(b_used, b_used_at(w, ch + -1, half))
                nc.scalar.copy(Bh[:, half, 0:n], ringB[:, bp, half * n:(half + 1) * n]
                               ).then_inc(bh_rdy, 1)

            def ffn_start(w, half):
                act.wait_ge(*a_free[S0[w] + half - 2])
                round_a(w, 0, 0, half)

            def ffn(w, gelu):
                g0 = G0[w]
                round_b(w, 0, 0, 0)

                def step(ch, par):
                    last = isinstance(ch, int) and ch == NCH[w] - 1
                    for half in range(2):
                        n = ch * 2 + (2 * g0 + half + 1)
                        if not last:
                            round_a(w, ch + 1, 1 - par, half)
                        if gelu:
                            act.wait_ge(gc_rdy, n)
                            A_(ge[:, half, :], gc[:, half, :], ACT.Gelu_apprx_tanh
                               ).then_inc(ge_rdy, 1)
                        else:
                            act.wait_ge(f1_rdy, n)
                            act.wait_ge(h_rdy, n + -2)
                            A_(rl[:, half, :], ps[:, 4 + half, :], ACT.Relu).then_inc(ge_rdy, 1)
                        if half == 0:
                            round_b(w, ch, par, 1)
                        elif not last:
                            round_b(w, ch + 1, 1 - par, 0)

                chunk_walk(act, w, step)

            def feature_copies(j, dst):
                for s in range(4):
                    o = dst[:, 512 * s:512 * s + 512]
                    job(j + s, lambda p, o=o: nc.scalar.copy(o, p))

            def v_copies(j, half):
                for t in range(NT):
                    o = vtok[:, t * D + half * 512:t * D + half * 512 + 512]
                    job(j + t, lambda p, o=o: nc.scalar.copy(o, p))

            act.wait_ge(con_in, 32)
            prime(ACT.Sqrt)
            norm("n0")
            turned("n0", "g0_mix")
            j = J["lora"][0]
            job(j, lambda p: A_(lT[0:LORA, 0:T], p[0:LORA, 0:T], ACT.Tanh),
                lambda p: nc.scalar.copy(lT[0:LORA, T:2 * T], p[0:LORA, T:2 * T]))
            job(j + 1, lambda p: A_(sigg[:, 0:T], p[:, 0:T], ACT.Sigmoid),
                lambda p: A_(sigg[0:GLORA - P, T:2 * T], p[0:GLORA - P, T:2 * T], ACT.Sigmoid))
            feature_copies(J["k"][0], kT_)
            j = J["wz"][0]
            for dst, bias in ((zs, "w0"), (aT, "a0")):
                for s in range(4):
                    job(j, *[lambda p, q=q: A_(fm(dst)[:, 2 * s + q, :], p[:, q * T:(q + 1) * T],
                                               ACT.Sigmoid, bias=col(bias, 2 * s + q))
                             for q in range(2)])
                    j += 1
            act.wait_ge(wk["ang"], 1)
            A_(cs2[:, :, :, :], cs2[:, :, :, :], ACT.Sin).then_inc(wk["cs"], 1)
            feature_copies(J["r"][0], rT)
            for s in range(4):
                job(J["kk"][0] + s, lambda p: A_(xnflat[:, s * 512:(s + 1) * 512], p, ACT.Sqrt))
            v_copies(J["v"][0], 0)
            act.wait_ge(wk["lc"], 1)
            act.wait_ge(wk["kkn"], 1)
            act.wait_ge(wk["rkp"], 1)
            A_(eQ, zs, ACT.Exp).then_inc(wk["exp"], 1)
            A_(eN, Lc, ACT.Exp, scale=-1.0).then_inc(wk["exp"], 1)
            job(J["bonus"][0], lambda p: nc.scalar.copy(bon, p[:, 0:32]))
            A_(eP, Lc, ACT.Exp).then_inc(wk["exp"], 1)
            A_(cl, cl, ACT.Exp).then_inc(wk["exp"], 1)
            v_copies(J["v2"][0], 1)
            j = J["bk"][0]
            for m in range(2):
                for s in range(2):
                    o = btk[:, m, s * 512:(s + 1) * 512]
                    job(j, lambda p, o=o: nc.scalar.copy(o, p))
                    j += 1
            for u, name, e in ORDER:
                if e != "a":
                    continue
                ch, hs = heads_of(u)
                L = lanes[u % 2]
                act.wait_ge(wk["mm"], PE_N[u, name])
                if name == "rhs":
                    for i in range(2):
                        last = nc.scalar.copy(L["R"][:, i * P:(i + 1) * P],
                                              ps[:, lane_bank(u, name, i), 0:P])
                elif name == "y0":
                    last = nc.scalar.copy(L["u0"], ps[:, lane_bank(u, name), 0:T])
                elif name == "Y":
                    for i in range(2):
                        yv = ytok.rearrange("p (c k i v) -> p c k i v", c=2, k=KT, i=2)
                        k = hs[0][1]
                        last = nc.scalar.copy(yv[:, ch, k:k + 2, i, :],
                                              ps[:, lane_bank(u, name, i), 0:P].rearrange(
                                                  "p (k v) -> p k v", k=2))
                else:
                    last = nc.scalar.copy(L[name], ps[:, lane_bank(u, name), :])
                last.then_inc(wk["cpa"], 1)
                if (u, name) == (5, "M2T"):
                    root("lnx0", gs_[:, 32:48], gs_[:, 0:16], HD, eps_l)
            root("lnx1", gs_[:, 48:64], gs_[:, 16:32], HD, eps_l)
            act.wait_ge(xn_rdy, 2 * (XN["o0"] + 1))
            for half in range(2):
                round_slot(a_at["wo0"], half)
            turned_split("o0")
            for half in range(2):
                round_slot(a_at["wo0"] + 1, half)
            ffn_start("ffn0", 0)
            res_root(0)
            norm("nf0")
            turned_split("nf0", "g0_ffn")
            ffn_start("ffn0", 1)
            ffn("ffn0", True)
            prime(ACT.Sqrt)
            res_root(1)

            def attend(layer, softs):
                s_, pr, pT = soft(softs)
                diff = layer == 1
                per = 2 if diff else 1
                u0, h0 = 16 * layer, [0, 16, 24][layer]

                def turned_p(h):
                    act.wait_ge(pre["pt"], h0 + h + 1)
                    nc.scalar.copy(pT[:, (h0 + h) % 2, :], ps[:, 6 + (h0 + h) % 2, 0:384]
                                   ).then_inc(pre["pte"], 1)

                def squares(h):
                    act.wait_ge(pre["ov"], h0 + h + 1)
                    for t in range(NT):
                        o = (8 * t + h) * P
                        ins = A_(d_sq[:, o:o + P], xn[:, t, h * P:(h + 1) * P], ACT.Square,
                                 accum_out=st[:, 24 + 8 * t + h:25 + 8 * t + h])
                    return ins

                for u in range(16):
                    if layer == 0 and u in (3, 7):
                        round_slot(a_at["wo1"], u // 4)
                    act.wait_ge(pre["s"], u0 + u + 1)
                    nm = st[:, 64 + 2 * u:66 + 2 * u]
                    sm = st[:, 96 + 2 * u:98 + 2 * u]
                    i = u % 4
                    A_(pr[:, i, 0:P], s_[:, (u0 + u) % 3, 0:P], ACT.Exp, bias=nm[:, 0:1],
                       accum_out=sm[:, 0:1])
                    A_(pr[:, i, P:384], s_[:, (u0 + u) % 3, P:384], ACT.Exp, bias=nm[:, 1:2],
                       accum_out=sm[:, 1:2]).then_inc(pre["e"], 1)
                    if diff and u % 2 and u >= 3:
                        turned_p(u // 2 - 1)
                        if u >= 9:
                            squares(u // 2 - 4)
                    if not diff and u:
                        turned_p(u - 1)
                turned_p(16 // per - 1)
                prime(ACT.Sqrt)
                if diff:
                    for h in range(4, 8):
                        ins = squares(h)
                    link(ins)

            norm("n1")
            turned("n1", "g1_mix", "g_kv")
            j = J["kvd"][0]
            for t in range(NT):
                job(j + t, lambda p: nc.scalar.copy(m_down[:, t, :], p[:, 0:288]))
            root("ckv", st[:, 18:20], st[:, 16:18], KV_LORA, eps)
            for t in range(NT):
                job(J["qd"][0] + t, lambda p: nc.scalar.copy(m_qd[:, t, :], p[:, 0:Q_LORA]))
            j = J["ckv"][0]
            job(j, *[lambda p, k=k: A_(m_ckvT[:, k, :], p[:, k * T:(k + 1) * T], ACT.Copy,
                                       scale=col("kv_a", k)) for k in range(2)])
            root("cq", st[:, 22:24], st[:, 20:22], Q_LORA, eps)
            j = J["kvu"][0]
            for q in range(4):
                for t in range(NT):
                    def kpart(p):
                        return nc.scalar.copy(m_k[:, t, 4 * q:4 * q + 4, 0:64],
                                              p.rearrange("p (h n) -> p h n", h=4)[:, :, 0:64])

                    def vpart(p):
                        return nc.scalar.copy(
                            m_v[:, t, q * 256:(q + 1) * 256].rearrange("p (h n) -> p h n", h=4),
                            p.rearrange("p (h n) -> p h n", h=4)[:, :, 64:128])
                    job(j, kpart, vpart)
                    j += 1
            j = J["cq"][0]
            job(j, *[lambda p, k=k: A_(m_cqT[:, k, :], p[:, k * T:(k + 1) * T], ACT.Copy,
                                       scale=col("q_n", k)) for k in range(2)])
            job(j + 1, lambda p: A_(m_cqT[:, 2, :], p[:, 0:T], ACT.Copy, scale=col("q_n", 2)))
            j = J["qu"][0]
            for q in range(4):
                for t in range(NT):
                    job(j, lambda p: nc.scalar.copy(m_q[:, t, 4 * q:4 * q + 4, :],
                                                    p[:, 0:384].rearrange("p (h n) -> p h n", h=4)))
                    j += 1
            prime(ACT.Exp)
            j = J["qk1"][0]
            for dst in (m_QT, m_KT):
                for s in range(8):
                    job(j, lambda p: nc.scalar.copy(
                        dst[0:QD, 2 * s:2 * s + 2, :].rearrange("p h t -> p (h t)"), p[0:QD, :]))
                    j += 1
            attend(0, m_soft)
            turned_split("o1")
            for half in range(2):
                round_slot(a_at["wo1"] + 1, half)
            ffn_start("ffn1", 0)
            res_root(2)
            norm("nf1")
            turned_split("nf1", "g1_ffn")
            ffn_start("ffn1", 1)
            ffn("ffn1", True)
            prime(ACT.Sqrt)
            round_slot(a_at["din"], 0)
            res_root(3)

            norm("n2")
            turned_split("n2", "n0_mix")
            round_slot(a_at["din"], 1)
            j = J["din"][0]
            for s in range(6):
                a = a_at["din"] + s + 1
                round_slot(a, 0)
                if s == 2:
                    head_root("dq", 0)
                elif s == 4:
                    head_root("dk", 1)
                for t in range(NT):
                    job(j, lambda p: nc.scalar.copy(
                        d_p[:, s // 2, t, (s % 2) * 512:(s % 2) * 512 + 512], p))
                    j += 1
                round_slot(a, 1)
            act.wait_ge(pre["src2"], 1)
            A_(d_lam[:, 2:4], d_lam[:, 0:2], ACT.Exp).then_inc(pre["osd"], 1)
            j = J["qk2"][0]
            for dst in (d_QT, d_KT):
                for s in range(4):
                    job(j, lambda p: nc.scalar.copy(
                        dst[:, 2 * s:2 * s + 2, :].rearrange("p h t -> p (h t)"), p))
                    j += 1
            attend(1, d_soft)
            A_(st[:, 40:56], st[:, 24:40], ACT.Sqrt, bias=eps, scale=0.5 / HD).then_inc(pre["osd"], 1)
            turned_split("o2", "sub")
            for half in range(2):
                round_slot(a_at["wo2"] + 1, half)
            ffn_start("mlp0", 0)
            norm("nm0")
            turned_split("nm0", "n0_mlp")
            ffn_start("mlp0", 1)
            ffn("mlp0", False)
            prime(ACT.Sqrt)
            round_slot(a_at["sin"], 0)

            norm("n3")
            turned_split("n3", "n1_mix")
            round_slot(a_at["sin"], 1)
            j = J["sin"][0]
            for s in range(5):
                w = min(512, DSA_IN - 512 * s)
                if s < 4:
                    round_slot(a_at["sin"] + s + 1, 0)
                if s == 3:
                    head_root("sk", 1)
                for t in range(NT):
                    job(j, lambda p: nc.scalar.copy(s_p[:, t, s * 512:s * 512 + w], p[:, 0:w]))
                    j += 1
                if s < 4:
                    round_slot(a_at["sin"] + s + 1, 1)
                if s == 0:
                    root("scq", st[:, 18:20], st[:, 16:18], DSA_Q, eps)
            job(J["scq"][0], *[lambda p, k=k: A_(s_cqT[:, k, :], p[:, k * T:(k + 1) * T], ACT.Copy,
                                                 scale=col("cq_n", k)) for k in range(2)])
            root("kidx", st[:, 22:24], st[:, 20:22], 64, eps)
            j = J["uq"][0]
            for q in range(3):
                for t in range(NT):
                    dst = s_q[:, t, q * 512:(q + 1) * 512] if q < 2 else s_qi[:, t, :]
                    job(j, lambda p: nc.scalar.copy(dst, p))
                    j += 1
            head_root("sq", 0)
            for half in range(2):
                round_slot(a_at["wo3"], half)
            j = J["ixt"][0]
            for s in range(2):
                job(j, lambda p: nc.scalar.copy(
                    s_QIT[:, 2 * s:2 * s + 2, :].rearrange("p h t -> p (h t)"), p))
                j += 1
            job(j, lambda p: nc.scalar.copy(s_KIT, p[:, 0:T]))
            for i in range(IDX_H):
                act.wait_ge(pre["ix"], i + 1)
                if i >= 2:
                    act.wait_ge(pre["ixs"], i - 1)
                A_(s_ixr[:, i % 2, :], ps[:, 3 + i % 3, 0:384], ACT.Relu).then_inc(pre["ixr"], 1)
            j = J["qk3"][0]
            for dst in (s_QT, s_KT):
                for s in range(4):
                    job(j, lambda p: nc.scalar.copy(
                        dst[:, 2 * s:2 * s + 2, :].rearrange("p h t -> p (h t)"), p))
                    j += 1
            attend(2, s_soft)
            turned_split("o3")
            for half in range(2):
                round_slot(a_at["wo3"] + 1, half)
            ffn_start("mlp1", 0)
            norm("nm1")
            turned_split("nm1", "n1_mlp")
            ffn_start("mlp1", 1)
            ffn("mlp1", False)

        @block.gpsimd
        def _(pool):
            chain = [0]
            G = nc.gpsimd

            def link(ins):
                chain[0] += 1
                ins.then_inc(pool_c, 1)
                pool.wait_ge(pool_c, chain[0])

            def heads(src, gain, tmp, inv=None):
                x4 = src.rearrange("p t (h n) -> p t h n", h=H)
                if inv is not None:
                    for t in range(NT):
                        ins = G.tensor_tensor(x4[:, t], x4[:, t],
                                              bc(inv[:, 16 * t:16 * t + 16], 2, 64), ALU.mult)
                    link(ins)
                for t in range(NT):
                    ins = G.tensor_tensor(x4[:, t], x4[:, t], bc(row(gain), 1, H), ALU.mult)
                link(ins)
                for t in range(NT):
                    x1, x2 = x4[:, t, :, 0:8], x4[:, t, :, 8:16]
                    cos, sin = bc(cs2[:, 0, t, :], 1, H), bc(cs2[:, 1, t, :], 1, H)
                    tm = [tmp[:, i * 128:(i + 1) * 128].rearrange("p (h n) -> p h n", h=H)
                          for i in range(4)]
                    G.tensor_tensor(tm[0], x1, cos, ALU.mult)
                    G.tensor_tensor(tm[1], x2, sin, ALU.mult)
                    G.tensor_tensor(tm[2], x1, sin, ALU.mult)
                    link(G.tensor_tensor(tm[3], x2, cos, ALU.mult))
                    G.tensor_tensor(x1, tm[0], tm[1], ALU.subtract)
                    ins = G.tensor_tensor(x2, tm[2], tm[3], ALU.add)
                    if t == 0:
                        link(ins)
                ins.then_inc(hd_rdy, 1)

            def rest_slot(a, half):
                n = 2 * SPLIT[a] + half
                pool.wait_ge(al_rdy, n)
                pool.wait_ge(ah_rdy, n + 1)
                G.tensor_tensor(k_half(Al[:, half, :], a, 0), k_half(ringA[:, a % 2, :], a, half),
                                k_half(Ah[:, half, :], a, 0).bitcast(F32), ALU.subtract
                                ).then_inc(al_rdy, 1)

            pool.wait_ge(wk["cs"], 1)
            for half in range(2):
                rest_slot(a_at["wo1"], half)
            pool.wait_ge(hd_go, 1)
            heads(d_p[:, 0], "dq", d_rt[:, 512:1024])
            for half in range(2):
                rest_slot(a_at["wo2"], half)
            pool.wait_ge(hd_go, 2)
            heads(s_p[:, :, 256:1280], "sk", s_rtp)
            pool.wait_ge(hd_go, 3)
            heads(s_q, "sq", s_rtp, inv=st[:, 128:160])
            for half in range(2):
                rest_slot(a_at["wo3"], half)

        @block.vector
        def _(dve):
            chain = [0]
            V = nc.vector

            def link(ins):
                chain[0] += 1
                ins.then_inc(dve_c, 1)
                dve.wait_ge(dve_c, chain[0])

            def norm(name, tiles=range(NT)):
                for t in tiles:
                    dve.wait_ge(rms_rdy, 2 * NI[name] + t + 1)
                    link(V.reciprocal(st[:, 4 + t:5 + t], st[:, 2 + t:3 + t]))
                    V.tensor_scalar(diag[:, t, :], ident, st[:, 4 + t:5 + t], None, ALU.mult
                                    ).then_inc(xn_rdy, 1)

            def turned(name, gain, gain2=None):
                n = TI[name]
                for k in range(4):
                    dve.wait_ge(tp_rdy, 4 * n + k // 2 + 1)
                    src = ps[:, tbank(name, k // 2), (k % 2) * T:(k % 2) * T + T]
                    if gain2:
                        V.tensor_scalar(hT2[:, k, :], src, col(gain2, k), None, ALU.mult)
                    if gain:
                        ins = V.tensor_scalar(hT[:, k, :], src, col(gain, k), None, ALU.mult)
                    else:
                        ins = V.tensor_copy(hT[:, k, :], src)
                    ins.then_inc(hv_rdy, 1)

            def mview(t):
                return ps[:, 2 * t:2 * t + 2, :].rearrange("p b n -> p (b n)")

            def res_norm(mi, gain, following):
                for t in range(NT):
                    dve.wait_ge(msd_rdy, 2 * mi + t + 1)
                    link(V.reciprocal(st[:, 12 + t:13 + t], st[:, 10 + t:11 + t]))
                    link(V.scalar_tensor_tensor(xn[:, t, :], mview(t), st[:, 12 + t:13 + t], row(gain),
                                                ALU.mult, ALU.mult))
                    if t == 1:
                        norm(following, [0])
                    V.tensor_tensor(x[:, t, :], x[:, t, :], xn[:, t, :], ALU.add).then_inc(x_done, 1)
                dve.wait_ge(x_done, 2 * mi + 2)

            def res_plain(mi):
                for t in range(NT):
                    dve.wait_ge(m_rdy, 2 * mi + t + 1)
                    V.tensor_tensor(x[:, t, :], x[:, t, :], mview(t), ALU.add).then_inc(x_done, 1)
                dve.wait_ge(x_done, 2 * mi + 2)

            def turned_split(name, gain=None):
                n = TI[name]
                for b in range(4):
                    dve.wait_ge(ha_rdy, 4 * n + b + 1)
                    if gain is None:
                        last = V.tensor_tensor(
                            hTl[:, 2 * b:2 * b + 2, :].rearrange("p k t -> p (k t)"),
                            ps[:, tbank(name, b), :],
                            hTh[:, 2 * b:2 * b + 2, :].rearrange("p k t -> p (k t)").bitcast(F32),
                            ALU.subtract)
                    for k in (2 * b, 2 * b + 1) if gain else ():
                        last = V.scalar_tensor_tensor(
                            hTl[:, k, :], ps[:, tbank(name, b), (k % 2) * T:(k % 2) * T + T],
                            gcol(gain, k), hTh[:, k, :].bitcast(F32), ALU.mult, ALU.subtract)
                    last.then_inc(hv_rdy, 1)

            def rest_slot(a, half):
                dve.wait_ge(ah_rdy, 2 * SPLIT[a] + half + 1)
                V.tensor_tensor(k_half(Al[:, half, :], a, 0), k_half(ringA[:, a % 2, :], a, half),
                                k_half(Ah[:, half, :], a, 0).bitcast(F32), ALU.subtract
                                ).then_inc(al_rdy, 1)

            def rest_a(w, ch, par, half):
                dve.wait_ge(ah_rdy, ch * 2 + (S0[w] + half + 1))
                V.tensor_tensor(a_split(w, Al, half), a_half(w, (a_at[w] + par) % 2, half),
                                a_split(w, Ah, half).bitcast(F32), ALU.subtract).then_inc(al_rdy, 1)

            def rest_b(w, ch, par, half):
                n = b_len(w)
                dve.wait_ge(bh_rdy, ch * 2 + (2 * G0[w] + half + 1))
                V.tensor_tensor(Bl[:, half, 0:n], ringB[:, (G0[w] + par) % 2, half * n:(half + 1) * n],
                                Bh[:, half, 0:n].bitcast(F32), ALU.subtract).then_inc(bl_rdy, 1)

            def ffn_start(w, half):
                rest_a(w, 0, 0, half)

            def ffn(w, layer=None):
                g0 = G0[w]
                F = DFF // P
                rest_b(w, 0, 0, 0)

                def conv(ch, half):
                    cw, cb = "conv_w%d" % layer, "conv_b%d" % layer
                    f = ch * 2 + half
                    gate, o = ps[:, 4 + half, 0:T], gc[:, half, :]
                    n = ch * 4 + (4 * g0 + 2 * half + 1)
                    dve.wait_ge(f1_rdy, ch * 2 + (2 * g0 + half + 1))
                    V.tensor_scalar(o, gate, colx(cw, f + 2 * F), colx(cb, f), ALU.mult, ALU.add
                                    ).then_inc(wk["cv"], 1)
                    dve.wait_ge(wk["cv"], n)
                    V.scalar_tensor_tensor(o[:, 1:T], gate[:, 0:T - 1], colx(cw, f + F), o[:, 1:T],
                                           ALU.mult, ALU.add).then_inc(wk["cv"], 1)
                    dve.wait_ge(wk["cv"], n + 1)
                    V.scalar_tensor_tensor(o[:, 2:T], gate[:, 0:T - 2], colx(cw, f), o[:, 2:T],
                                           ALU.mult, ALU.add).then_inc(gc_rdy, 1)

                def step(ch, par):
                    last = isinstance(ch, int) and ch == NCH[w] - 1
                    for half in range(2):
                        if layer is not None:
                            conv(ch, half)
                        if not last:
                            rest_a(w, ch + 1, 1 - par, half)
                        n = ch * 2 + (2 * g0 + half + 1)
                        m = ch * 4 + (4 * g0 + 2 * half + 1)
                        dve.wait_ge(ge_rdy, n)
                        if not isinstance(ch, int) or n >= 2:
                            dve.wait_ge(h_rdy, n + -1)
                        if layer is None:
                            wid = 2 * T
                            V.tensor_tensor(ht, rl[:, half, :], rl[:, half, :], ALU.mult
                                            ).then_inc(ht_rdy, 1)
                        else:
                            wid = T
                            V.tensor_tensor(ht[:, 0:T], ge[:, half, :], ps[:, 4 + half, T:2 * T],
                                            ALU.mult).then_inc(ht_rdy, 1)
                        if not isinstance(ch, int) or ch >= 1:
                            dve.wait_ge(b_used, b_used_at(w, ch + -1, half))
                        dve.wait_ge(ht_rdy, m)
                        V.tensor_copy(hidh[:, half, 0:wid], ht[:, 0:wid]).then_inc(ht_rdy, 1)
                        dve.wait_ge(ht_rdy, m + 1)
                        V.tensor_tensor(hidl[:, half, 0:wid], ht[:, 0:wid],
                                        hidh[:, half, 0:wid].bitcast(F32), ALU.subtract
                                        ).then_inc(h_rdy, 1)
                        if half == 0:
                            rest_b(w, ch, par, 1)
                        elif not last:
                            rest_b(w, ch + 1, 1 - par, 0)

                chunk_walk(dve, w, step)

            dve.wait_ge(con_in, 32)
            norm("n0")
            turned("n0", "g0_mix")
            dve.wait_ge(hv_rdy, 4)
            dve.wait_ge(ha_rdy, 4)
            xf = fm(xx)
            V.tensor_scalar(xf[:, :, 0:1], hT[:, :, 0:1], -1.0, None, ALU.mult)
            link(V.tensor_tensor(xf[:, :, 1:T], hT[:, :, 0:T - 1], hT[:, :, 1:T], ALU.subtract))
            for n_, (i, buf) in enumerate(MIXES):
                if n_ == 5:
                    dve.wait_ge(job_rdy, J["lora"][0] + 1)
                for k in range(KT):
                    last = V.scalar_tensor_tensor(fm(buf)[:, k, :], xf[:, k, :],
                                                  col("mu", 8 * i + k), hT[:, k, :],
                                                  ALU.mult, ALU.add)
                last.then_inc(xs_rdy, 1)
            dve.wait_ge(const_in, 16 * 7)
            inv = con[:, CON["inv2"][0]:CON["inv2"][0] + 8]
            posf, ang = gs_[:, 0:2], st[:, 128:144].rearrange("p (t n) -> p t n", t=2)
            cnt = st[:, 144:176].rearrange("p (j t n) -> p j t n", j=2, t=2)
            link(V.tensor_copy(posf, posi[:, :]))
            for t in range(NT):
                ins = V.tensor_scalar(ang[:, t, :], inv, posf[:, t:t + 1], None, ALU.mult)
            link(ins)
            V.tensor_scalar(cnt[:, 0], ang, 1.0 / (2 * math.pi), 0.25, ALU.mult, ALU.add)
            link(V.tensor_scalar(cnt[:, 1], ang, 1.0 / (2 * math.pi), None, ALU.mult))
            link(V.tensor_scalar(cnt, cnt, MAGIC, None, ALU.add))
            link(V.tensor_scalar(cnt, cnt, -MAGIC, None, ALU.add))
            for j in range(2):
                ins = V.scalar_tensor_tensor(cs2[:, j], cnt[:, j], -TWO_PI[0], ang, ALU.mult, ALU.add)
            link(ins)
            link(V.scalar_tensor_tensor(cs2[:, :, :, :].rearrange("p j t n -> p (j t n)"),
                                        st[:, 144:176], -TWO_PI[1],
                                        cs2[:, :, :, :].rearrange("p j t n -> p (j t n)"),
                                        ALU.mult, ALU.add))
            link(V.scalar_tensor_tensor(cs2[:, :, :, :].rearrange("p j t n -> p (j t n)"),
                                        st[:, 144:176], -TWO_PI[2],
                                        cs2[:, :, :, :].rearrange("p j t n -> p (j t n)"),
                                        ALU.mult, ALU.add))
            link(V.tensor_scalar(cs2[:, 0], cs2[:, 0], math.pi / 2, None, ALU.add))
            V.tensor_scalar(cs2[:, :, :, :], cs2[:, :, :, :], 3.1415925, -3.1415925, ALU.min, ALU.max
                            ).then_inc(wk["ang"], 1)

            dve.wait_ge(job_out, J["k"][0] + 4)
            for k in range(KT):
                ins = V.tensor_scalar(fm(kkb)[:, k, :], fm(kT_)[:, k, :], col("k_k", k), None, ALU.mult)
            link(ins)
            V.tensor_tensor(xnflat, kkb, kkb, ALU.mult).then_inc(wk["sq"], 1)
            dve.wait_ge(job_out, J["wz"][0] + 4)
            link(V.tensor_scalar(zs, zs, -E05, None, ALU.mult))
            ones = cst("ones")
            for s in range(2 * KT):
                ins = V.tensor_tensor_scan(Lc[:, s * P:(s + 1) * P], ones, zs[:, s * P:(s + 1) * P],
                                           0.0, ALU.mult, ALU.add)
            link(ins)
            L3 = Lc.rearrange("p (s t) -> p s t", t=P)
            link(V.tensor_copy(lm, L3[:, :, P // 2 - 1]))
            link(V.tensor_tensor(L3, L3, bc(lm, 2, P), ALU.subtract))
            V.tensor_tensor(zs, Lc, zs, ALU.subtract)
            lms = lm.rearrange("p (k c) -> p k c", c=2)
            L4 = Lc.rearrange("p (k c t) -> p k c t", c=2, t=P)
            V.tensor_tensor(cl, L4[:, :, 0, P - 1], lms[:, :, 1], ALU.add).then_inc(wk["lc"], 1)
            dve.wait_ge(job_out, J["az"][0] + 4)
            for k in range(KT):
                ins = V.tensor_scalar(fm(k2)[:, k, :], fm(aT)[:, k, :], 1.0, col("k_a", k),
                                      ALU.subtract, ALU.mult)
            link(ins)
            link(V.scalar_tensor_tensor(k2, k2, 1.0, kT_, ALU.add, ALU.mult))
            dve.wait_ge(job_out, J["r"][0] + 4)
            for k in range(KT):
                last = V.scalar_tensor_tensor(hT[:, k, :], fm(rT)[:, k, :], col("r_k", k),
                                              fm(k2)[:, k, :], ALU.mult, ALU.mult)
            last.then_inc(wk["rkp"], 1)
            dve.wait_ge(job_out, J["kk"][0] + 4)
            link(V.tensor_scalar(xnflat, xnflat, 1e-12, None, ALU.max))
            link(V.reciprocal(xnflat, xnflat))
            V.tensor_tensor(kkb, kkb, xnflat, ALU.mult).then_inc(wk["kkn"], 1)
            dve.wait_ge(wk["kkn"], 1)
            dve.wait_ge(wk["exp"], 1)
            a5 = AR[:, :, :, 0, :]
            r5 = AR[:, :, :, 1, :]

            def v4(ap):
                return ap.rearrange("p (k c t) -> p k c t", c=2, t=P)

            for c_ in range(2):
                V.scalar_tensor_tensor(a5[:, :, c_, :], v4(kkb)[:, :, c_, :], -1.0, v4(eQ)[:, :, c_, :],
                                       ALU.mult, ALU.mult)
            link(V.tensor_tensor(aT, aT, kkb, ALU.mult))
            dve.wait_ge(wk["exp"], 2)
            V.tensor_tensor(aT, aT, eN, ALU.mult)
            V.tensor_tensor(k2, k2, eN, ALU.mult)
            dve.wait_ge(wk["exp"], 4)
            for c_ in range(2):
                last = V.tensor_tensor(r5[:, :, c_, :], v4(rT)[:, :, c_, :], v4(eP)[:, :, c_, :],
                                       ALU.mult)
            last.then_inc(wk["ops"], 1)
            dve.wait_ge(wk["ops"], 1)
            for n_, L in enumerate(lanes):
                if n_ == 1:
                    dve.wait_ge(job_rdy, J["v2"][0] + 2)
                for buf in ("NdT", "rb", "ak", "rk", "Nd", "No"):
                    last = V.memset(L[buf], 0.0)
            last.then_inc(wk["clr"], 1)
            dve.wait_ge(wk["clr"], 1)

            def h4(ap, i):
                return ap.rearrange("p (q t) -> p q t", q=4)[:, 2 * i:2 * i + 2, :]

            yt = ytok.rearrange("p (t n) -> p t n", t=2)

            def group_norm(t, part):
                y1, x1 = yt[:, t, :], xn[:, t, :]
                y3 = y1.rearrange("p (g v) -> p g v", v=64)
                x3 = x1.rearrange("p (g v) -> p g v", v=64)
                v3 = vtok[:, t * D:(t + 1) * D].rearrange("p (g v) -> p g v", v=64)
                g, gr = gs_[:, 16 * t:16 * t + 16], gs_[:, 32 + 16 * t:48 + 16 * t]
                if part == 0:
                    link(V.tensor_reduce(g, y3, AX_X, ALU.add))
                    link(V.tensor_scalar(g, g, 1.0 / HD, None, ALU.mult))
                elif part == 1:
                    link(V.tensor_tensor(y3, y3, bc(g, 2, 64), ALU.subtract))
                elif part == 2:
                    link(V.tensor_tensor(x1, y1, y1, ALU.mult))
                elif part == 3:
                    V.tensor_reduce(g, x3, AX_X, ALU.add).then_inc(ss_rdy, 1)
                elif part == 4:
                    dve.wait_ge(sd_rdy, SD["lnx%d" % t] + 1)
                    link(V.reciprocal(g, gr))
                    link(V.tensor_tensor(y3, y3, bc(g, 2, 64), ALU.mult))
                elif part == 5:
                    link(V.tensor_tensor(y1, y1, row("lnx_w"), ALU.mult))
                elif part == 6:
                    V.tensor_tensor(x3, v3, bc(bon[:, 16 * t:16 * t + 16], 2, 64), ALU.mult)
                elif part == 7:
                    link(V.tensor_tensor(y1, y1, row("lnx_b"), ALU.add))
                else:
                    link(V.tensor_tensor(y1, y1, x1, ALU.add))

            GN_AT = {(5, "E2"): 0, (5, "E3"): 1, (5, "E4"): 2, (5, "MT"): 3, (5, "M4T"): 4,
                     (5, "y1"): 5, (5, "y2"): 6, (7, "E2"): 7, (7, "E3"): 8}
            for u, name, e in ORDER:
                if e != "v":
                    continue
                ch, hs = heads_of(u)
                L = lanes[u % 2]
                dve.wait_ge(wk["mm"], PE_N[u, name])
                if name in ("sb", "sk"):
                    for i in range(2):
                        p4 = ps[:, lane_bank(u, name, i), :].rearrange("p (q j t) -> p q j t", q=2, j=2)
                        for j, (dst, m) in enumerate((("NdT", "dstrict"), ("rb", "incl"))
                                                     if name == "sb" else
                                                     (("ak", "strict"), ("rk", "incl"))):
                            last = V.copy_predicated(h4(L[dst], i), bc(mask(m), 1, 2), p4[:, :, j, :])
                elif name == "sn":
                    for i in range(2):
                        p4 = ps[:, lane_bank(u, name, i), 0:T].rearrange("p (q t) -> p q t", q=2)
                        V.copy_predicated(h4(L["Nd"], i), bc(mask("dlow"), 1, 2), p4)
                        V.copy_predicated(h4(L["No"], i), bc(mask("olow"), 1, 2), p4)
                    last = V.tensor_tensor(L["E"].rearrange("p (q t) -> p q t", q=4),
                                           L["NdT"].rearrange("p (q t) -> p q t", q=4),
                                           bc(ident, 1, 4), ALU.add)
                elif name in ("E2", "E3", "E4"):
                    last = V.tensor_tensor(L["E"], L["E"], ps[:, lane_bank(u, name), :], ALU.add)
                elif name in ("MT", "M4T"):
                    last = V.tensor_copy(L[name], ps[:, lane_bank(u, name), :])
                elif name in ("y1", "y2", "U"):
                    src, dst = ("u1", "u0") if name == "y2" else ("u0", "u1")
                    last = V.tensor_tensor(L[dst], L[src], ps[:, lane_bank(u, name), 0:T], ALU.add)
                else:
                    b = lane_bank(u, name)
                    for q in range(2):
                        k = hs[q][1]
                        for p0 in (0, 64):
                            o = q * P + p0
                            last = V.tensor_scalar(Sst[p0:p0 + 64, k, :], ps[p0:p0 + 64, b, o:o + 64],
                                                   cl[p0:p0 + 64, k:k + 1], None, ALU.mult)
                last.then_inc(wk["cpv"], 1)
                if (u, name) in GN_AT:
                    if GN_AT[u, name] == 0:
                        dve.wait_ge(*EV_N[3, "Y"])
                    group_norm(0, GN_AT[u, name])

            dve.wait_ge(*EV_N[7, "Y"])
            for part in range(9):
                group_norm(1, part)
            dve.wait_ge(wk["g"], 1)
            for t in range(NT):
                V.tensor_tensor(xn[:, t, :], yt[:, t, :], mview(t), ALU.mult).then_inc(xn_rdy, 1)
            for half in range(2):
                rest_slot(a_at["wo0"], half)
            turned_split("o0")
            for half in range(2):
                rest_slot(a_at["wo0"] + 1, half)
            res_norm(0, "g0_res", "nf0")
            norm("nf0", [1])
            ffn_start("ffn0", 0)
            turned_split("nf0", "g0_ffn")
            ffn_start("ffn0", 1)
            ffn("ffn0", 0)
            res_norm(1, "g0_fres", "n1")

            def attend(layer, dv, softs, scale, add):
                s_, pr, _ = soft(softs)
                diff = layer == 1
                u0, h0 = 16 * layer, [0, 16, 24][layer]

                def out(h):
                    dve.wait_ge(pre["o"], h0 + h + 1)
                    b = (h0 + h) % 2
                    for t in range(NT):
                        dst = xn[:, t, h * dv:(h + 1) * dv]
                        src = ps[:, b, t * dv:(t + 1) * dv]
                        if diff:
                            ins = V.tensor_copy(dst, src)
                        else:
                            ins = V.tensor_scalar(dst, src, st[:, 128 + 2 * h + t:129 + 2 * h + t],
                                                  None, ALU.mult)
                    ins.then_inc(pre["ov"], 1)

                def combine(h):
                    u = 2 * h
                    dve.wait_ge(pre["e"], u0 + u + 2)
                    r = st[:, 128 + 4 * h:132 + 4 * h]
                    link(V.reciprocal(r, st[:, 96 + 2 * u:100 + 2 * u]))
                    V.tensor_scalar(pr[:, u % 4, 0:P], pr[:, u % 4, 0:P], r[:, 0:1], None, ALU.mult)
                    V.tensor_scalar(pr[:, u % 4, P:384], pr[:, u % 4, P:384], r[:, 1:2], None, ALU.mult)
                    link(V.tensor_scalar(r[:, 2:4], r[:, 2:4], d_lam[:, 5:6], None, ALU.mult))
                    V.scalar_tensor_tensor(pr[:, u % 4, 0:P], pr[:, u % 4 + 1, 0:P], r[:, 2:3],
                                           pr[:, u % 4, 0:P], ALU.mult, ALU.add)
                    V.scalar_tensor_tensor(pr[:, u % 4, P:384], pr[:, u % 4 + 1, P:384], r[:, 3:4],
                                           pr[:, u % 4, P:384], ALU.mult, ALU.add
                                           ).then_inc(pre["p"], 1)

                for u in range(16):
                    dve.wait_ge(pre["sc"], u0 + u + 1)
                    if u >= 3:
                        dve.wait_ge(pre["e"], u0 + u - 2)
                    s1 = s_[:, (u0 + u) % 3, :]
                    link(V.scalar_tensor_tensor(s1, ps[:, 2 + (u0 + u) % 4, 0:384], scale, add,
                                                ALU.mult, ALU.add))
                    V.tensor_reduce(st[:, 64 + 2 * u:65 + 2 * u], s1[:, 0:P], AX_X, ALU.max,
                                    negate=True)
                    V.tensor_reduce(st[:, 65 + 2 * u:66 + 2 * u], s1[:, P:384], AX_X, ALU.max,
                                    negate=True).then_inc(pre["s"], 1)
                    if diff:
                        if u % 2 and u >= 3:
                            combine(u // 2 - 1)
                            if u >= 7:
                                out(u // 2 - 3)
                    elif u >= 2:
                        h = u - 2
                        dve.wait_ge(pre["e"], u0 + h + 1)
                        link(V.reciprocal(st[:, 128 + 2 * h:130 + 2 * h], st[:, 96 + 2 * h:98 + 2 * h]))
                        if h:
                            out(h - 1)
                if diff:
                    combine(7)
                    out(5)
                    out(6)
                    out(7)
                else:
                    for h in (14, 15):
                        dve.wait_ge(pre["e"], u0 + h + 1)
                        link(V.reciprocal(st[:, 128 + 2 * h:130 + 2 * h], st[:, 96 + 2 * h:98 + 2 * h]))
                        out(h - 1)
                    out(15)
                dve.wait_ge(pre["ov"], h0 + 16 // (2 if diff else 1))

            def rms_tiles(name, src, n, at, dst, scale=None):
                for t in range(NT):
                    ins = V.tensor_tensor_reduce(dst[:, t, :], src[:, t, :], src[:, t, :], 1.0, 0.0,
                                                 ALU.mult, ALU.add, st[:, at + t:at + t + 1])
                ins.then_inc(ss_rdy, 1)
                dve.wait_ge(sd_rdy, SD[name] + 1)
                link(V.reciprocal(st[:, at:at + 2], st[:, at + 2:at + 4]))
                for t in range(NT):
                    ins = V.tensor_scalar(dst[:, t, :], src[:, t, :], st[:, at + t:at + t + 1], None,
                                          ALU.mult)
                return ins

            def rotate(x1, x2, cos, sin, tmp, last=False):
                V.tensor_tensor(tmp[0], x1, cos, ALU.mult)
                V.tensor_tensor(tmp[1], x2, sin, ALU.mult)
                V.tensor_tensor(tmp[2], x1, sin, ALU.mult)
                link(V.tensor_tensor(tmp[3], x2, cos, ALU.mult))
                V.tensor_tensor(x1, tmp[0], tmp[1], ALU.subtract)
                ins = V.tensor_tensor(x2, tmp[2], tmp[3], ALU.add)
                if last:
                    ins.then_inc(pre["src"], 1)
                else:
                    link(ins)

            def quarters(buf, h, n):
                return [buf[:, i * h * n:(i + 1) * h * n].rearrange("p (h n) -> p h n", h=h)
                        for i in range(4)]

            norm("n1", [1])
            turned("n1", "g1_mix", "g_kv")
            dve.wait_ge(job_out, J["kvd"][0] + 2)
            rms_tiles("ckv", m_down[:, :, 0:KV_LORA], KV_LORA, 16, m_ckvn).then_inc(pre["tsm"], 1)
            cos1 = cst("cos1").rearrange("p (t n) -> p t n", t=2)
            sin1 = cst("sin1").rearrange("p (t n) -> p t n", t=2)
            rotate(m_down[:, :, 256:272], m_down[:, :, 272:288], cos1, sin1, quarters(m_rt, 2, 16))
            for t in range(NT):
                V.tensor_copy(m_k[:, t, :, 64:96], bc(m_down[:, t, 256:288], 1, H))
            dve.wait_ge(job_out, J["qd"][0] + 2)
            rms_tiles("cq", m_qd, Q_LORA, 20, m_cqn).then_inc(pre["tsm"], 1)
            dve.wait_ge(job_out, J["qu"][0] + 8)
            for t in range(NT):
                rotate(m_q[:, t, :, 64:80], m_q[:, t, :, 80:96], bc(cos1[:, t, :], 1, H),
                       bc(sin1[:, t, :], 1, H), quarters(m_rt, H, 16), last=(t == 1))
            dve.wait_ge(job_out, J["qk1"][0] + 16)
            attend(0, 64, m_soft, 1.0 / math.sqrt(QD), cst("amask"))
            turned_split("o1")
            dve.wait_ge(al_rdy, 2 * SPLIT[a_at["wo1"]] + 2)
            for half in range(2):
                rest_slot(a_at["wo1"] + 1, half)
            res_norm(2, "g1_res", "nf1")
            norm("nf1", [1])
            ffn_start("ffn1", 0)
            turned_split("nf1", "g1_ffn")
            ffn_start("ffn1", 1)
            ffn("ffn1", 1)
            rest_slot(a_at["din"], 0)
            res_norm(3, "g1_fres", "n2")

            def heads(src, t=None):
                if t is None:
                    return src.rearrange("p t (h n) -> p t h n", h=H)
                return src[:, t, :].rearrange("p (h n) -> p h n", h=H)

            def head_squares(src, i, tmp):
                t4 = tmp[:, i * 2048:(i + 1) * 2048].rearrange("p (t h n) -> p t h n", t=2, h=H)
                V.tensor_tensor(t4, heads(src), heads(src), ALU.mult).then_inc(pre["osq"], 1)

            def head_sums(i, tmp, n):
                dve.wait_ge(pre["osq"], n)
                V.tensor_reduce(st[:, 128 + 32 * i:160 + 32 * i],
                                tmp[:, i * 2048:(i + 1) * 2048].rearrange("p (g n) -> p g n", n=64),
                                AX_X, ALU.add).then_inc(ss_rdy, 1)

            def head_scale(name, src, i, go=False):
                dve.wait_ge(sd_rdy, SD[name] + 1)
                link(V.reciprocal(st[:, 128 + 32 * i:160 + 32 * i], st[:, 192 + 32 * i:224 + 32 * i]))
                for t in range(NT):
                    s3 = heads(src, t)
                    r = st[:, 128 + 32 * i + 16 * t:144 + 32 * i + 16 * t]
                    ins = V.tensor_tensor(s3, s3, bc(r, 2, 64), ALU.mult)
                if go:
                    ins.then_inc(hd_go, 1)
                else:
                    link(ins)

            def head_gain(src, gain):
                for t in range(NT):
                    s3 = heads(src, t)
                    ins = V.tensor_tensor(s3, s3, bc(row(gain), 1, H), ALU.mult)
                link(ins)

            def rope2(src, h, tmp, last=False):
                for t in range(NT):
                    s3 = src[:, t, :].rearrange("p (h n) -> p h n", h=h)
                    rotate(s3[:, :, 0:8], s3[:, :, 8:16], bc(cs2[:, 0, t, :], 1, h),
                           bc(cs2[:, 1, t, :], 1, h), quarters(tmp, h, 8), last and t == 1)

            norm("n2", [1])
            turned_split("n2", "n0_mix")
            rest_slot(a_at["din"], 1)
            a, _n = ROW["lam"]
            for i in range(2):
                last = V.tensor_tensor_reduce(d_rt[:, i * 64:(i + 1) * 64],
                                              rows[:, a + 128 * i:a + 128 * i + 64],
                                              rows[:, a + 128 * i + 64:a + 128 * i + 128], 1.0, 0.0,
                                              ALU.mult, ALU.add, d_lam[:, i:i + 1])
            last.then_inc(pre["src2"], 1)
            for s, half in ((1, 0), (1, 1), (2, 0), (2, 1)):
                rest_slot(a_at["din"] + s, half)
            dve.wait_ge(job_out, J["din"][0] + 4)
            head_squares(d_p[:, 0], 0, d_sq)
            rest_slot(a_at["din"] + 3, 0)
            head_sums(0, d_sq, 1)
            rest_slot(a_at["din"] + 3, 1)
            head_scale("dq", d_p[:, 0], 0, go=True)
            rest_slot(a_at["din"] + 4, 0)
            rest_slot(a_at["din"] + 4, 1)
            dve.wait_ge(job_out, J["din"][0] + 8)
            head_squares(d_p[:, 1], 1, d_sq)
            rest_slot(a_at["din"] + 5, 0)
            head_sums(1, d_sq, 2)
            rest_slot(a_at["din"] + 5, 1)
            dve.wait_ge(wk["cs"], 1)
            head_scale("dk", d_p[:, 1], 1)
            head_gain(d_p[:, 1], "dk")
            dve.wait_ge(pre["osd"], 1)
            link(V.tensor_tensor(d_lam[:, 4:5], d_lam[:, 3:4], d_lam[:, 2:3], ALU.subtract))
            link(V.tensor_scalar(d_lam[:, 5:6], d_lam[:, 4:5], LAM_INIT, None, ALU.subtract))
            rope2(d_p[:, 1], H, d_rt, last=True)
            attend(1, P, d_soft, HD ** -0.5, cst("amask"))
            dve.wait_ge(pre["osd"], 2)
            link(V.reciprocal(st[:, 24:40], st[:, 40:56]))
            link(V.tensor_scalar(st[:, 24:40], st[:, 24:40], 1.0 - LAM_INIT, None, ALU.mult))
            xg = xnflat.rearrange("p (g n) -> p g n", n=P)
            for t in range(NT):
                V.tensor_tensor(xg[:, 8 * t:8 * t + 8, :], xg[:, 8 * t:8 * t + 8, :],
                                bc(st[:, 24 + 8 * t:32 + 8 * t], 2, P), ALU.mult).then_inc(xn_rdy, 1)
            turned_split("o2", "sub")
            dve.wait_ge(al_rdy, 2 * SPLIT[a_at["wo2"]] + 2)
            for half in range(2):
                rest_slot(a_at["wo2"] + 1, half)
            res_plain(4)
            norm("nm0")
            ffn_start("mlp0", 0)
            turned_split("nm0", "n0_mlp")
            ffn_start("mlp0", 1)
            ffn("mlp0")
            rest_slot(a_at["sin"], 0)
            res_plain(5)

            norm("n3")
            turned_split("n3", "n1_mix")
            rest_slot(a_at["sin"], 1)
            s_k = s_p[:, :, 256:1280]
            rest_slot(a_at["sin"] + 1, 0)
            rest_slot(a_at["sin"] + 1, 1)
            dve.wait_ge(job_out, J["sin"][0] + 2)
            rms_tiles("scq", s_p[:, :, 0:256], 256, 16, s_cqn).then_inc(pre["tsm"], 1)
            for s, half in ((2, 0), (2, 1), (3, 0), (3, 1)):
                rest_slot(a_at["sin"] + s, half)
            dve.wait_ge(job_out, J["sin"][0] + 6)
            head_squares(s_k, 1, s_sq)
            rest_slot(a_at["sin"] + 4, 0)
            head_sums(1, s_sq, 3)
            rest_slot(a_at["sin"] + 4, 1)
            head_scale("sk", s_k, 1, go=True)
            dve.wait_ge(job_out, J["sin"][0] + 10)
            ki = s_ki[:, :, 0, :]
            link(rms_tiles("kidx", s_p[:, :, 2304:2368], 64, 20, ki))
            rope2(ki, 1, s_rt)
            V.tensor_copy(s_ki[:, :, 1, :], ki)
            link(V.tensor_scalar(s_p[:, :, 2368:2376], s_p[:, :, 2368:2376],
                                 IDX_H ** -0.5 * 64 ** -0.5, None, ALU.mult))
            dve.wait_ge(job_out, J["uq"][0] + 4)
            head_squares(s_q, 0, s_sq)
            head_sums(0, s_sq, 4)
            dve.wait_ge(job_out, J["uq"][0] + 6)
            rope2(s_qi, IDX_H, s_rt, last=True)
            dve.wait_ge(sd_rdy, SD["sq"] + 1)
            V.reciprocal(st[:, 128:160], st[:, 192:224]).then_inc(hd_go, 1)
            for i in range(IDX_H):
                dve.wait_ge(pre["ixr"], i + 1)
                for t, (lo, hi) in enumerate(((0, P), (P, 384))):
                    w = s_p[:, t, 2368 + i:2369 + i]
                    r = s_ixr[:, i % 2, lo:hi]
                    if i == 0:
                        ins = V.tensor_scalar(s_acc[:, lo:hi], r, w, None, ALU.mult)
                    else:
                        ins = V.scalar_tensor_tensor(s_acc[:, lo:hi], r, w, s_acc[:, lo:hi],
                                                     ALU.mult, ALU.add)
                ins.then_inc(pre["ixs"], 1)
                dve.wait_ge(pre["ixs"], i + 1)
            link(V.tensor_tensor(s_w, s_acc, cst("amask"), ALU.add))
            m8 = st[:, 32:48]
            for r in range(TOPK // 8):
                for t, (lo, hi) in enumerate(((0, P), (P, 384))):
                    ins = V.max(m8[:, 8 * t:8 * t + 8], s_w[:, lo:hi])
                link(ins)
                for t, (lo, hi) in enumerate(((0, P), (P, 384))):
                    ins = V.match_replace(s_w[:, lo:hi], m8[:, 8 * t:8 * t + 8], s_w[:, lo:hi], TAKEN)
                link(ins)
            link(V.tensor_scalar(s_sel, s_w, TAKEN, -NEG, ALU.is_equal, ALU.mult))
            link(V.tensor_scalar(s_sel, s_sel, NEG, None, ALU.add))
            attend(2, 64, s_soft, HD ** -0.5, s_sel)
            turned_split("o3")
            dve.wait_ge(al_rdy, 2 * SPLIT[a_at["wo3"]] + 2)
            for half in range(2):
                rest_slot(a_at["wo3"] + 1, half)
            res_plain(6)
            norm("nm1")
            ffn_start("mlp1", 0)
            turned_split("nm1", "n1_mlp")
            ffn_start("mlp1", 1)
            ffn("mlp1")
            res_plain(7)


def constants():
    con, ncon = offsets(CONSTS)
    c = np.zeros((P, ncon), np.float32)

    def put(name, v):
        a, n = con[name]
        c[:, a:a + n] = v

    p = np.arange(P)
    put("ident", np.eye(P))
    put("blk1", (p[:, None] // 64 == p[None, :] // 64))
    put("sel2", (p[:, None] // 64 == np.arange(2)[None, :]))
    m = np.zeros((P, 384))
    m[:64, 64:128] = NEG
    m[:64, 320:384] = NEG
    put("amask", m)
    inv = (np.float32(1.0) / (np.float32(10000.0) ** (np.arange(0, QK_ROPE, 2, dtype=np.float32) / np.float32(QK_ROPE))))
    ang = np.arange(T, dtype=np.float32)[:, None] * inv[None, :].astype(np.float32)
    for name, f in (("cos1", np.cos), ("sin1", np.sin)):
        put(name, f(ang.astype(np.float64)).reshape(2, P, 16).transpose(1, 0, 2).reshape(P, 32))
    put("inv2", (np.float32(500000.0) ** (-np.arange(0, 16, 2, dtype=np.float32) / np.float32(16)))[None, :])
    put("eps", np.array([[EPS_NORM, EPS_LNX]]))
    put("ones", 1.0)
    a, b = p[:, None], p[None, :]
    ms = {"incl": a <= b, "strict": a < b, "dstrict": (a < b) & (a // 16 == b // 16),
          "dlow": (b < a) & (a // 16 == b // 16), "olow": (b < a) & (a // 16 != b // 16)}
    return c, np.concatenate([ms[n].astype(np.float32) for n in MASKS], axis=1)


def kernel(**inputs):
    import concourse.bacc as bacc
    from concourse.bass_utils import run_bass_kernel_spmd

    g = {k: np.asarray(v) for k, v in inputs.items()}

    def tiles(v):
        return np.ascontiguousarray(v.reshape(-1, P).T)

    parts = {"g0_mix": g["norm_g"][0, 0], "g0_ffn": g["norm_g"][0, 2], "g1_mix": g["norm_g"][1, 0],
             "g_kv": g["kv_norm_g"], "g1_ffn": g["norm_g"][1, 2], "n0_mix": g["norm_mix_2"][0],
             "n0_mlp": g["norm_mlp_2"][0], "n1_mix": g["norm_mix_2"][1], "n1_mlp": g["norm_mlp_2"][1],
             "mu": g["a_mu"][0], "w0": g["a_w0"], "a0": g["a_a0"], "k_k": g["a_k_k"],
             "k_a": g["a_k_a"], "r_k": g["a_r_k"], "kv_a": g["kv_a_norm_g"], "q_n": g["q_norm_g"],
             "cq_n": g["dsa_cq_norm_2"], "conv_w0": g["ffn_conv_w"][0], "conv_b0": g["ffn_conv_b"][0],
             "conv_w1": g["ffn_conv_w"][1], "conv_b1": g["ffn_conv_b"][1], "sub": g["diff_subln_2"]}
    rws = {"g0_res": g["norm_g"][0, 1], "g0_fres": g["norm_g"][0, 3], "g1_res": g["norm_g"][1, 1],
           "g1_fres": g["norm_g"][1, 3], "lnx_w": g["a_lnx_w"], "lnx_b": g["a_lnx_b"],
           "dq": g["diff_q_norm_2"], "dk": g["diff_k_norm_2"],
           "sq": g["dsa_q_norm_2"], "sk": g["dsa_k_norm_2"],
           "lam": np.concatenate([g[n].reshape(-1) for n in
                                  ("diff_lam_q1_2", "diff_lam_k1_2", "diff_lam_q2_2", "diff_lam_k2_2")])}
    con, masks = constants()
    arrays = {
        "x": g["x"][0], "positions": tiles(g["positions_2"]), "con": con, "masks": masks,
        "cols": np.concatenate([tiles(parts[n]) for n, _ in COLS], axis=1),
        "rows": np.concatenate([rws[n].reshape(1, -1) for n, _ in ROWS], axis=1),
        "w_r": g["a_w_rkv"][0, 0], "w_k": g["a_w_rkv"][0, 1], "w_v": g["a_w_rkv"][0, 2],
        "w_lora": np.concatenate([g["a_w1"][0], g["a_a1"][0], g["a_g1"][0]], axis=1),
        "a_w2": g["a_w2"][0], "a_a2": g["a_a2"][0], "a_g2": g["a_g2"][0], "a_w_o": g["a_w_o"][0],
        "kv_w_down": g["kv_w_down"], "kv_w_up": g["kv_w_up"], "q_w_down": g["q_w_down"][0],
        "q_w_up": g["q_w_up"][0], "o_w": g["o_w"][0], "diff_w_in": g["diff_w_in_2"][0],
        "diff_w_out": g["diff_w_out_2"][0], "dsa_w_in": g["dsa_w_in_2"][0],
        "w_uqi": np.concatenate([g["dsa_w_uq_2"][0], g["dsa_w_uq_idx_2"][0]], axis=1),
        "dsa_w_out": g["dsa_w_out_2"][0],
    }
    for n in range(2):
        arrays["ffn_w_in%d" % n] = g["ffn_w_in"][n]
        arrays["ffn_w_out%d" % n] = g["ffn_w_out"][n]
        arrays["mlp_w1_%d" % n] = g["mlp_w1_2"][n]
        arrays["mlp_w2_%d" % n] = g["mlp_w2_2"][n]
    arrays = {"in_" + k: np.ascontiguousarray(v) for k, v in arrays.items()}
    nc = bacc.Bacc("TRN2", target_bir_lowering=False, num_devices=1)
    d = {k[3:]: nc.dram_tensor(k, v.shape, mybir.dt.from_np(v.dtype), kind="ExternalInput").ap()
         for k, v in arrays.items()}
    out = nc.dram_tensor("out", (T, D), F32, kind="ExternalOutput").ap()
    program(nc, d, out)
    r = run_bass_kernel_spmd(nc, [arrays], core_ids=[0])
    return r.results[0]["out"].reshape(1, T, D)
```
